# Optimizing a Trainium2 kernel written in Bass

```python
import jax, jax.numpy as jnp
from jax import lax
import numpy as np

D_MODEL = 1024
BATCH = 1
SEQ = 1024
DEPTH = 1
DEC_BATCH = 8
DEC_SEQ = 16
PAST_LEN = 512

CHUNK = 64
MIX_W = D_MODEL // 2
N_BRANCH = 4
CONV_W = 4
EPS = 1e-6
S5_GROUP = 16
S5_GROUPS = MIX_W // S5_GROUP
S5_STATE = 64
GDN_HEADS = 4
GDN_DK = MIX_W // GDN_HEADS
GDN_DV = MIX_W // GDN_HEADS
LRU_BLOCKS = 8
LRU_BW = MIX_W // LRU_BLOCKS
LRU_C = 8.0
SSD_HEADS = 8
SSD_HEADDIM = MIX_W // SSD_HEADS
SSD_GROUPS = 2
SSD_STATE = 128
SSD_CONV_DIM = MIX_W + 2 * SSD_GROUPS * SSD_STATE
N_EXPERTS = 16
N_EXPERT_GROUPS = 4
EXPERTS_PER_GROUP = N_EXPERTS // N_EXPERT_GROUPS
TOP_K = 2
D_EXPERT = D_MODEL // 2
MOE_BLOCK = 128
IN_SPLITS = (MIX_W, 3 * MIX_W, MIX_W, GDN_HEADS, GDN_HEADS, MIX_W, MIX_W, MIX_W, SSD_CONV_DIM, SSD_HEADS, N_BRANCH * D_MODEL)
IN_COLS = sum(IN_SPLITS)

kernel_name = 'hybrid_streaming_encoder_step'

def _rmsnorm(x, w):
    xf = x.astype(jnp.float32)
    y = xf * lax.rsqrt(jnp.mean(xf * xf, axis=-1, keepdims=True) + EPS)
    return y.astype(x.dtype) * w

def _split(x, sizes):
    return jnp.split(x, np.cumsum(sizes)[:-1].tolist(), axis=-1)

def _causal_conv(x, buf, w, b):
    L = x.shape[1]
    xp = jnp.concatenate([buf.astype(x.dtype), x], axis=1)
    out = xp[:, 0:L] * w[0]
    for k in range(1, CONV_W):
        out = out + xp[:, k:k + L] * w[k]
    if b is not None:
        out = out + b
    return out, xp[:, L:]

def _chunk(a, axis, c):
    s = a.shape
    a = a.reshape(s[:axis] + (s[axis] // c, c) + s[axis + 1:])
    return jnp.moveaxis(a, axis, 0)

def _unchunk(a, axis):
    a = jnp.moveaxis(a, 0, axis)
    s = a.shape
    return a.reshape(s[:axis] + (s[axis] * s[axis + 1],) + s[axis + 2:])

def _affine_combine(left, right):
    a1, b1 = left
    a2, b2 = right
    return (a2 * a1, a2 * b1 + b2)

def _complex_affine_combine(left, right):
    a1r, a1i, b1r, b1i = left
    a2r, a2i, b2r, b2i = right
    return (a2r * a1r - a2i * a1i, a2r * a1i + a2i * a1r,
            a2r * b1r - a2i * b1i + b2r, a2r * b1i + a2i * b1r + b2i)

def _s5_mixer(u, st_re, st_im, P):
    f32 = jnp.float32
    bsz, L, _ = u.shape
    uf = u.astype(f32)
    ug = uf.reshape(bsz, L, S5_GROUPS, S5_GROUP)
    lam_re = P['s5_a_re'].astype(f32)
    lam_im = P['s5_a_im'].astype(f32)
    dt = jnp.exp(P['s5_log_dt'].astype(f32))[:, None]
    mag = jnp.exp(lam_re * dt)
    lb_re = mag * jnp.cos(lam_im * dt)
    lb_im = mag * jnp.sin(lam_im * dt)
    den = lam_re * lam_re + lam_im * lam_im
    f_re = ((lb_re - 1.0) * lam_re + lb_im * lam_im) / den
    f_im = (lb_im * lam_re - (lb_re - 1.0) * lam_im) / den
    b_re = P['s5_b_re'].astype(f32)
    b_im = P['s5_b_im'].astype(f32)
    bb_re = f_re[..., None] * b_re - f_im[..., None] * b_im
    bb_im = f_re[..., None] * b_im + f_im[..., None] * b_re
    bu_re = jnp.einsum('gpc,blgc->blgp', bb_re, ug)
    bu_im = jnp.einsum('gpc,blgc->blgp', bb_im, ug)
    x0_re = st_re.astype(f32)
    x0_im = st_im.astype(f32)
    bu_re = bu_re.at[:, 0].add(lb_re * x0_re - lb_im * x0_im)
    bu_im = bu_im.at[:, 0].add(lb_re * x0_im + lb_im * x0_re)
    a_re = jnp.broadcast_to(lb_re, bu_re.shape)
    a_im = jnp.broadcast_to(lb_im, bu_im.shape)
    _, _, xs_re, xs_im = lax.associative_scan(_complex_affine_combine, (a_re, a_im, bu_re, bu_im), axis=1)
    y = (jnp.einsum('gcp,blgp->blgc', P['s5_c_re'].astype(f32), xs_re)
         - jnp.einsum('gcp,blgp->blgc', P['s5_c_im'].astype(f32), xs_im))
    y = y.reshape(bsz, L, MIX_W) + P['s5_d'].astype(f32) * uf
    y = jax.nn.gelu(y)
    y = y * jax.nn.sigmoid(y @ P['s5_w_glu'].astype(f32))
    return y.astype(u.dtype), xs_re[:, -1].astype(st_re.dtype), xs_im[:, -1].astype(st_im.dtype)

def _gdn_chunked(q, k, v, g, beta, s0):
    L = q.shape[2]
    c = min(CHUNK, L)
    incl = jnp.tril(jnp.ones((c, c), dtype=bool))
    strict = jnp.tril(jnp.ones((c, c), dtype=bool), k=-1)
    eye = jnp.eye(c, dtype=jnp.float32)

    def step(S, inp):
        qc, kc, vc, gc, bc = inp
        gcum = jnp.cumsum(gc, axis=-1)
        decay = jnp.exp(jnp.where(incl, gcum[..., :, None] - gcum[..., None, :], -jnp.inf))
        kk = jnp.einsum('bhtk,bhsk->bhts', kc, kc)
        lhs = eye + jnp.where(strict, bc[..., :, None] * kk * decay, 0.0)
        rhs = jnp.concatenate([vc * bc[..., None], kc * (bc * jnp.exp(gcum))[..., None]], axis=-1)
        sol = lax.linalg.triangular_solve(lhs, rhs, left_side=True, lower=True, unit_diagonal=True)
        u = sol[..., :GDN_DV] - jnp.einsum('bhtk,bhkv->bhtv', sol[..., GDN_DV:], S)
        attn = jnp.einsum('bhtk,bhsk->bhts', qc, kc) * decay
        o = (jnp.einsum('bhtk,bhkv->bhtv', qc * jnp.exp(gcum)[..., None], S)
             + jnp.einsum('bhts,bhsv->bhtv', attn, u))
        k_end = kc * jnp.exp(gcum[..., -1:] - gcum)[..., None]
        S = S * jnp.exp(gcum[..., -1])[..., None, None] + jnp.einsum('bhsk,bhsv->bhkv', k_end, u)
        return S, o

    xs = tuple(_chunk(a, 2, c) for a in (q, k, v, g, beta))
    s_fin, o = lax.scan(step, s0, xs)
    return _unchunk(o, 2), s_fin

def _gdn_mixer(qkv, z, a_raw, b_raw, s0, buf, P):
    f32 = jnp.float32
    bsz, L, _ = qkv.shape
    qkv_c, new_buf = _causal_conv(qkv, buf, P['gdn_conv_w'], None)
    qkv_c = jax.nn.silu(qkv_c.astype(f32))
    q, k, v = jnp.split(qkv_c, 3, axis=-1)

    def heads(t):
        return t.reshape(bsz, L, GDN_HEADS, -1).transpose(0, 2, 1, 3)

    q, k, v = heads(q), heads(k), heads(v)
    q = q * lax.rsqrt(jnp.sum(q * q, axis=-1, keepdims=True) + EPS) * (GDN_DK ** -0.5)
    k = k * lax.rsqrt(jnp.sum(k * k, axis=-1, keepdims=True) + EPS)
    beta = jax.nn.sigmoid(b_raw.astype(f32)).transpose(0, 2, 1)
    g = (-jnp.exp(P['gdn_a_log'].astype(f32))
         * jax.nn.softplus(a_raw.astype(f32) + P['gdn_dt_bias'].astype(f32))).transpose(0, 2, 1)
    o, s_fin = _gdn_chunked(q, k, v, g, beta, s0.astype(f32))
    o = o.transpose(0, 2, 1, 3)
    o = o * lax.rsqrt(jnp.mean(o * o, axis=-1, keepdims=True) + EPS) * P['gdn_norm_w'].astype(f32)
    o = o * jax.nn.silu(z.astype(f32)).reshape(bsz, L, GDN_HEADS, GDN_DV)
    return o.reshape(bsz, L, MIX_W).astype(qkv.dtype), s_fin.astype(s0.dtype), new_buf.astype(buf.dtype)

def _lru_mixer(xc, gate, h0, buf, P):
    f32 = jnp.float32
    bsz, L, _ = xc.shape
    xt, new_buf = _causal_conv(xc, buf, P['lru_conv_w'], P['lru_conv_b'])
    xf = xt.astype(f32)
    xb = xf.reshape(bsz, L, LRU_BLOCKS, LRU_BW)
    r = jax.nn.sigmoid(jnp.einsum('blnc,ncd->blnd', xb, P['lru_w_a'].astype(f32)).reshape(bsz, L, MIX_W)
                       + P['lru_b_a'].astype(f32))
    i = jax.nn.sigmoid(jnp.einsum('blnc,ncd->blnd', xb, P['lru_w_x'].astype(f32)).reshape(bsz, L, MIX_W)
                       + P['lru_b_x'].astype(f32))
    log_a = -LRU_C * r * jax.nn.softplus(-P['lru_lambda'].astype(f32))
    a = jnp.exp(log_a)
    bterm = jnp.sqrt(-jnp.expm1(2.0 * log_a)) * (i * xf)
    bterm = bterm.at[:, 0].add(a[:, 0] * h0.astype(f32))
    _, h = lax.associative_scan(_affine_combine, (a, bterm), axis=1)
    y = h * jax.nn.gelu(gate.astype(f32))
    return y.astype(xc.dtype), h[:, -1].astype(h0.dtype), new_buf.astype(buf.dtype)

def _ssd_chunked(x, dt, la, bm, cm, h0):
    L = x.shape[1]
    c = min(CHUNK, L)
    incl = jnp.tril(jnp.ones((c, c), dtype=bool))[None, :, :, None]

    def step(h, inp):
        xc, dtc, lac, bc, cc = inp
        gcum = jnp.cumsum(lac, axis=1)
        decay = jnp.exp(jnp.where(incl, gcum[:, :, None, :] - gcum[:, None, :, :], -jnp.inf))
        scores = jnp.einsum('bthn,bshn->btsh', cc, bc) * decay
        y = jnp.einsum('btsh,bshp->bthp', scores, xc * dtc[..., None])
        y = y + jnp.einsum('bthn,bhpn->bthp', cc, h) * jnp.exp(gcum)[..., None]
        w_end = jnp.exp(gcum[:, -1:] - gcum) * dtc
        h = h * jnp.exp(gcum[:, -1])[:, :, None, None] + jnp.einsum('bsh,bshp,bshn->bhpn', w_end, xc, bc)
        return h, y

    xs = tuple(_chunk(a, 1, c) for a in (x, dt, la, bm, cm))
    h_fin, y = lax.scan(step, h0, xs)
    return _unchunk(y, 1), h_fin

def _ssd_mixer(z, xbc, dt_raw, h0, buf, P):
    f32 = jnp.float32
    bsz, L, _ = xbc.shape
    xbc_c, new_buf = _causal_conv(xbc, buf, P['ssd_conv_w'], P['ssd_conv_b'])
    xbc_c = jax.nn.silu(xbc_c.astype(f32))
    xs, bm, cm = _split(xbc_c, (MIX_W, SSD_GROUPS * SSD_STATE, SSD_GROUPS * SSD_STATE))
    xs = xs.reshape(bsz, L, SSD_HEADS, SSD_HEADDIM)
    rep = SSD_HEADS // SSD_GROUPS
    bm = jnp.repeat(bm.reshape(bsz, L, SSD_GROUPS, SSD_STATE), rep, axis=2)
    cm = jnp.repeat(cm.reshape(bsz, L, SSD_GROUPS, SSD_STATE), rep, axis=2)
    dt = jax.nn.softplus(dt_raw.astype(f32) + P['ssd_dt_bias'].astype(f32))
    la = -jnp.exp(P['ssd_a_log'].astype(f32)) * dt
    y, h_fin = _ssd_chunked(xs, dt, la, bm, cm, h0.astype(f32))
    y = y + P['ssd_d'].astype(f32)[:, None] * xs
    y = y.reshape(bsz, L, MIX_W) * jax.nn.silu(z.astype(f32))
    y = y * lax.rsqrt(jnp.mean(y * y, axis=-1, keepdims=True) + EPS) * P['ssd_norm_w'].astype(f32)
    return y.astype(xbc.dtype), h_fin.astype(h0.dtype), new_buf.astype(buf.dtype)

def _token_mixers(h, st, P):
    bsz, L, _ = h.shape
    s5_re0, s5_im0, gdn_s0, gdn_buf0, lru_h0, lru_buf0, ssd_h0, ssd_buf0 = st
    proj = h @ P['w_in']
    u_a, qkv_b, z_b, a_b, b_b, x_c, gate_c, z_d, xbc_d, dt_d, gate_raw = _split(proj, IN_SPLITS)
    y_a, s5_re, s5_im = _s5_mixer(u_a, s5_re0, s5_im0, P)
    y_b, gdn_s, gdn_buf = _gdn_mixer(qkv_b, z_b, a_b, b_b, gdn_s0, gdn_buf0, P)
    y_c, lru_h, lru_buf = _lru_mixer(x_c, gate_c, lru_h0, lru_buf0, P)
    y_d, ssd_h, ssd_buf = _ssd_mixer(z_d, xbc_d, dt_d, ssd_h0, ssd_buf0, P)
    ys = jnp.stack([y_a, y_b, y_c, y_d], axis=2)
    branches = jnp.einsum('blkm,kmd->blkd', ys, P['w_branch'])
    gates = jax.nn.sigmoid(gate_raw).reshape(bsz, L, N_BRANCH, D_MODEL)
    out = jnp.sum(gates * branches, axis=2) @ P['w_out']
    return out, (s5_re, s5_im, gdn_s, gdn_buf, lru_h, lru_buf, ssd_h, ssd_buf)

def _grouped_moe(h, router_w, router_bias, w_gate, w_up, w_down):
    f32 = jnp.float32
    T, D = h.shape
    scores = jax.nn.sigmoid(h.astype(f32) @ router_w.astype(f32))
    sel = (scores + router_bias.astype(f32)).reshape(T, N_EXPERT_GROUPS, EXPERTS_PER_GROUP)
    grp_score = jnp.sum(lax.top_k(sel, TOP_K)[0], axis=-1)
    g_idx = jnp.argmax(grp_score, axis=-1)
    in_grp = jnp.take_along_axis(sel, g_idx[:, None, None], axis=1)[:, 0]
    expert = g_idx[:, None] * EXPERTS_PER_GROUP + lax.top_k(in_grp, TOP_K)[1]
    wts = jnp.take_along_axis(scores, expert, axis=-1)
    wts = wts / jnp.sum(wts, axis=-1, keepdims=True)
    n_assign = T * TOP_K
    flat_e = expert.reshape(-1)
    order = jnp.argsort(flat_e)
    e_s = flat_e[order]
    t_s = (jnp.arange(n_assign) // TOP_K)[order]
    w_s = wts.reshape(-1)[order]
    counts = jnp.bincount(flat_e, length=N_EXPERTS)
    start = jnp.cumsum(counts) - counts
    padded = (counts + MOE_BLOCK - 1) // MOE_BLOCK * MOE_BLOCK
    pend = jnp.cumsum(padded)
    pos = (pend - padded)[e_s] + jnp.arange(n_assign) - start[e_s]
    n_blocks = -(-(n_assign + N_EXPERTS * (MOE_BLOCK - 1)) // MOE_BLOCK)
    block_expert = jnp.minimum(jnp.searchsorted(pend, jnp.arange(n_blocks) * MOE_BLOCK, side='right'), N_EXPERTS - 1)
    buf = jnp.zeros((n_blocks * MOE_BLOCK, D), h.dtype).at[pos].set(h[t_s])

    def expert_block(args):
        xb, e = args
        return (jax.nn.silu(xb @ w_gate[e]) * (xb @ w_up[e])) @ w_down[e]

    yb = lax.map(expert_block, (buf.reshape(n_blocks, MOE_BLOCK, D), block_expert)).reshape(n_blocks * MOE_BLOCK, D)
    return jnp.zeros_like(h).at[t_s].add(yb[pos] * w_s[:, None].astype(h.dtype))

def _layer(x, c, st, P, router_w, router_bias):
    bsz, L, _ = x.shape
    mod = jax.nn.silu(c) @ P['w_ada'] + P['b_ada']
    sh_m, sc_m, g_m, sh_f, sc_f, g_f = jnp.split(mod[:, None, :], 6, axis=-1)
    h = _rmsnorm(x, P['norm_mix_w']) * (1.0 + sc_m) + sh_m
    mix, new_st = _token_mixers(h, st, P)
    x = x + g_m * mix
    h = _rmsnorm(x, P['norm_moe_w']) * (1.0 + sc_f) + sh_f
    f = _grouped_moe(h.reshape(bsz * L, D_MODEL), router_w, router_bias, P['moe_w_gate'], P['moe_w_up'], P['moe_w_down'])
    x = x + g_f * f.reshape(bsz, L, D_MODEL)
    return x, new_st

def _zero_states(bsz, dtype):
    return (jnp.zeros((bsz, S5_GROUPS, S5_STATE), dtype),
            jnp.zeros((bsz, S5_GROUPS, S5_STATE), dtype),
            jnp.zeros((bsz, GDN_HEADS, GDN_DK, GDN_DV), dtype),
            jnp.zeros((bsz, CONV_W - 1, 3 * MIX_W), dtype),
            jnp.zeros((bsz, MIX_W), dtype),
            jnp.zeros((bsz, CONV_W - 1, MIX_W), dtype),
            jnp.zeros((bsz, SSD_HEADS, SSD_HEADDIM, SSD_STATE), dtype),
            jnp.zeros((bsz, CONV_W - 1, SSD_CONV_DIM), dtype))

def _trunk(x, c, layer_states, layer_params, router_w, router_bias, norm_final_w):
    new_states = []
    for l in range(DEPTH):
        x, st = _layer(x, c, layer_states[l], layer_params[l], router_w, router_bias)
        new_states.append(st)
    stacked = tuple(jnp.stack([new_states[l][i] for l in range(DEPTH)]) for i in range(8))
    return _rmsnorm(x, norm_final_w), stacked

def setup_inputs(seed: int = 0) -> dict:
    key = jax.random.key(seed)
    ks = iter(jax.random.split(key, 64))
    f32 = jnp.float32

    def nrm(shape, scale):
        return jax.random.normal(next(ks), shape, f32) * scale

    def unif(shape, lo, hi):
        return jax.random.uniform(next(ks), shape, f32, lo, hi)

    def gain(shape):
        return 1.0 + nrm(shape, 0.01)

    def dt_bias(shape):
        dt = jnp.exp(unif(shape, np.log(1e-3), np.log(1e-1)))
        return dt + jnp.log(-jnp.expm1(-dt))

    lru_u = unif((DEPTH, MIX_W), 0.9, 0.999) ** (1.0 / LRU_C)
    return {
        'x_prompt': nrm((BATCH, SEQ, D_MODEL), 1.0),
        'x_sample': nrm((DEC_BATCH, DEC_SEQ, D_MODEL), 1.0),
        'c_prompt': nrm((BATCH, D_MODEL), 1.0),
        'c_sample': nrm((DEC_BATCH, D_MODEL), 1.0),
        'state_s5_re': nrm((DEPTH, DEC_BATCH, S5_GROUPS, S5_STATE), 0.1),
        'state_s5_im': nrm((DEPTH, DEC_BATCH, S5_GROUPS, S5_STATE), 0.1),
        'state_gdn': nrm((DEPTH, DEC_BATCH, GDN_HEADS, GDN_DK, GDN_DV), 0.1),
        'cache_gdn_conv': nrm((DEPTH, DEC_BATCH, CONV_W - 1, 3 * MIX_W), 1.0),
        'state_lru': nrm((DEPTH, DEC_BATCH, MIX_W), 0.5),
        'cache_lru_conv': nrm((DEPTH, DEC_BATCH, CONV_W - 1, MIX_W), 1.0),
        'state_ssd': nrm((DEPTH, DEC_BATCH, SSD_HEADS, SSD_HEADDIM, SSD_STATE), 0.1),
        'cache_ssd_conv': nrm((DEPTH, DEC_BATCH, CONV_W - 1, SSD_CONV_DIM), 1.0),
        'norm_mix_w': gain((DEPTH, D_MODEL)),
        'norm_moe_w': gain((DEPTH, D_MODEL)),
        'norm_final_w': gain((D_MODEL,)),
        'w_ada': nrm((DEPTH, D_MODEL, 6 * D_MODEL), 0.5 * D_MODEL ** -0.5),
        'b_ada': nrm((DEPTH, 6 * D_MODEL), 0.01),
        'w_in': nrm((DEPTH, D_MODEL, IN_COLS), D_MODEL ** -0.5),
        's5_a_re': -0.5 + nrm((DEPTH, S5_GROUPS, S5_STATE), 0.01),
        's5_a_im': jnp.pi * jnp.arange(S5_STATE, dtype=f32) + nrm((DEPTH, S5_GROUPS, S5_STATE), 0.01),
        's5_b_re': nrm((DEPTH, S5_GROUPS, S5_STATE, S5_GROUP), (2 * S5_GROUP) ** -0.5),
        's5_b_im': nrm((DEPTH, S5_GROUPS, S5_STATE, S5_GROUP), (2 * S5_GROUP) ** -0.5),
        's5_c_re': nrm((DEPTH, S5_GROUPS, S5_GROUP, S5_STATE), (2 * S5_STATE) ** -0.5),
        's5_c_im': nrm((DEPTH, S5_GROUPS, S5_GROUP, S5_STATE), (2 * S5_STATE) ** -0.5),
        's5_log_dt': unif((DEPTH, S5_GROUPS), np.log(1e-3), np.log(1e-1)),
        's5_d': nrm((DEPTH, MIX_W), 1.0),
        's5_w_glu': nrm((DEPTH, MIX_W, MIX_W), MIX_W ** -0.5),
        'gdn_conv_w': nrm((DEPTH, CONV_W, 3 * MIX_W), CONV_W ** -0.5),
        'gdn_a_log': jnp.log(unif((DEPTH, GDN_HEADS), 1.0, 16.0)),
        'gdn_dt_bias': dt_bias((DEPTH, GDN_HEADS)),
        'gdn_norm_w': gain((DEPTH, GDN_DV)),
        'lru_conv_w': nrm((DEPTH, CONV_W, MIX_W), CONV_W ** -0.5),
        'lru_conv_b': nrm((DEPTH, MIX_W), 0.01),
        'lru_w_a': nrm((DEPTH, LRU_BLOCKS, LRU_BW, LRU_BW), LRU_BW ** -0.5),
        'lru_b_a': nrm((DEPTH, MIX_W), 0.01),
        'lru_w_x': nrm((DEPTH, LRU_BLOCKS, LRU_BW, LRU_BW), LRU_BW ** -0.5),
        'lru_b_x': nrm((DEPTH, MIX_W), 0.01),
        'lru_lambda': jnp.log(lru_u) - jnp.log1p(-lru_u),
        'ssd_conv_w': nrm((DEPTH, CONV_W, SSD_CONV_DIM), CONV_W ** -0.5),
        'ssd_conv_b': nrm((DEPTH, SSD_CONV_DIM), 0.01),
        'ssd_a_log': jnp.log(unif((DEPTH, SSD_HEADS), 1.0, 16.0)),
        'ssd_dt_bias': dt_bias((DEPTH, SSD_HEADS)),
        'ssd_d': gain((DEPTH, SSD_HEADS)),
        'ssd_norm_w': gain((DEPTH, MIX_W)),
        'w_branch': nrm((DEPTH, N_BRANCH, MIX_W, D_MODEL), MIX_W ** -0.5),
        'w_out': nrm((DEPTH, D_MODEL, D_MODEL), D_MODEL ** -0.5),
        'router_w': nrm((D_MODEL, N_EXPERTS), D_MODEL ** -0.5),
        'router_bias': nrm((N_EXPERTS,), 0.01),
        'moe_w_gate': nrm((DEPTH, N_EXPERTS, D_MODEL, D_EXPERT), D_MODEL ** -0.5),
        'moe_w_up': nrm((DEPTH, N_EXPERTS, D_MODEL, D_EXPERT), D_MODEL ** -0.5),
        'moe_w_down': nrm((DEPTH, N_EXPERTS, D_EXPERT, D_MODEL), D_EXPERT ** -0.5),
    }

def reference(x_prompt, x_sample, c_prompt, c_sample,
              state_s5_re, state_s5_im, state_gdn, cache_gdn_conv, state_lru, cache_lru_conv, state_ssd, cache_ssd_conv,
              norm_mix_w, norm_moe_w, norm_final_w, w_ada, b_ada, w_in,
              s5_a_re, s5_a_im, s5_b_re, s5_b_im, s5_c_re, s5_c_im, s5_log_dt, s5_d, s5_w_glu,
              gdn_conv_w, gdn_a_log, gdn_dt_bias, gdn_norm_w,
              lru_conv_w, lru_conv_b, lru_w_a, lru_b_a, lru_w_x, lru_b_x, lru_lambda,
              ssd_conv_w, ssd_conv_b, ssd_a_log, ssd_dt_bias, ssd_d, ssd_norm_w,
              w_branch, w_out,
              router_w, router_bias, moe_w_gate, moe_w_up, moe_w_down):
    layer_params = [
        dict(norm_mix_w=norm_mix_w[l], norm_moe_w=norm_moe_w[l], w_ada=w_ada[l], b_ada=b_ada[l], w_in=w_in[l],
             s5_a_re=s5_a_re[l], s5_a_im=s5_a_im[l], s5_b_re=s5_b_re[l], s5_b_im=s5_b_im[l],
             s5_c_re=s5_c_re[l], s5_c_im=s5_c_im[l], s5_log_dt=s5_log_dt[l], s5_d=s5_d[l], s5_w_glu=s5_w_glu[l],
             gdn_conv_w=gdn_conv_w[l], gdn_a_log=gdn_a_log[l], gdn_dt_bias=gdn_dt_bias[l], gdn_norm_w=gdn_norm_w[l],
             lru_conv_w=lru_conv_w[l], lru_conv_b=lru_conv_b[l], lru_w_a=lru_w_a[l], lru_b_a=lru_b_a[l],
             lru_w_x=lru_w_x[l], lru_b_x=lru_b_x[l], lru_lambda=lru_lambda[l],
             ssd_conv_w=ssd_conv_w[l], ssd_conv_b=ssd_conv_b[l], ssd_a_log=ssd_a_log[l],
             ssd_dt_bias=ssd_dt_bias[l], ssd_d=ssd_d[l], ssd_norm_w=ssd_norm_w[l],
             w_branch=w_branch[l], w_out=w_out[l],
             moe_w_gate=moe_w_gate[l], moe_w_up=moe_w_up[l], moe_w_down=moe_w_down[l])
        for l in range(DEPTH)]
    prompt_states = [_zero_states(x_prompt.shape[0], x_prompt.dtype) for _ in range(DEPTH)]
    cache_inputs = (state_s5_re, state_s5_im, state_gdn, cache_gdn_conv, state_lru, cache_lru_conv, state_ssd, cache_ssd_conv)
    sample_states = [tuple(s[l] for s in cache_inputs) for l in range(DEPTH)]
    y_prompt, p_states = _trunk(x_prompt, c_prompt, prompt_states, layer_params, router_w, router_bias, norm_final_w)
    y_sample, s_states = _trunk(x_sample, c_sample, sample_states, layer_params, router_w, router_bias, norm_final_w)
    p_s5_re, p_s5_im, p_gdn, p_gdn_conv, p_lru, p_lru_conv, p_ssd, p_ssd_conv = p_states
    s_s5_re, s_s5_im, s_gdn, s_gdn_conv, s_lru, s_lru_conv, s_ssd, s_ssd_conv = s_states
    return (y_prompt, y_sample,
            p_s5_re, p_s5_im, p_gdn, p_gdn_conv, p_lru, p_lru_conv, p_ssd, p_ssd_conv,
            s_s5_re, s_s5_im, s_gdn, s_gdn_conv, s_lru, s_lru_conv, s_ssd, s_ssd_conv)


_drawn_inputs = setup_inputs


def setup_inputs(seed=0):
    import zlib

    import numpy as np

    out = dict(_drawn_inputs(seed))
    spreads = {}
    factors = {'norm_mix_w': 2.672,
     'norm_moe_w': 3.326,
     'norm_final_w': 5.723,
     's5_a_re': 3.954,
     's5_c_re': 6.87,
     's5_c_im': 5.247,
     'gdn_norm_w': 8.0,
     'lru_b_a': 8.0,
     'lru_b_x': 8.0,
     'ssd_conv_b': 3.86,
     'ssd_d': 8.0,
     'ssd_norm_w': 8.0}
    for name, (base, spread) in spreads.items():
        noise = np.random.default_rng([zlib.crc32(name.encode()), seed]).standard_normal(out[name].shape)
        drawn = base * np.exp(spread * noise) if base else spread * noise
        out[name] = __import__('jax').numpy.asarray(drawn.astype(out[name].dtype))
    for name, factor in factors.items():
        out[name] = (out[name] * factor).astype(out[name].dtype)
    return out
```

```python
from contextlib import ExitStack

import numpy as np

import concourse.bass as bass
from concourse import mybir

F32 = mybir.dt.float32
ALU = mybir.AluOpType
ACT = mybir.ActivationFunctionType
AX = mybir.AxisListType

P = 128
D = 1024
KD = D // P
NP_TOK, NSEQ, SLEN = 1024, 8, 16
T = NP_TOK + NSEQ * SLEN
N3 = T // 3
NT = T // P
MIX = D // 2
KM = MIX // P
GH, SH = 4, 8
NE = 16
EPS = 1e-6
CW = 3 + NP_TOK + NSEQ * (3 + SLEN)
TWO_PI_HI = 6.28125
TWO_PI_LO = float(2 * np.pi - 6.28125)
ROUND = 12582912.0

CST = {}
def _cst(name, n):
    CST[name] = (sum(v[1] for v in CST.values()), n)
_cst("ident", P); _cst("ones", P); _cst("level", 7 * P)
_cst("neg_prompt", P); _cst("neg_sample", P); _cst("last", P); _cst("row", NSEQ); _cst("eps", 1); _cst("tri", 16)
NCST = sum(v[1] for v in CST.values())

VEC = {}
def _vec(name, n):
    VEC[name] = (sum(v[1] for v in VEC.values()), n)
for _n, _w in (("norm_mix", 8), ("norm_moe", 8), ("norm_final", 8), ("b_ada", 48), ("s5_d", 4), ("gdn_conv", 48),
               ("gdn_norm", 1), ("lru_conv", 16), ("lru_conv_b", 4), ("lru_b_a", 4), ("lru_b_x", 4), ("lru_lambda", 4),
               ("ssd_conv", 32), ("ssd_conv_b", 8), ("ssd_d", 4), ("ssd_norm", 4), ("s5_re", 16), ("s5_im", 16),
               ("s5_dt", 16), ("alog", 1), ("dtb", 1), ("rbias", NE), ("lru_h0", 32), ("s5_x0r", 128), ("s5_x0i", 128)):
    _vec(_n, _w)
NVEC = sum(v[1] for v in VEC.values())

def plan_tiles():
    names = [("ss_mix", 0, 0)]
    names += [("rows", 0, 1)]
    names += [("qkv", m, m % 2) for m in range(12)] + [("zb", m, m % 2) for m in range(KM)]
    names += [("qkn", m, m % 2) for m in range(8)]
    names += [("gdn_ss", m, m % 2) for m in range(4)]
    def merge(k):
        return [x for m in range(KD) for x in (("gate%d" % k, m, 0), ("br%d" % k, m, 1))]
    names += merge(1)
    names += [("xbc", m, m % 2) for m in range(8)] + [("zd", m, m % 2) for m in range(KM)]
    names += [("ssd_ss", 0, 0)]
    names += merge(3)
    names += [("xc", m, m % 2) for m in range(4)] + [("gc", m, m % 2) for m in range(4)]
    names += [x for m in range(4) for x in (("lru_r", m, 0), ("lru_i", m, 1))]
    names += merge(2)
    names += [("ua", m, m % 2) for m in range(4)]
    for i in range(4):
        names += [x for q in range(4) for x in (("bu_re", 4 * i + q, 0), ("bu_im", 4 * i + q, 1))]
    names += [("glu", m, m % 2) for m in range(4)]
    names += merge(0)
    names += [("out", m, m % 2) for m in range(KD)]
    names += [("ss_moe", 0, 0)]
    for e in range(NE):
        names += [x for m in range(4) for x in (("hg%d" % e, m, 0), ("hu%d" % e, m, 1))]
        names += [("down%d" % e, m, m % 2) for m in range(KD)]
    names += [("ss_final", 0, 0)]
    count, at = [0, 0], {}
    for name, m, s in names:
        at[(name, m)] = (s, count[s])
        count[s] += 1
    return at

FILL = plan_tiles()

def plan_loads():
    loads = [("ada", g, g % 2) for g in range(12)]
    def add(*names):
        for a, g in names:
            loads.append((a, g, (len(loads)) % 2))
    add(("qkv", 0), ("qkv", 1), ("qkv", 2), ("zb", 0), ("gdn_state", 0))
    def merge(k):
        add(("gate%d" % k, 0), ("br%d" % k, 0), ("gate%d" % k, 1))
    merge(1)
    add(("xbc", 0), ("xbc", 1), ("zd", 0), ("ssd_state", 0))
    merge(3)
    add(("xc", 0), ("gc", 0), ("lru_w", 0))
    merge(2)
    add(("ua", 0), ("s5_bc", 0), ("glu", 0))
    merge(0)
    add(("out", 0), ("out", 1))
    for e in range(NE):
        loads += [("hg%d" % e, 0, 0), ("hu%d" % e, 0, 1), ("down%d" % e, 0, 2)]
    return loads

LOADS = plan_loads()
SLOT = {(a, g): s for a, g, s in LOADS}

def slot_count(a, g):
    n = 0
    for x, y, s in LOADS:
        if s == SLOT[(a, g)]:
            n += 1
        if (x, y) == (a, g):
            return n

def last_reader(a, g):
    if a in ("ada", "gdn_state", "ssd_state", "lru_w", "s5_bc"):
        return None
    if a.startswith("down") or a.startswith("br"):
        return (a, KD - 1)
    if a == "glu":
        return (a, 3)
    return (a, 4 * g + 3)


def build(nc, A):
    with ExitStack() as ctx:
        def sb(name, shape):
            return ctx.enter_context(nc.sbuf_tensor(name, shape, F32))

        def sem(name):
            return ctx.enter_context(nc.semaphore(name))

        cst = sb("cst", [P, NCST])
        vec = sb("vec", [P, NVEC])
        mod = sb("mod", [P, 48 * 9])
        amul = sb("amul", [P, 2 * 72])
        cond = sb("cond", [P, 72])
        rows = sb("rows", [P, T])
        hist = sb("hist", [P, 24 * 24])
        hist_out = sb("hist_out", [P, 24 * 27])
        s5c = sb("s5c", [P, 16 * 36])
        s5x = sb("s5x", [P, 2 * 16 * 8])
        s5_out = sb("s5_out", [P, 2 * 16 * 9])
        lru_out = sb("lru_out", [P, 4 * 9])
        lruc = sb("lruc", [P, 32])
        wrows = sb("wrows", [P, KD * 16])
        wrouter = sb("wrouter", [P, KD * 16])
        small = sb("small", [P, 512])
        ARENA = 46080
        arena = sb("arena", [P, ARENA])
        psum = ctx.enter_context(nc.psum_tensor("psum", [P, 8 * 512], F32))

        def cut(start, n):
            assert start + n <= ARENA
            return arena[:, start:start + n]

        W = [cut(0, 4096), cut(4096, 4096), cut(31232, 4096)]
        HT = cut(8192, KD * T).rearrange("p (k t) -> p k t", k=KD)
        Y = cut(17408, KM * T).rearrange("p (k t) -> p k t", k=KM)
        R0 = 22016
        MRG0 = 36864
        merged = cut(MRG0, KD * T).rearrange("p (k t) -> p k t", k=KD)
        X = cut(R0, KD * T).rearrange("p (k t) -> p k t", k=KD)

        def bank(b, n=512, w=1):
            return psum[:, 512 * b:512 * b + n]

        def pset(s):
            return psum[:, 1536 * s:1536 * (s + 1)].rearrange("p (b c) -> p b c", b=3)[:, :, 0:N3]

        def tri3(ap):
            return ap.rearrange("p (b c) -> p b c", b=3)

        def c_(name, a=0, n=None):
            o, w = CST[name]
            return cst[:, o + a:o + a + (w if n is None else n)]

        def v_(name, a=0, n=1):
            return vec[:, VEC[name][0] + a:VEC[name][0] + a + n]

        ident, ones = c_("ident"), c_("ones")
        mod3 = mod[:, :].rearrange("p (m s) -> p m s", s=9)
        amul3 = amul[:, :].rearrange("p (w m s) -> p w m s", w=2, s=9)

        def seqs(ap):
            return ap[:, NP_TOK:T].rearrange("p (b t) -> p b t", t=SLEN)

        s_const = sem("s_const"); s_x = sem("s_x"); s_xr = sem("s_xr")
        s_w = [sem("s_w%d" % i) for i in range(3)]
        s_fill = [sem("s_fillA"), sem("s_fillB")]
        s_free = [sem("s_freeA"), sem("s_freeB")]
        s_dve = sem("s_dve"); s_act = sem("s_act")
        s_phase = sem("s_phase")
        s_cond = sem("s_cond"); s_ada = sem("s_ada"); s_mod = sem("s_mod")
        s_sq = sem("s_sq"); s_sq_used = sem("s_sq_used"); s_root = sem("s_root"); s_h = sem("s_h"); s_recip = sem("s_recip")
        s_cb = sem("s_cb"); s_conv = sem("s_conv")
        r_z = sem("r_z"); r_l = sem("r_l"); r_sg = sem("r_sg")
        s_sig = sem("s_sig"); s_acc = sem("s_acc")
        s_out = sem("s_out"); s_pstate = sem("s_pstate")
        c_bc = sem("c_bc"); c_cols = sem("c_cols"); c_diff = sem("c_diff"); c_exp = sem("c_exp")
        c_gram = sem("c_gram"); c_tok = sem("c_tok"); c_ops = sem("c_ops"); c_lk = sem("c_lk"); c_p = sem("c_p")
        c_ps = sem("c_ps"); c_d = sem("c_d"); c_x = sem("c_x"); c_w = sem("c_w"); c_nw = sem("c_nw"); c_u = sem("c_u")
        c_us = sem("c_us"); c_o = sem("c_o"); c_os = sem("c_os"); c_ut = sem("c_ut"); c_um = sem("c_um")
        c_s = sem("c_s"); c_ss = sem("c_ss")
        d_bc = sem("d_bc"); d_diff = sem("d_diff"); d_exp = sem("d_exp"); d_ops = sem("d_ops"); d_y = sem("d_y")
        d_ys = sem("d_ys"); d_bm = sem("d_bm"); d_s = sem("d_s"); d_ss = sem("d_ss"); d_gated = sem("d_gated")
        l_sp = sem("l_sp"); l_col = sem("l_col"); l_a = sem("l_a"); l_m = sem("l_m"); l_b = sem("l_b"); l_done = sem("l_done")
        a_mag = sem("a_mag"); a_th = sem("a_th"); a_sin = sem("a_sin"); a_bs = sem("a_bs"); a_bt = sem("a_bt")
        a_btc = sem("a_btc"); a_u = sem("a_u"); a_x = sem("a_x"); a_y = sem("a_y"); a_ys = sem("a_ys")
        a_yd = sem("a_yd"); a_g = sem("a_g"); a_gs = sem("a_gs")
        m_r = sem("m_r"); m_sc = sem("m_sc"); m_gate = sem("m_gate"); m_gt = sem("m_gt"); m_gtc = sem("m_gtc")
        m_gb = sem("m_gb"); m_gbc = sem("m_gbc"); m_sg = sem("m_sg"); m_hid = sem("m_hid")

        class Steps:
            def __init__(self, eng, own):
                self.eng, self.own, self.n = eng, own, {}

            def tell(self, ins, s):
                ins.then_inc(s, 1)
                self.n[s.name] = self.n.get(s.name, 0) + 1

            def then(self, ins, s=None):
                s = self.own if s is None else s
                self.tell(ins, s)
                self.eng.wait_ge(s, self.n[s.name])

        def end_phase(eng, n):
            eng.drain().then_inc(s_phase, 1)
            eng.wait_ge(s_phase, 3 * (n + 1))

        def wait_fill(eng, name, m):
            s, k = FILL[(name, m)]
            eng.wait_ge(s_fill[s], k + 1)
            return s

        def freed(eng, name, m):
            s, k = FILL[(name, m)]
            eng.wait_ge(s_free[s], k + 1)

        def wait_load(eng, a, g):
            s = SLOT[(a, g)]
            eng.wait_ge(s_w[s], 16 * slot_count(a, g))
            return W[s]

        block = ctx.enter_context(nc.Block())

        tmp0 = 35840
        QKV = cut(R0, 12 * T).rearrange("p (m t) -> p m t", m=12)
        cb_g = [cut(tmp0, CW), cut(tmp0 + CW + 1, CW)]
        sq_a = [cut(tmp0, T), cut(tmp0 + T, T)]
        rs_a, rt_a = cut(tmp0 + 2 * T, T), cut(tmp0 + 3 * T, T)
        rowt = [cut(tmp0 + (4 + i) * T, T) for i in range(4)]
        (cDT, cEG, cLT, cAT, cQE, cKE, cKB, cVB, cLK, cPS, cX, cXT, cU, cS, cNW) = [
            cut(tmp0 + 512 * i, 512) for i in range(15)]
        cUM = cut(tmp0 + 512 * 15, 1024)
        Rb = R0 + 8 * T
        XBC = cut(R0, 8 * T).rearrange("p (m t) -> p m t", m=8)
        cb_s = [cut(Rb, CW), cut(Rb + CW + 1, CW)]
        sq_s = [cut(Rb, T), cut(Rb + T, T)]
        rs_s, rt_s = cut(Rb + 2 * T, T), cut(Rb + 3 * T, T)
        dDT, dEG = cut(Rb, 1024), cut(Rb + 1024, 1024)
        dXD, dXW = cut(Rb + 2048, 512), cut(Rb + 2560, 512)
        dB, dBM, dH, dTMP = cut(Rb + 3072, 256), cut(Rb + 3328, 256), cut(Rb + 3584, 512), cut(Rb + 4096, 512)
        Rl = R0 + 4 * T
        XF = cut(R0, 4 * T).rearrange("p (m t) -> p m t", m=4)
        cb_l = [cut(Rl, CW), cut(Rl + CW + 1, CW)]
        lt = [cut(Rl + 2400 + i * T, T) for i in range(6)]
        U = XF
        sCOS, sSIN = cut(Rl, T), cut(Rl + T, T)
        st = [cut(Rl + (2 + i) * T, T) for i in range(6)]
        sBT = cut(Rl + 8 * T, 1024)
        sMASK = rows[:, :]
        hid = cut(35328, KM * T).rearrange("p (k t) -> p k t", k=KM)
        E0 = 35328 + 4 * T
        sq_e = [cut(E0, T), cut(E0 + T, T)]
        rs_e, rt_e = cut(E0 + 2 * T, T), cut(E0 + 3 * T, T)
        sg = sq_e
        gbc = [rs_e, rt_e]
        gateT = cut(E0 + 4 * T, T)
        G0 = 35328
        res_tmp = cut(E0 + 5 * T, P)
        cmpA, cmpB = cut(E0, 576), cut(E0 + 576, 576)
        scores, rsel, rank, top, rw, gates = [cut(G0 + 144 * i, 144) for i in range(6)]
        grp = cut(G0 + 144 * 6, 36 * 4)
        mg_sig = [cut(R0, T), cut(R0 + T, T)]
        mg_tmp = cut(R0 + 2 * T, T)

        colG, colE, colB = small[:, 0:80], small[:, 96:112], small[:, 112:116]
        colK, colW, colL = small[:, 116:124], small[:, 124:132], small[:, 132:196]
        nexpa = small[0:16, 200:201]

        S5N = ["dt", "mag", "th", "sin", "cos", "den", "fre", "fim", "t0", "t1", "lre", "lim", "c1", "s1"]

        def s5(name, k=0):
            i = (S5N.index(name) if name in S5N else len(S5N) + 2 * k + (name == "pi")) * 16
            return s5c[:, i:i + 16]

        def hd(ap, h):
            return ap.rearrange("p (h t) -> p h t", h=h)

        def over(ap, n):
            return ap.unsqueeze(2).to_broadcast([ap.shape[0], ap.shape[1], n])

        def by(ap, n):
            return ap.unsqueeze(1).to_broadcast([ap.shape[0], n, ap.shape[1]])

        sq_no, sq_reader, root_no = {}, {}, {}
        n_sq = used = 0
        for name, m, terms in ([("ss_mix", 0, KD)] + [("qkn", m, 1) for m in range(8)] +
                               [("gdn_ss", m, 1) for m in range(4)] + [("ssd_ss", 0, KM)] +
                               [("ss_moe", 0, KD), ("ss_final", 0, KD)]):
            root_no[(name, m)] = len(root_no)
            sq_no[(name, m)] = list(range(n_sq, n_sq + terms))
            for i in range(terms):
                if i < terms - 1:
                    used += 1
                    sq_reader[n_sq + i] = (s_sq_used, used)
                else:
                    fs, fk = FILL[(name, m)]
                    sq_reader[n_sq + i] = (s_fill[fs], fk + 1)
            n_sq += terms

        def pe_tile(pe, name, m, w, src, K):
            s, k = FILL[(name, m)]
            if k >= 1:
                pe.wait_ge(s_free[s], k)
            for n in range(3):
                for kk in range(K):
                    last = nc.tensor.matmul(pset(s)[:, n, :], w[:, kk, :], src[:, kk, n * N3:(n + 1) * N3],
                                            start=(kk == 0), stop=(kk == K - 1))
            last.then_inc(s_fill[s], 1)

        def pe_group(pe, name, g, src, K, per):
            w = wait_load(pe, name, g).rearrange("p (m k c) -> p m k c", m=4096 // (K * P), k=K)
            for m in range(per):
                pe_tile(pe, name, per * g + m, w[:, m], src, K)

        def pe_sumsq(pe, name, m, sq):
            s, k = FILL[(name, m)]
            if k >= 1:
                pe.wait_ge(s_free[s], k)
            terms = sq_no[(name, m)]
            for i, q in enumerate(terms):
                pe.wait_ge(s_sq, q + 1)
                for n in range(3):
                    last = nc.tensor.matmul(pset(s)[:, n, :], ones, sq[q % 2][:, n * N3:(n + 1) * N3],
                                            start=(i == 0), stop=(i == len(terms) - 1))
                last.then_inc(s_sq_used if i < len(terms) - 1 else s_fill[s], 1)

        def act_sumsq(act, name, m, sq, srcs):
            for q, src in zip(sq_no[(name, m)], srcs):
                if q >= 2:
                    act.wait_ge(*sq_reader[q - 2])
                nc.scalar.activation(sq[q % 2], src, ACT.Square).then_inc(s_sq, 1)

        def act_root(St, name, m, dst, scale):
            s = wait_fill(St.eng, name, m)
            if root_no[(name, m)] >= 1:
                St.eng.wait_ge(s_recip, root_no[(name, m)])
            nc.scalar.activation(tri3(dst), pset(s), ACT.Sqrt, bias=c_("eps"), scale=scale).then_inc(s_free[s], 1)

        def dve_recip(V, name, m, rs, rt):
            freed(V.eng, name, m)
            V.then(nc.vector.reciprocal(rs, rt), s_recip)

        def dve_norm(V, x, h, aw, sh):
            for k in range(KD):
                V.then(nc.vector.tensor_tensor(h[:, k, :], x[:, k, :], V.rs, ALU.mult))
                nc.vector.tensor_scalar(h[:, k, 0:NP_TOK], h[:, k, 0:NP_TOK], aw[:, k, 0:1], sh[:, k, 0:1],
                                        ALU.mult, ALU.add)
                hs = seqs(h[:, k, :])
                V.then(nc.vector.tensor_tensor(hs, hs, over(aw[:, k, 1:9], SLEN), ALU.mult))
                V.then(nc.vector.tensor_tensor(hs, hs, over(sh[:, k, 1:9], SLEN), ALU.add),
                       s_h if k == KD - 1 else None)

        def cb_seq(c):
            return c[:, 3 + NP_TOK:CW].rearrange("p (b t) -> p b t", t=3 + SLEN)

        def act_conv_in(St, name, m, n, c):
            s = wait_fill(St.eng, name, m)
            if n >= 2:
                St.eng.wait_ge(s_conv, n - 1)
            ps, d = pset(s), c[n % 2]
            nc.scalar.activation(cb_seq(d)[:, :, 0:3], hist[:, 24 * n:24 * (n + 1)].rearrange("p (b t) -> p b t", t=3),
                                 ACT.Copy)
            nc.scalar.activation(d[:, 3:3 + 2 * N3].rearrange("p (b t) -> p b t", b=2), ps[:, 0:2, :], ACT.Copy)
            nc.scalar.activation(d[:, 3 + 2 * N3:3 + NP_TOK], ps[:, 2, 0:NP_TOK - 2 * N3], ACT.Copy)
            St.then(nc.scalar.activation(cb_seq(d)[:, :, 3:3 + SLEN],
                                         ps[:, 2, NP_TOK - 2 * N3:N3].rearrange("p (b t) -> p b t", t=SLEN), ACT.Copy),
                    s_cb)
            St.eng.sem_inc(s_free[s], 1)

        def dve_cb_start(V, c):
            nc.vector.memset(c[0][:, 0:3], 0.0)
            V.then(nc.vector.memset(c[1][:, 0:3], 0.0))

        def dve_conv(V, n, c, dst, wname, wt, ntile, bias=None):
            V.eng.wait_ge(s_cb, n + 1)
            d = c[n % 2]
            ho = hist_out[:, 27 * n:27 * (n + 1)].rearrange("p (b t) -> p b t", t=3)
            nc.vector.tensor_copy(ho[:, 0, :], d[:, NP_TOK:NP_TOK + 3])
            nc.vector.tensor_copy(ho[:, 1:9, :], cb_seq(d)[:, :, SLEN:SLEN + 3])
            ds = seqs(dst)
            for k in range(4):
                a, b, w = d[:, k:k + NP_TOK], cb_seq(d)[:, :, k:k + SLEN], v_(wname, k * ntile + wt)
                if k == 0 and bias is None:
                    nc.vector.tensor_scalar(dst[:, 0:NP_TOK], a, w, None, ALU.mult)
                    V.then(nc.vector.tensor_scalar(ds, b, w, None, ALU.mult))
                elif k == 0:
                    nc.vector.tensor_scalar(dst[:, 0:NP_TOK], a, w, bias, ALU.mult, ALU.add)
                    V.then(nc.vector.tensor_scalar(ds, b, w, bias, ALU.mult, ALU.add))
                else:
                    nc.vector.scalar_tensor_tensor(out=dst[:, 0:NP_TOK], in0=a, scalar=w, in1=dst[:, 0:NP_TOK],
                                                   op0=ALU.mult, op1=ALU.add)
                    V.then(nc.vector.scalar_tensor_tensor(out=ds, in0=b, scalar=w, in1=ds, op0=ALU.mult, op1=ALU.add),
                           s_conv if k == 3 else None)

        MERGES = [1, 3, 2, 0]

        def pe_merge(pe, k):
            g = "gate%d" % k
            for m in range(KD):
                if m % 4 == 0:
                    wg = wait_load(pe, g, m // 4).rearrange("p (m k c) -> p m k c", m=4, k=KD)
                pe_tile(pe, g, m, wg[:, m % 4], HT, KD)
                if m == 0:
                    wb = wait_load(pe, "br%d" % k, 0).rearrange("p (m k c) -> p m k c", m=8, k=KM)
                pe_tile(pe, "br%d" % k, m, wb[:, m], Y, KM)

        def act_merge(act, k):
            at = MERGES.index(k) * KD
            for m in range(KD):
                s = wait_fill(act, "gate%d" % k, m)
                if at + m >= 2:
                    act.wait_ge(s_acc, at + m - 1)
                nc.scalar.activation(tri3(mg_sig[m % 2]), pset(s), ACT.Sigmoid).then_inc(s_free[s], 1)

        def dve_merge(V, k):
            for m in range(KD):
                freed(V.eng, "gate%d" % k, m)
                s = wait_fill(V.eng, "br%d" % k, m)
                dst = merged[:, m, :] if k == MERGES[0] else mg_tmp
                nc.vector.tensor_tensor(tri3(dst), tri3(mg_sig[m % 2]), pset(s), ALU.mult).then_inc(s_free[s], 1)
                freed(V.eng, "br%d" % k, m)
                if k == MERGES[0]:
                    V.eng.sem_inc(s_acc, 1)
                    V.n[s_acc.name] = V.n.get(s_acc.name, 0) + 1
                else:
                    V.then(nc.vector.tensor_tensor(merged[:, m, :], merged[:, m, :], mg_tmp, ALU.add), s_acc)

        def dve_residual(V, name, m, gate, tmp):
            s = wait_fill(V.eng, name, m)
            ps, x = pset(s), X[:, m, :]
            g = mod3[:, gate + m, :]
            xa = x[:, 0:2 * N3].rearrange("p (b t) -> p b t", b=2)
            nc.vector.scalar_tensor_tensor(out=xa, in0=ps[:, 0:2, :], scalar=g[:, 0:1], in1=xa, op0=ALU.mult, op1=ALU.add)
            xb = x[:, 2 * N3:NP_TOK]
            nc.vector.scalar_tensor_tensor(out=xb, in0=ps[:, 2, 0:NP_TOK - 2 * N3], scalar=g[:, 0:1], in1=xb,
                                           op0=ALU.mult, op1=ALU.add)
            t = tmp[:, 0:P].rearrange("p (b t) -> p b t", t=SLEN)
            nc.vector.tensor_tensor(t, ps[:, 2, NP_TOK - 2 * N3:N3].rearrange("p (b t) -> p b t", t=SLEN),
                                    over(g[:, 1:9], SLEN), ALU.mult).then_inc(s_free[s], 1)
            freed(V.eng, name, m)
            V.then(nc.vector.tensor_tensor(seqs(x), seqs(x), t, ALU.add))

        LEV = [7] * 8 + [4]
        LEV0 = [7 * c for c in range(9)]
        NC7 = NT - 1

        @block.sync
        def _(sp):
            for dst, name in ((cst, "cst"), (vec, "vec"), (cond, "cT"), (hist, "hist"), (wrows, "wrows"), (wrouter, "wrouter")):
                sp.dma_start(dst[:, :], A[name]).then_inc(s_const, 16)
            sp.dma_start(X, A["xT"]).then_inc(s_x, 16)
            before = {}
            for a, g, s in LOADS:
                if s == 2 and s not in before:
                    sp.wait_ge(s_phase, 3 * 14)
                if s in before:
                    pa, pg = before[s]
                    if pa == "ada":
                        sp.wait_ge(s_ada, pg + 1)
                    elif pa == "gdn_state":
                        sp.wait_ge(c_ss, NC7)
                        sp.dma_start(A["gdn_p"], cS).then_inc(s_pstate, 16)
                        sp.wait_ge(c_ss, NC7 + GH)
                        sp.dma_start(A["gdn_s"], W[s]).then_inc(s_pstate, 16)
                        sp.wait_ge(s_pstate, 32)
                    elif pa == "ssd_state":
                        sp.wait_ge(d_ss, NC7)
                        sp.dma_start(A["ssd_p"], dH).then_inc(s_pstate, 16)
                        sp.wait_ge(d_ss, NC7 + NSEQ)
                        sp.dma_start(A["ssd_s"], W[s]).then_inc(s_pstate, 16)
                        sp.wait_ge(s_pstate, 64)
                    elif pa == "lru_w":
                        sp.wait_ge(s_phase, 3 * 11)
                    elif pa == "s5_bc":
                        sp.wait_ge(s_phase, 3 * 13)
                    else:
                        f, k = FILL[last_reader(pa, pg)]
                        sp.wait_ge(s_fill[f], k + 1)
                sp.dma_start(W[s], A[a][g]).then_inc(s_w[s], 16)
                before[s] = (a, g)
                if a == "out" and g == 1:
                    sp.wait_ge(s_phase, 3 * 14)
                    sp.dma_start(X, A["xT"]).then_inc(s_xr, 16)
            sp.wait_ge(s_phase, 3 * 18)
            sp.dma_start(A["yT"], HT).then_inc(s_out, 16)
            for name, t in (("hist_out", hist_out), ("s5_out", s5_out), ("lru_out", lru_out)):
                sp.dma_start(A[name], t[:, :]).then_inc(s_out, 16)
            sp.wait_ge(s_out, 16 * 4)

        @block.tensor
        def _(pe):
            pe.wait_ge(s_const, 16 * 6)
            pe.wait_ge(s_cond, 1)
            for g in range(12):
                w = wait_load(pe, "ada", g).rearrange("p (m k c) -> p m k c", m=4, k=KD)
                for m in range(4 * g, 4 * g + 4):
                    for k in range(KD):
                        last = nc.tensor.matmul(bank(6)[:, 9 * m:9 * m + 9], w[:, m % 4, k, :], cond[:, 9 * k:9 * k + 9],
                                                start=(k == 0), stop=(k == KD - 1))
                last.then_inc(s_ada, 1)
            pe_sumsq(pe, "ss_mix", 0, sq_a)
            pe.wait_ge(s_h, 1)
            s, k = FILL[("rows", 0)]
            pe.wait_ge(s_free[s], k) if k else None
            wr = wrows[:, :].rearrange("p (k c) -> p k c", k=KD)
            for n in range(3):
                for kk in range(KD):
                    last = nc.tensor.matmul(pset(s)[0:16, n, :], wr[:, kk, :], HT[:, kk, n * N3:(n + 1) * N3],
                                            start=(kk == 0), stop=(kk == KD - 1))
            last.then_inc(s_fill[s], 1)
            end_phase(pe, 0)
            for g in range(3):
                pe_group(pe, "qkv", g, HT, KD, 4)
            pe_group(pe, "zb", 0, HT, KD, 4)
            end_phase(pe, 1)
            for m in range(8):
                pe_sumsq(pe, "qkn", m, sq_a)
            end_phase(pe, 2)

            def sel(r):
                return ident[0:80, r:r + 1].to_broadcast([80, P])

            for c in range(NT):
                t0 = c * P
                sample = c == NC7
                ck = lambda m: QKV[:, m, t0:t0 + P]
                hs = [slice(h * P, (h + 1) * P) for h in range(GH)]
                if c:
                    pe.wait_ge(c_ss, c)
                    pe.wait_ge(c_os, c)
                for h in range(GH):
                    nc.tensor.matmul(bank(0)[:, hs[h]], sel(h), rows[0:80, t0:t0 + P], start=True, stop=True)
                for h in range(GH):
                    nc.tensor.matmul(bank(1)[:, hs[h]], sel(76 + h), rows[0:80, t0:t0 + P], start=True, stop=True)
                nc.tensor.transpose(bank(2)[:, 0:80], rows[0:80, t0:t0 + P], ident[0:80, 0:80]).then_inc(c_bc, 1)
                for h in range(GH):
                    nc.tensor.matmul(bank(3)[:, hs[h]], ck(4 + h), ck(4 + h), start=True, stop=True)
                for h in range(GH):
                    last = nc.tensor.matmul(bank(4)[:, hs[h]], ck(4 + h), ck(h), start=True, stop=True)
                last.then_inc(c_gram, 1)
                for h in range(GH):
                    nc.tensor.transpose(bank(5)[:, hs[h]], ck(4 + h), ident)
                for h in range(GH):
                    last = nc.tensor.transpose(bank(6)[:, hs[h]], ck(8 + h), ident)
                last.then_inc(c_tok, 1)
                pe.wait_ge(c_ops, c + 1)
                for n in range(LEV0[c], LEV0[c] + LEV[c]):
                    pe.wait_ge(c_lk, n + 1)
                    for a in hs:
                        last = nc.tensor.matmul(bank(0)[:, a], cLK[:, a], cX[:, a], start=True, stop=True)
                    last.then_inc(c_p, 1)
                    pe.wait_ge(c_ps, n + 1)
                    for a in hs:
                        nc.tensor.matmul(bank(1)[:, a], cXT[:, a], cPS[:, a], start=True, stop=True)
                    for a in hs:
                        last = nc.tensor.matmul(bank(2)[:, a], cPS[:, a], cXT[:, a], start=True, stop=True)
                    last.then_inc(c_d, 1)
                pe.wait_ge(c_x, LEV0[c] + LEV[c])
                for a in hs:
                    last = nc.tensor.matmul(bank(3)[:, a], cKB[:, a], cXT[:, a], start=True, stop=True)
                last.then_inc(c_w, 1)
                pe.wait_ge(c_nw, c + 1)
                if not sample:
                    for a in hs:
                        nc.tensor.matmul(bank(4)[:, a], cXT[:, a], cVB[:, a], start=True, stop=False)
                        last = nc.tensor.matmul(bank(4)[:, a], cNW[:, a], cS[:, a], start=False, stop=True)
                    last.then_inc(c_u, 1)
                    pe.wait_ge(c_us, c + 1)
                    for a in hs:
                        nc.tensor.matmul(bank(5)[:, a], cS[:, a], cQE[:, a], start=True, stop=False)
                        last = nc.tensor.matmul(bank(5)[:, a], cU[:, a], cAT[:, a], start=False, stop=True)
                    last.then_inc(c_o, 1)
                    for a in hs:
                        last = nc.tensor.matmul(bank(6)[:, a], cKE[:, a], cU[:, a], start=True, stop=True)
                    last.then_inc(c_s, 1)
                else:
                    S0 = wait_load(pe, "gdn_state", 0).rearrange("p (b h v) -> p b h v", b=NSEQ, h=GH)
                    for h in range(GH):
                        nc.tensor.matmul(bank(4)[:, hs[h]], cVB[:, hs[h]], cXT[:, hs[h]], start=True, stop=False)
                        for b in range(NSEQ):
                            a = slice(h * P + SLEN * b, h * P + SLEN * (b + 1))
                            last = nc.tensor.matmul(bank(4)[:, a], S0[:, b, h, :], cNW[:, a],
                                                    start=False, stop=(b == NSEQ - 1))
                    last.then_inc(c_u, 1)
                    pe.wait_ge(c_ut, 1)
                    for a in hs:
                        last = nc.tensor.transpose(bank(7)[:, a], cPS[:, a], ident)
                    last.then_inc(c_u, 1)
                    pe.wait_ge(c_us, c + 1)
                    for h in range(GH):
                        nc.tensor.matmul(bank(5)[:, hs[h]], cU[:, hs[h]], cAT[:, hs[h]], start=True, stop=False)
                        for b in range(NSEQ):
                            a = slice(h * P + SLEN * b, h * P + SLEN * (b + 1))
                            last = nc.tensor.matmul(bank(5)[:, a], S0[:, b, h, :], cQE[:, a],
                                                    start=False, stop=(b == NSEQ - 1))
                    last.then_inc(c_o, 1)
                    for h in range(GH):
                        pe.wait_ge(c_um, h + 1)
                        for j in range(2):
                            last = nc.tensor.matmul(bank(j), cKE[:, hs[h]], cUM[:, 512 * j:512 * (j + 1)],
                                                    start=True, stop=True)
                        last.then_inc(c_s, 1)
            end_phase(pe, 3)
            for m in range(GH):
                pe_sumsq(pe, "gdn_ss", m, sq_a)
            end_phase(pe, 4)
            pe_merge(pe, 1)
            end_phase(pe, 5)
            for g in range(2):
                pe_group(pe, "xbc", g, HT, KD, 4)
            pe_group(pe, "zd", 0, HT, KD, 4)
            end_phase(pe, 6)
            for c in range(NT):
                t0 = c * P
                sample = c == NC7
                xk = lambda m: XBC[:, m, t0:t0 + P]
                if c:
                    pe.wait_ge(d_ss, c)
                    pe.wait_ge(d_ys, c)
                for h in range(SH):
                    nc.tensor.matmul(bank(h // 4)[:, (h % 4) * P:(h % 4 + 1) * P], sel(4 + h), rows[0:80, t0:t0 + P],
                                     start=True, stop=True)
                nc.tensor.transpose(bank(2)[:, 0:80], rows[0:80, t0:t0 + P], ident[0:80, 0:80])
                for g in range(2):
                    nc.tensor.matmul(bank(3)[:, g * P:(g + 1) * P], xk(4 + g), xk(6 + g), start=True, stop=True)
                for g in range(2):
                    nc.tensor.transpose(bank(4)[:, g * P:(g + 1) * P], xk(4 + g), ident)
                for m in range(KM):
                    last = nc.tensor.transpose(bank(5)[:, m * P:(m + 1) * P], xk(m), ident)
                last.then_inc(d_bc, 1)
                pe.wait_ge(d_ops, c + 1)
                if sample:
                    H0 = wait_load(pe, "ssd_state", 0).rearrange("p (b h d) -> p b h d", b=NSEQ, h=SH)
                for h in range(SH):
                    q0, o0 = 64 * (h % 2), 6 * 512 + (h // 2) * P
                    y = psum[q0:q0 + 64, o0:o0 + P]
                    nc.tensor.matmul(y, dXD[:, 64 * h:64 * h + 64], dDT[:, h * P:(h + 1) * P], start=True, stop=False)
                    if not sample:
                        last = nc.tensor.matmul(y, dH[:, 64 * h:64 * h + 64], dEG[:, h * P:(h + 1) * P],
                                                start=False, stop=True)
                    else:
                        for b in range(NSEQ):
                            last = nc.tensor.matmul(psum[q0:q0 + 64, o0 + SLEN * b:o0 + SLEN * (b + 1)], H0[:, b, h, :],
                                                    dEG[:, h * P + SLEN * b:h * P + SLEN * (b + 1)],
                                                    start=False, stop=(b == NSEQ - 1))
                last.then_inc(d_y, 1)
                for b in range(NSEQ if sample else 1):
                    if sample:
                        pe.wait_ge(d_bm, b + 1)
                    bt = dBM if sample else dB
                    for g in range(2):
                        last = nc.tensor.matmul(bank(7)[:, 256 * g:256 * (g + 1)], bt[:, g * P:(g + 1) * P],
                                                dXW[:, 256 * g:256 * (g + 1)], start=True, stop=True)
                    last.then_inc(d_s, 1)
            end_phase(pe, 7)
            pe_sumsq(pe, "ssd_ss", 0, sq_s)
            end_phase(pe, 8)
            pe_merge(pe, 3)
            end_phase(pe, 9)
            pe_group(pe, "xc", 0, HT, KD, 4)
            pe_group(pe, "gc", 0, HT, KD, 4)
            wl = wait_load(pe, "lru_w", 0)[:, 0:1024].rearrange("p (w m c) -> p w m c", w=2, m=4)
            for m in range(4):
                pe.wait_ge(s_conv, 20 + m + 1)
                for w, name in ((0, "lru_r"), (1, "lru_i")):
                    s, k = FILL[(name, m)]
                    pe.wait_ge(s_free[s], k)
                    for n in range(3):
                        last = nc.tensor.matmul(pset(s)[:, n, :], wl[:, w, m, :], XF[:, m, n * N3:(n + 1) * N3],
                                                start=True, stop=True)
                    last.then_inc(s_fill[s], 1)
            end_phase(pe, 10)
            pe_merge(pe, 2)
            end_phase(pe, 11)
            pe_group(pe, "ua", 0, HT, KD, 4)
            bc = wait_load(pe, "s5_bc", 0)
            pe.wait_ge(a_bs, 1)
            for w in range(2):
                for i in range(4):
                    last = nc.tensor.transpose(bank(6 + w)[:, i * P:(i + 1) * P],
                                               bc[:, 512 * w + P * i:512 * w + P * (i + 1)], ident)
            last.then_inc(a_bt, 1)
            pe.wait_ge(a_btc, 1)
            pe.wait_ge(a_u, 4)
            cc = bc[:, 1024:2048].rearrange("p (w j c) -> p w j c", w=2, c=32)
            for j in range(16):
                i, q = divmod(j, 4)
                for w, name in ((0, "bu_re"), (1, "bu_im")):
                    s, k = FILL[(name, j)]
                    pe.wait_ge(s_free[s], k)
                    for n in range(3):
                        last = nc.tensor.matmul(pset(s)[:, n, :],
                                                sBT[32 * q:32 * q + 32, 512 * w + P * i:512 * w + P * i + P],
                                                U[32 * q:32 * q + 32, i, n * N3:(n + 1) * N3], start=True, stop=True)
                    last.then_inc(s_fill[s], 1)
                pe.wait_ge(a_x, j + 1)
                for n in range(3):
                    b = 3 * j + n
                    if b >= 2:
                        pe.wait_ge(a_ys, b - 1)
                    dst = psum[32 * q:32 * q + 32, 512 * (6 + b % 2):512 * (6 + b % 2) + N3]
                    nc.tensor.matmul(dst, cc[:, 0, j, :], st[2][:, n * N3:(n + 1) * N3], start=True, stop=False)
                    nc.tensor.matmul(dst, cc[:, 1, j, :], st[3][:, n * N3:(n + 1) * N3],
                                     start=False, stop=True).then_inc(a_y, 1)
            wg = wait_load(pe, "glu", 0).rearrange("p (m k c) -> p m k c", m=8, k=KM)
            pe.wait_ge(a_g, 4)
            for m in range(4):
                pe_tile(pe, "glu", m, wg[:, m], U, KM)
            end_phase(pe, 12)
            pe_merge(pe, 0)
            end_phase(pe, 13)
            pe_group(pe, "out", 0, merged, KD, 4)
            pe_group(pe, "out", 1, merged, KD, 4)
            end_phase(pe, 14)
            pe_sumsq(pe, "ss_moe", 0, sq_e)
            pe.wait_ge(s_h, 2)
            wr = wrouter[:, :].rearrange("p (k c) -> p k c", k=KD)
            for c in range(NT):
                for k in range(KD):
                    last = nc.tensor.matmul(bank(6)[:, 16 * c:16 * c + 16], HT[:, k, c * P:(c + 1) * P], wr[:, k, :],
                                            start=(k == 0), stop=(k == KD - 1))
            last.then_inc(m_r, 1)
            pe.wait_ge(m_gate, 1)
            for c in range(NT):
                last = nc.tensor.transpose(psum[0:16, P * c:P * (c + 1)], gates[:, 16 * c:16 * c + 16], ident)
            last.then_inc(m_gt, 1)
            end_phase(pe, 15)
            for e in range(NE):
                wg = wait_load(pe, "hg%d" % e, 0).rearrange("p (m k c) -> p m k c", m=4, k=KD)
                wu = wait_load(pe, "hu%d" % e, 0).rearrange("p (m k c) -> p m k c", m=4, k=KD)
                for n in range(3):
                    b = 3 * e + n
                    if b >= 2:
                        pe.wait_ge(m_gbc, b - 1)
                    nc.tensor.matmul(bank(6 + b % 2)[:, 0:N3], ident[0:16, e:e + 1].to_broadcast([16, P]),
                                     gateT[0:16, n * N3:(n + 1) * N3], start=True, stop=True).then_inc(m_gb, 1)
                for m in range(4):
                    pe_tile(pe, "hg%d" % e, m, wg[:, m], HT, KD)
                    pe_tile(pe, "hu%d" % e, m, wu[:, m], HT, KD)
                pe.wait_ge(m_hid, 4 * (e + 1))
                wd = wait_load(pe, "down%d" % e, 0).rearrange("p (m k c) -> p m k c", m=8, k=KM)
                for m in range(KD):
                    pe_tile(pe, "down%d" % e, m, wd[:, m], hid, KM)
            end_phase(pe, 16)
            pe_sumsq(pe, "ss_final", 0, sq_e)
            end_phase(pe, 17)

        @block.scalar
        def _(act):
            S = Steps(act, s_act)
            act.wait_ge(s_const, 16 * 6)
            act.wait_ge(s_x, 16)
            S.then(nc.scalar.activation(cond[:, :], cond[:, :], ACT.Silu), s_cond)
            act_sumsq(act, "ss_mix", 0, sq_a, [X[:, k, :] for k in range(KD)])
            act_root(S, "ss_mix", 0, rt_a, 1.0 / D)
            S.then(nc.scalar.activation(nexpa, v_("alog")[0:16], ACT.Exp))
            act.wait_ge(r_z, 1)
            S.then(nc.scalar.activation(rowt[1][0:16], rowt[0][0:16], ACT.Abs))
            S.then(nc.scalar.activation(rowt[1][0:16], rowt[1][0:16], ACT.Exp, scale=-1.0))
            S.then(nc.scalar.activation(rowt[1][0:16], rowt[1][0:16], ACT.Ln, bias=ones[0:16, 0:1]), r_l)
            S.then(nc.scalar.activation(rows[64:80, :], rowt[0][0:16], ACT.Sigmoid))
            end_phase(act, 0)
            for m in range(12):
                act_conv_in(S, "qkv", m, m, cb_g)
                if m:
                    act.wait_ge(s_conv, m)
                    nc.scalar.activation(QKV[:, m - 1, :], QKV[:, m - 1, :], ACT.Silu)
            act.wait_ge(s_conv, 12)
            nc.scalar.activation(QKV[:, 11, :], QKV[:, 11, :], ACT.Silu)
            for m in range(KM):
                s = wait_fill(act, "zb", m)
                nc.scalar.activation(tri3(Y[:, m, :]), pset(s), ACT.Silu).then_inc(s_free[s], 1)
            end_phase(act, 1)
            for m in range(8):
                act_sumsq(act, "qkn", m, sq_a, [QKV[:, m, :]])
                act_root(S, "qkn", m, rt_a, 1.0)
            end_phase(act, 2)
            for c in range(NT):
                sample = c == NC7
                act.wait_ge(c_cols, c + 1)
                nc.scalar.activation(colE, colG[:, 0:16], ACT.Exp)
                act.wait_ge(c_diff, c + 1)
                nc.scalar.activation(cEG, bank(0), ACT.Exp)
                nc.scalar.activation(cDT, cDT, ACT.Exp).then_inc(c_exp, 1)
                for n in range(LEV0[c], LEV0[c] + LEV[c]):
                    act.wait_ge(c_p, n + 1)
                    nc.scalar.activation(cPS, bank(0), ACT.Copy).then_inc(c_ps, 1)
                act.wait_ge(c_u, c + (2 if sample else 1))
                nc.scalar.activation(cU, bank(7 if sample else 4), ACT.Copy).then_inc(c_us, 1)
            end_phase(act, 3)
            for m in range(GH):
                act_sumsq(act, "gdn_ss", m, sq_a, [QKV[:, m, :]])
                act_root(S, "gdn_ss", m, rt_a, 1.0 / P)
            end_phase(act, 4)
            act_merge(act, 1)
            end_phase(act, 5)
            for m in range(8):
                act_conv_in(S, "xbc", m, 12 + m, cb_s)
                if m:
                    act.wait_ge(s_conv, 12 + m)
                    nc.scalar.activation(XBC[:, m - 1, :], XBC[:, m - 1, :], ACT.Silu)
            act.wait_ge(s_conv, 20)
            nc.scalar.activation(XBC[:, 7, :], XBC[:, 7, :], ACT.Silu)
            for m in range(KM):
                s = wait_fill(act, "zd", m)
                nc.scalar.activation(tri3(Y[:, m, :]), pset(s), ACT.Silu).then_inc(s_free[s], 1)
            end_phase(act, 6)
            for c in range(NT):
                act.wait_ge(d_diff, c + 1)
                nc.scalar.activation(dDT, dDT, ACT.Exp)
                nc.scalar.activation(dEG, psum[:, 0:1024], ACT.Exp).then_inc(d_exp, 1)
            act.wait_ge(s_pstate, 16 * 4)
            end_phase(act, 7)
            act.wait_ge(d_gated, KM)
            act_sumsq(act, "ssd_ss", 0, sq_s, [XBC[:, m, :] for m in range(KM)])
            act_root(S, "ssd_ss", 0, rt_s, 1.0 / MIX)
            end_phase(act, 8)
            act_merge(act, 3)
            end_phase(act, 9)
            lam = v_("lru_lambda", 0, 4)
            S.then(nc.scalar.activation(lruc[:, 8:12], lam, ACT.Abs))
            S.then(nc.scalar.activation(lruc[:, 8:12], lruc[:, 8:12], ACT.Exp, scale=-1.0))
            S.then(nc.scalar.activation(lruc[:, 8:12], lruc[:, 8:12], ACT.Ln, bias=ones[:, 0:1]), l_sp)
            for m in range(4):
                act_conv_in(S, "xc", m, 20 + m, cb_l)
            for m in range(4):
                s = wait_fill(act, "gc", m)
                nc.scalar.activation(tri3(Y[:, m, :]), pset(s), ACT.Gelu_apprx_tanh).then_inc(s_free[s], 1)
            act.wait_ge(l_col, 1)
            for m in range(4):
                s = wait_fill(act, "lru_r", m)
                if m:
                    act.wait_ge(l_done, m)
                nc.scalar.activation(tri3(lt[0]), pset(s), ACT.Sigmoid, bias=v_("lru_b_a", m)).then_inc(s_free[s], 1)
                freed(act, "lru_r", m)
                s = wait_fill(act, "lru_i", m)
                nc.scalar.activation(tri3(lt[1]), pset(s), ACT.Sigmoid, bias=v_("lru_b_x", m)).then_inc(s_free[s], 1)
                nc.scalar.activation(lt[2], lt[0], ACT.Exp, scale=lruc[:, 4 + m:5 + m])
                nc.scalar.activation(lt[3], lt[0], ACT.Tanh, scale=lruc[:, m:m + 1]).then_inc(l_a, 1)
                act.wait_ge(l_m, m + 1)
                nc.scalar.activation(lt[4], lt[4], ACT.Sqrt).then_inc(l_b, 1)
            end_phase(act, 10)
            act_merge(act, 2)
            end_phase(act, 11)
            S.then(nc.scalar.activation(s5("dt"), v_("s5_dt", 0, 16), ACT.Exp), a_mag)
            act.wait_ge(a_th, 1)
            nc.scalar.activation(s5("mag"), s5("mag"), ACT.Exp)
            nc.scalar.activation(s5("sin"), s5("sin"), ACT.Sin)
            nc.scalar.activation(s5("cos"), s5("cos"), ACT.Sin).then_inc(a_sin, 1)
            for m in range(4):
                s = wait_fill(act, "ua", m)
                nc.scalar.activation(tri3(U[:, m, :]), pset(s), ACT.Copy).then_inc(s_free[s], 1)
                freed(act, "ua", m)
                act.sem_inc(a_u, 1)
            for j in range(16):
                i, q = divmod(j, 4)
                for n in range(3):
                    b = 3 * j + n
                    act.wait_ge(a_y, b + 1)
                    nc.scalar.activation(Y[32 * q:32 * q + 32, i, n * N3:(n + 1) * N3],
                                         psum[32 * q:32 * q + 32, 512 * (6 + b % 2):512 * (6 + b % 2) + N3],
                                         ACT.Copy).then_inc(a_ys, 1)
            for m in range(4):
                act.wait_ge(a_yd, m + 1)
                nc.scalar.activation(U[:, m, :], Y[:, m, :], ACT.Gelu_apprx_tanh).then_inc(a_g, 1)
            for m in range(4):
                s = wait_fill(act, "glu", m)
                nc.scalar.activation(tri3(st[m]), pset(s), ACT.Sigmoid).then_inc(s_free[s], 1)
            end_phase(act, 12)
            act_merge(act, 0)
            end_phase(act, 13)
            end_phase(act, 14)
            act_sumsq(act, "ss_moe", 0, sq_e, [X[:, k, :] for k in range(KD)])
            act_root(S, "ss_moe", 0, rt_e, 1.0 / D)
            act.wait_ge(m_r, 1)
            nc.scalar.activation(scores, bank(6)[:, 0:144], ACT.Sigmoid).then_inc(m_sc, 1)
            end_phase(act, 15)
            for e in range(NE):
                for n in range(3):
                    b = 3 * e + n
                    act.wait_ge(m_gb, b + 1)
                    if e >= 2:
                        act.wait_ge(m_hid, 4 * (e - 1))
                    nc.scalar.activation(gbc[e % 2][:, n * N3:(n + 1) * N3], bank(6 + b % 2)[:, 0:N3],
                                         ACT.Copy).then_inc(m_gbc, 1)
                for m in range(4):
                    s = wait_fill(act, "hg%d" % e, m)
                    if 4 * e + m >= 2:
                        act.wait_ge(m_hid, 4 * e + m - 1)
                    nc.scalar.activation(tri3(sg[m % 2]), pset(s), ACT.Silu).then_inc(s_free[s], 1)
            end_phase(act, 16)
            act_sumsq(act, "ss_final", 0, sq_e, [X[:, k, :] for k in range(KD)])
            act_root(S, "ss_final", 0, rt_e, 1.0 / D)
            end_phase(act, 17)

        @block.vector
        def _(dve):
            V = Steps(dve, s_dve)
            tt, ts, stt = nc.vector.tensor_tensor, nc.vector.tensor_scalar, nc.vector.scalar_tensor_tensor

            dve.wait_ge(s_const, 16 * 6)
            dve.wait_ge(s_ada, 12)
            V.then(tt(mod3, bank(6)[:, 0:432].rearrange("p (m s) -> p m s", s=9), over(v_("b_ada", 0, 48), 9), ALU.add))
            for w, scale, nw in ((0, 8, "norm_mix"), (1, 32, "norm_moe")):
                V.then(ts(amul3[:, w], mod3[:, scale:scale + 8, :], 1.0, None, ALU.add))
                V.then(tt(amul3[:, w], amul3[:, w], over(v_(nw, 0, 8), 9), ALU.mult))
            dve.wait_ge(s_x, 16)
            dve_recip(V, "ss_mix", 0, rs_a, rt_a)
            V.rs = rs_a
            dve_norm(V, X, HT, amul3[:, 0], mod3[:, 0:8, :])
            V.then(nc.vector.memset(rows[0:64, :], 0.0))
            s = wait_fill(dve, "rows", 0)
            ts(tri3(rowt[0][0:16]), pset(s)[0:16], v_("dtb")[0:16], None, ALU.add).then_inc(s_free[s], 1)
            freed(dve, "rows", 0)
            dve.sem_inc(r_z, 1)
            dve.wait_ge(r_l, 1)
            V.then(stt(out=rowt[3][0:16], in0=rowt[0][0:16], scalar=0.0, in1=rowt[1][0:16], op0=ALU.max, op1=ALU.add))
            V.then(nc.vector.tensor_copy(rows[32:48, :], rowt[3][0:16]))
            V.then(ts(rowt[2][0:16], rowt[3][0:16], nexpa, -1.0, ALU.mult, ALU.mult))
            V.then(nc.vector.memset(rowt[1][0:16], 1.0))
            V.then(nc.vector.memset(rowt[1][0:16, 0:NP_TOK:P], 0.0))
            V.then(nc.vector.memset(rowt[1][0:16, NP_TOK:T:SLEN], 0.0))
            V.then(nc.vector.tensor_tensor_scan(rows[0:16, :], rowt[1][0:16], rowt[2][0:16], 0.0, ALU.mult, ALU.add))
            end_phase(dve, 0)
            dve_cb_start(V, cb_g)
            for m in range(12):
                dve_conv(V, m, cb_g, QKV[:, m, :], "gdn_conv", m, 12)
            end_phase(dve, 1)
            for m in range(8):
                dve_recip(V, "qkn", m, rs_a, rt_a)
                V.then(stt(out=QKV[:, m, :], in0=QKV[:, m, :], scalar=(P ** -0.5 if m < 4 else 1.0), in1=rs_a,
                           op0=ALU.mult, op1=ALU.mult))
            end_phase(dve, 2)
            V.then(nc.vector.memset(cS, 0.0))
            for c in range(NT):
                t0 = c * P
                sample = c == NC7
                dve.wait_ge(c_bc, c + 1)
                V.then(nc.vector.tensor_copy(colG, bank(2)[:, 0:80]), c_cols)
                V.then(tt(hd(cDT, 4), hd(bank(0), 4), over(colG[:, 0:4], P), ALU.subtract))
                V.then(tt(hd(cDT, 4), hd(cDT, 4), by(c_("neg_sample" if sample else "neg_prompt"), 4), ALU.add), c_diff)
                dve.wait_ge(c_exp, c + 1)
                dve.wait_ge(c_gram, c + 1)
                V.then(tt(cLT, cDT, bank(3), ALU.mult))
                V.then(tt(cLT, cLT, bank(1), ALU.mult))
                V.then(tt(cAT, cDT, bank(4), ALU.mult))
                V.then(tt(hd(cQE, 4), QKV[:, 0:4, t0:t0 + P], hd(cEG, 4), ALU.mult))
                V.then(tt(colB, colG[:, 76:80], colE[:, 0:4], ALU.mult))
                if sample:
                    V.then(tt(hd(cUM[:, 0:512], 4), hd(cDT, 4), by(c_("last"), 4), ALU.mult))
                    V.then(nc.vector.reduce_sum(colK[:, 0:4], hd(cUM[:, 0:512], 4), axis=AX.X))
                else:
                    V.then(nc.vector.tensor_copy(colK[:, 0:4], hd(cDT, 4)[:, :, P - 1]))
                dve.wait_ge(c_tok, c + 1)
                V.then(tt(hd(cKE, 4), hd(bank(5), 4), over(colK[:, 0:4], P), ALU.mult))
                V.then(tt(hd(cKB, 4), hd(bank(5), 4), over(colB, P), ALU.mult))
                V.then(tt(hd(cVB, 4), hd(bank(6), 4), over(colG[:, 76:80], P), ALU.mult))
                V.then(nc.vector.tensor_copy(hd(cX, 4), by(ident, 4)))
                V.then(nc.vector.tensor_copy(hd(cXT, 4), by(ident, 4)), c_ops)
                for lv in range(LEV[c]):
                    n = LEV0[c] + lv
                    V.then(tt(hd(cLK, 4), hd(cLT, 4), by(c_("level", P * lv, P), 4), ALU.mult), c_lk)
                    dve.wait_ge(c_d, n + 1)
                    V.then(tt(cX, cX, bank(1), ALU.subtract))
                    V.then(tt(cXT, cXT, bank(2), ALU.subtract), c_x)
                dve.wait_ge(c_w, c + 1)
                V.then(ts(cNW, bank(3), -1.0, None, ALU.mult), c_nw)
                if sample:
                    dve.wait_ge(c_u, c + 1)
                    V.then(nc.vector.tensor_copy(cPS, bank(4)), c_ut)
                dve.wait_ge(c_o, c + 1)
                V.then(nc.vector.tensor_copy(QKV[:, 0:4, t0:t0 + P], hd(bank(5), 4)), c_os)
                if not sample:
                    dve.wait_ge(c_s, c + 1)
                    V.then(tt(hd(cS, 4), hd(cS, 4), hd(cEG, 4)[:, :, P - 1:P].to_broadcast([P, 4, P]), ALU.mult))
                    V.then(tt(cS, cS, bank(6), ALU.add), c_ss)
                else:
                    S0 = wait_load(dve, "gdn_state", 0).rearrange("p (b h v) -> p b h v", b=NSEQ, h=GH)
                    dve.wait_ge(c_us, c + 1)
                    for h in range(GH):
                        V.then(tt(hd(cUM, 8), by(cU[:, h * P:(h + 1) * P], 8), over(c_("row"), P), ALU.mult), c_um)
                        dve.wait_ge(c_s, c + h + 1)
                        V.then(tt(S0[:, :, h, :], S0[:, :, h, :],
                                  over(cEG[:, h * P + SLEN - 1:(h + 1) * P:SLEN], P), ALU.mult))
                        V.then(tt(S0[:, :, h, :], S0[:, :, h, :], hd(psum[:, 0:1024], 8), ALU.add), c_ss)
            end_phase(dve, 3)
            for m in range(GH):
                dve_recip(V, "gdn_ss", m, rs_a, rt_a)
                V.then(stt(out=QKV[:, m, :], in0=QKV[:, m, :], scalar=v_("gdn_norm"), in1=rs_a, op0=ALU.mult, op1=ALU.mult))
                V.then(tt(Y[:, m, :], Y[:, m, :], QKV[:, m, :], ALU.mult))
            dve.wait_ge(s_pstate, 32)
            end_phase(dve, 4)
            dve_merge(V, 1)
            end_phase(dve, 5)
            dve_cb_start(V, cb_s)
            for m in range(8):
                dve_conv(V, 12 + m, cb_s, XBC[:, m, :], "ssd_conv", m, 8, bias=v_("ssd_conv_b", m))
            end_phase(dve, 6)
            V.then(nc.vector.memset(dH, 0.0))
            for c in range(NT):
                t0 = c * P
                sample = c == NC7
                dve.wait_ge(d_bc, c + 1)
                V.then(nc.vector.tensor_copy(colG, bank(2)[:, 0:80]))
                V.then(tt(hd(dDT, 8), hd(psum[:, 0:1024], 8), over(colG[:, 4:12], P), ALU.subtract))
                V.then(tt(hd(dDT, 8), hd(dDT, 8), by(c_("neg_sample" if sample else "neg_prompt"), 8), ALU.add), d_diff)
                V.then(nc.vector.tensor_copy(dB, bank(4)[:, 0:256]))
                V.then(tt(hd(dXD, 8), hd(bank(5), 8), over(colG[:, 36:44], 64), ALU.mult))
                dve.wait_ge(d_exp, c + 1)
                if sample:
                    for g in range(2):
                        V.then(tt(hd(dTMP, 4), hd(dDT[:, 512 * g:512 * (g + 1)], 4), by(c_("last"), 4), ALU.mult))
                        V.then(nc.vector.reduce_sum(colK[:, 4 * g:4 * g + 4], hd(dTMP, 4), axis=AX.X))
                    V.then(nc.vector.tensor_copy(hd(colL, 8), hd(dEG, 8)[:, :, SLEN - 1:P:SLEN]))
                else:
                    V.then(nc.vector.tensor_copy(colK, hd(dDT, 8)[:, :, P - 1]))
                    V.then(nc.vector.tensor_copy(colL[:, 0:8], hd(dEG, 8)[:, :, P - 1]))
                V.then(tt(colW, colK, colG[:, 36:44], ALU.mult))
                V.then(tt(hd(dXW, 8), hd(bank(5), 8), over(colW, 64), ALU.mult))
                d4 = dDT.rearrange("p (g h t) -> p g h t", g=2, h=4)
                e4 = dEG.rearrange("p (g h t) -> p g h t", g=2, h=4)
                V.then(tt(d4, d4, hd(bank(3)[:, 0:256], 2).unsqueeze(2).to_broadcast([P, 2, 4, P]), ALU.mult))
                V.then(tt(e4, e4, XBC[:, 6:8, t0:t0 + P].unsqueeze(2).to_broadcast([P, 2, 4, P]), ALU.mult), d_ops)
                dve.wait_ge(d_y, c + 1)
                for m in range(KM):
                    V.then(stt(out=XBC[:, m, t0:t0 + P], in0=XBC[:, m, t0:t0 + P], scalar=v_("ssd_d", m),
                               in1=bank(6)[:, m * P:(m + 1) * P], op0=ALU.mult, op1=ALU.add),
                           d_ys if m == KM - 1 else None)
                if not sample:
                    dve.wait_ge(d_s, c + 1)
                    V.then(tt(hd(dH, 8), hd(dH, 8), over(colL[:, 0:8], 64), ALU.mult))
                    V.then(tt(dH, dH, bank(7), ALU.add), d_ss)
                else:
                    H0 = wait_load(dve, "ssd_state", 0).rearrange("p (b h d) -> p b h d", b=NSEQ, h=SH)
                    for b in range(NSEQ):
                        V.then(ts(dBM, dB, c_("row", b, 1), None, ALU.mult), d_bm)
                        dve.wait_ge(d_s, c + b + 1)
                        V.then(tt(H0[:, b], H0[:, b], over(hd(colL, 8)[:, :, b], 64), ALU.mult))
                        V.then(tt(H0[:, b], H0[:, b], hd(bank(7), 8), ALU.add), d_ss)
            end_phase(dve, 7)
            for m in range(KM):
                V.then(tt(XBC[:, m, :], XBC[:, m, :], Y[:, m, :], ALU.mult), d_gated)
            dve_recip(V, "ssd_ss", 0, rs_s, rt_s)
            for m in range(KM):
                V.then(stt(out=Y[:, m, :], in0=XBC[:, m, :], scalar=v_("ssd_norm", m), in1=rs_s, op0=ALU.mult, op1=ALU.mult))
            end_phase(dve, 8)
            dve_merge(V, 3)
            end_phase(dve, 9)
            lam = v_("lru_lambda", 0, 4)
            V.then(ts(lruc[:, 12:16], lam, -1.0, 0.0, ALU.mult, ALU.max))
            dve.wait_ge(l_sp, 1)
            V.then(tt(lruc[:, 12:16], lruc[:, 12:16], lruc[:, 8:12], ALU.add))
            V.then(ts(lruc[:, 0:4], lruc[:, 12:16], 8.0, None, ALU.mult))
            V.then(ts(lruc[:, 4:8], lruc[:, 12:16], -8.0, None, ALU.mult), l_col)
            dve_cb_start(V, cb_l)
            for m in range(4):
                dve_conv(V, 20 + m, cb_l, XF[:, m, :], "lru_conv", m, 4, bias=v_("lru_conv_b", m))
            lo = lru_out[:, :].rearrange("p (m b) -> p m b", b=9)
            for m in range(4):
                a, b = lt[2], lt[5]
                first = slice(NP_TOK, T, SLEN)
                dve.wait_ge(l_a, m + 1)
                V.then(tt(lt[4], a, a, ALU.mult))
                V.then(stt(out=lt[4], in0=lt[4], scalar=1.0, in1=lt[3], op0=ALU.add, op1=ALU.mult), l_m)
                V.then(tt(b, lt[1], XF[:, m, :], ALU.mult))
                dve.wait_ge(l_b, m + 1)
                V.then(tt(b, b, lt[4], ALU.mult))
                V.then(tt(lruc[:, 16:24], a[:, first], v_("lru_h0", 8 * m, 8), ALU.mult))
                V.then(tt(b[:, first], b[:, first], lruc[:, 16:24], ALU.add))
                V.then(nc.vector.memset(a[:, first], 0.0))
                V.then(nc.vector.tensor_tensor_scan(b, a, b, 0.0, ALU.mult, ALU.add))
                V.then(nc.vector.tensor_copy(lo[:, m, 0:1], b[:, NP_TOK - 1:NP_TOK]))
                V.then(nc.vector.tensor_copy(lo[:, m, 1:9], b[:, NP_TOK + SLEN - 1:T:SLEN]))
                freed(dve, "gc", m)
                V.then(tt(Y[:, m, :], Y[:, m, :], b, ALU.mult), l_done)
            end_phase(dve, 10)
            dve_merge(V, 2)
            end_phase(dve, 11)
            are, aim = v_("s5_re", 0, 16), v_("s5_im", 0, 16)
            dve.wait_ge(a_mag, 1)
            V.then(tt(s5("mag"), are, s5("dt"), ALU.mult))
            V.then(tt(s5("th"), aim, s5("dt"), ALU.mult))

            def reduce_angle(dst, shift):
                V.then(ts(s5("t1"), s5("th"), shift, None, ALU.add))
                V.then(ts(s5("t0"), s5("t1"), float(1 / (2 * np.pi)), ROUND, ALU.mult, ALU.add))
                V.then(ts(s5("t0"), s5("t0"), ROUND, None, ALU.subtract))
                V.then(stt(out=s5("t1"), in0=s5("t0"), scalar=-TWO_PI_HI, in1=s5("t1"), op0=ALU.mult, op1=ALU.add))
                V.then(stt(out=s5("t1"), in0=s5("t0"), scalar=-TWO_PI_LO, in1=s5("t1"), op0=ALU.mult, op1=ALU.add))
                V.then(ts(dst, s5("t1"), 3.141592, -3.141592, ALU.min, ALU.max))

            reduce_angle(s5("sin"), 0.0)
            reduce_angle(s5("cos"), float(np.pi / 2))
            dve.sem_inc(a_th, 1)
            dve.wait_ge(a_sin, 1)
            V.then(tt(s5("lre"), s5("mag"), s5("cos"), ALU.mult))
            V.then(tt(s5("lim"), s5("mag"), s5("sin"), ALU.mult))
            V.then(tt(s5("den"), are, are, ALU.mult))
            V.then(tt(s5("t0"), aim, aim, ALU.mult))
            V.then(tt(s5("den"), s5("den"), s5("t0"), ALU.add))
            V.then(nc.vector.reciprocal(s5("den"), s5("den")))
            V.then(ts(s5("t0"), s5("lre"), -1.0, None, ALU.add))
            V.then(tt(s5("fre"), s5("t0"), are, ALU.mult))
            V.then(tt(s5("t1"), s5("lim"), aim, ALU.mult))
            V.then(tt(s5("fre"), s5("fre"), s5("t1"), ALU.add))
            V.then(tt(s5("fre"), s5("fre"), s5("den"), ALU.mult))
            V.then(tt(s5("fim"), s5("lim"), are, ALU.mult))
            V.then(tt(s5("t1"), s5("t0"), aim, ALU.mult))
            V.then(tt(s5("fim"), s5("fim"), s5("t1"), ALU.subtract))
            V.then(tt(s5("fim"), s5("fim"), s5("den"), ALU.mult))
            V.then(nc.vector.tensor_copy(s5("pr", 0), s5("cos")))
            V.then(nc.vector.tensor_copy(s5("pi", 0), s5("sin")))
            for k in range(9):
                V.then(tt(s5("t0"), s5("pi", k), s5("pi", k), ALU.mult))
                V.then(tt(s5("pr", k + 1), s5("pr", k), s5("pr", k), ALU.mult))
                V.then(tt(s5("pr", k + 1), s5("pr", k + 1), s5("t0"), ALU.subtract))
                V.then(tt(s5("t0"), s5("pr", k), s5("pi", k), ALU.mult))
                V.then(ts(s5("pi", k + 1), s5("t0"), 2.0, None, ALU.mult))
            x0 = [v_("s5_x0r", 0, 128).rearrange("p (j b) -> p j b", b=8),
                  v_("s5_x0i", 0, 128).rearrange("p (j b) -> p j b", b=8)]
            xs = [s5x[:, 128 * w:128 * (w + 1)].rearrange("p (j b) -> p j b", b=8) for w in range(2)]
            xt = small[:, 256:384].rearrange("p (j b) -> p j b", b=8)
            V.then(tt(xs[0], x0[0], over(s5("lre"), 8), ALU.mult))
            V.then(tt(xt, x0[1], over(s5("lim"), 8), ALU.mult))
            V.then(tt(xs[0], xs[0], xt, ALU.subtract))
            V.then(tt(xs[1], x0[1], over(s5("lre"), 8), ALU.mult))
            V.then(tt(xt, x0[0], over(s5("lim"), 8), ALU.mult))
            V.then(tt(xs[1], xs[1], xt, ALU.add))
            bc = wait_load(dve, "s5_bc", 0)
            br, bi = [bc[:, 512 * w:512 * (w + 1)].rearrange("p (j c) -> p j c", c=32) for w in range(2)]
            t = [x[:, 0:512].rearrange("p (j c) -> p j c", c=32) for x in st[0:4]]
            V.then(tt(t[0], br, over(s5("fre"), 32), ALU.mult))
            V.then(tt(t[1], bi, over(s5("fim"), 32), ALU.mult))
            V.then(tt(t[2], bi, over(s5("fre"), 32), ALU.mult))
            V.then(tt(t[3], br, over(s5("fim"), 32), ALU.mult))
            V.then(tt(br, t[0], t[1], ALU.subtract))
            V.then(tt(bi, t[2], t[3], ALU.add), a_bs)
            dve.wait_ge(a_bt, 1)
            V.then(nc.vector.tensor_copy(sBT, psum[:, 6 * 512:8 * 512]), a_btc)
            V.then(nc.vector.memset(sMASK, 1.0))
            V.then(nc.vector.memset(sMASK[:, NP_TOK:T:SLEN], 0.0))
            so = s5_out[:, :].rearrange("p (w j b) -> p w j b", w=2, b=9)
            first = slice(NP_TOK, T, SLEN)
            for j in range(16):
                V.then(nc.vector.memset(sCOS[:, 0:1], 1.0))
                V.then(nc.vector.memset(sSIN[:, 0:1], 0.0))
                for k in range(10):
                    n = 1 << k
                    pr, pi = s5("pr", k)[:, j:j + 1], s5("pi", k)[:, j:j + 1]
                    ts(st[0][:, 0:n], sSIN[:, 0:n], pi, None, ALU.mult)
                    V.then(ts(st[1][:, 0:n], sCOS[:, 0:n], pi, None, ALU.mult))
                    stt(out=sCOS[:, n:2 * n], in0=sCOS[:, 0:n], scalar=pr, in1=st[0][:, 0:n], op0=ALU.mult, op1=ALU.subtract)
                    V.then(stt(out=sSIN[:, n:2 * n], in0=sSIN[:, 0:n], scalar=pr, in1=st[1][:, 0:n],
                               op0=ALU.mult, op1=ALU.add))
                nc.vector.tensor_copy(seqs(sCOS), by(sCOS[:, 0:SLEN], 8))
                V.then(nc.vector.tensor_copy(seqs(sSIN), by(sSIN[:, 0:SLEN], 8)))
                sA, sB = wait_fill(dve, "bu_re", j), wait_fill(dve, "bu_im", j)
                c3, s3 = tri3(sCOS), tri3(sSIN)
                tt(tri3(st[0]), pset(sA), c3, ALU.mult)
                V.then(tt(tri3(st[1]), pset(sB), s3, ALU.mult))
                V.then(tt(st[4], st[0], st[1], ALU.add))
                tt(tri3(st[0]), pset(sA), s3, ALU.mult).then_inc(s_free[sA], 1)
                tt(tri3(st[1]), pset(sB), c3, ALU.mult).then_inc(s_free[sB], 1)
                freed(dve, "bu_re", j)
                freed(dve, "bu_im", j)
                V.then(tt(st[5], st[1], st[0], ALU.subtract))
                tt(st[4][:, first], st[4][:, first], xs[0][:, j, :], ALU.add)
                tt(st[5][:, first], st[5][:, first], xs[1][:, j, :], ALU.add)
                V.then(ts(st[0], sMASK, s5("mag")[:, j:j + 1], None, ALU.mult))
                nc.vector.tensor_tensor_scan(st[4], st[0], st[4], 0.0, ALU.mult, ALU.add)
                V.then(nc.vector.tensor_tensor_scan(st[5], st[0], st[5], 0.0, ALU.mult, ALU.add))
                tt(st[0], st[4], sCOS, ALU.mult)
                V.then(tt(st[1], st[5], sSIN, ALU.mult))
                if j:
                    dve.wait_ge(a_y, 3 * j)
                V.then(tt(st[2], st[0], st[1], ALU.subtract))
                tt(st[0], st[4], sSIN, ALU.mult)
                V.then(tt(st[1], st[5], sCOS, ALU.mult))
                V.then(stt(out=st[3], in0=st[0], scalar=-1.0, in1=st[1], op0=ALU.mult, op1=ALU.subtract), a_x)
                nc.vector.tensor_copy(so[:, 0, j, 0:1], st[2][:, NP_TOK - 1:NP_TOK])
                nc.vector.tensor_copy(so[:, 0, j, 1:9], st[2][:, NP_TOK + SLEN - 1:T:SLEN])
                ts(so[:, 1, j, 0:1], st[3][:, NP_TOK - 1:NP_TOK], -1.0, None, ALU.mult)
                V.then(ts(so[:, 1, j, 1:9], st[3][:, NP_TOK + SLEN - 1:T:SLEN], -1.0, None, ALU.mult))
            for m in range(4):
                dve.wait_ge(a_ys, 12 * (m + 1))
                V.then(stt(out=Y[:, m, :], in0=U[:, m, :], scalar=v_("s5_d", m), in1=Y[:, m, :], op0=ALU.mult, op1=ALU.add),
                       a_yd)
            for m in range(4):
                freed(dve, "glu", m)
                V.then(tt(Y[:, m, :], U[:, m, :], st[m], ALU.mult), a_gs)
            end_phase(dve, 12)
            dve_merge(V, 0)
            end_phase(dve, 13)
            dve.wait_ge(s_xr, 16)
            for m in range(KD):
                dve_residual(V, "out", m, 16, hid[:, 0, :])
            end_phase(dve, 14)
            dve_recip(V, "ss_moe", 0, rs_e, rt_e)
            V.rs = rs_e
            dve_norm(V, X, HT, amul3[:, 1], mod3[:, 24:32, :])
            dve.wait_ge(m_sc, 1)
            V.then(tt(hd(rsel, 9), hd(scores, 9), by(v_("rbias", 0, NE), 9), ALU.add))

            def ranks(dst, src, n):
                s4 = src.rearrange("p (n j) -> p n j", j=4)
                si, sj = s4.unsqueeze(2).to_broadcast([P, n, 4, 4]), s4.unsqueeze(3).to_broadcast([P, n, 4, 4])
                ca = cmpA[:, 0:16 * n].rearrange("p (n j i) -> p n j i", j=4, i=4)
                cb_ = cmpB[:, 0:16 * n].rearrange("p (n j i) -> p n j i", j=4, i=4)
                V.then(tt(ca, si, sj, ALU.is_gt))
                V.then(tt(cb_, si, sj, ALU.is_equal))
                V.then(tt(cmpB[:, 0:16 * n].rearrange("p (n x) -> p n x", x=16),
                          cmpB[:, 0:16 * n].rearrange("p (n x) -> p n x", x=16), by(c_("tri"), n), ALU.mult))
                V.then(tt(cmpA[:, 0:16 * n], cmpA[:, 0:16 * n], cmpB[:, 0:16 * n], ALU.add))
                V.then(nc.vector.reduce_sum(dst.rearrange("p (n j) -> p n j", j=4), ca, axis=AX.X))

            ranks(rank, rsel, 36)
            V.then(ts(top, rank, 1.5, None, ALU.is_lt))
            V.then(tt(rw, top, rsel, ALU.mult))
            V.then(nc.vector.reduce_sum(grp[:, 0:36], rw.rearrange("p (n j) -> p n j", j=4), axis=AX.X))
            ranks(grp[:, 36:72], grp[:, 0:36], 9)
            V.then(ts(grp[:, 36:72], grp[:, 36:72], 0.5, None, ALU.is_lt))
            V.then(tt(rw, scores, top, ALU.mult))
            V.then(tt(hd(rw, 36), hd(rw, 36), over(grp[:, 36:72], 4), ALU.mult))
            V.then(nc.vector.reduce_sum(grp[:, 72:81], hd(rw, 9), axis=AX.X))
            V.then(nc.vector.reciprocal(grp[:, 72:81], grp[:, 72:81]))
            V.then(tt(hd(gates, 9), hd(rw, 9), over(grp[:, 72:81], NE), ALU.mult), m_gate)
            dve.wait_ge(m_gt, 1)
            V.then(nc.vector.tensor_copy(gateT[0:16, :], psum[0:16, 0:T]), m_gtc)
            end_phase(dve, 15)
            for e in range(NE):
                dve.wait_ge(m_gbc, 3 * (e + 1))
                for m in range(4):
                    freed(dve, "hg%d" % e, m)
                    s = wait_fill(dve, "hu%d" % e, m)
                    tt(tri3(hid[:, m, :]), tri3(sg[m % 2]), pset(s), ALU.mult).then_inc(s_free[s], 1)
                    freed(dve, "hu%d" % e, m)
                    V.then(tt(hid[:, m, :], hid[:, m, :], gbc[e % 2], ALU.mult), m_hid)
                for m in range(KD):
                    dve_residual(V, "down%d" % e, m, 40, res_tmp)
            end_phase(dve, 16)
            dve_recip(V, "ss_final", 0, rs_e, rt_e)
            for k in range(KD):
                V.then(stt(out=HT[:, k, :], in0=X[:, k, :], scalar=v_("norm_final", k), in1=rs_e, op0=ALU.mult, op1=ALU.mult))
            end_phase(dve, 17)


def _outs():
    return {"yT": (P, KD, T), "hist_out": (P, 24 * 27), "s5_out": (P, 288), "lru_out": (P, 36),
            "gdn_p": (P, 512), "gdn_s": (P, 4096), "ssd_p": (P, 512), "ssd_s": (P, 4096)}


def _constants():
    c = np.zeros((P, NCST), np.float32)

    def put(name, a):
        o, w = CST[name]
        c[:, o:o + w] = a
    s, t = np.arange(P)[:, None], np.arange(P)[None, :]
    put("ident", np.eye(P))
    put("ones", 1.0)
    put("level", np.concatenate([(s >> (k + 1) == t >> (k + 1)) & ((s >> k) & 1 == 0) & ((t >> k) & 1 == 1)
                                 for k in range(7)], axis=1))
    put("neg_prompt", np.where(t >= s, 0.0, -1e30))
    put("neg_sample", np.where((t >= s) & (t // SLEN == s // SLEN), 0.0, -1e30))
    put("last", np.broadcast_to(t % SLEN == SLEN - 1, (P, P)))
    put("row", s // SLEN == np.arange(NSEQ)[None, :])
    put("eps", EPS)
    j, i = np.arange(16) // 4, np.arange(16) % 4
    put("tri", np.broadcast_to(i < j, (P, 16)))
    return c


def _pack(w):
    k, m = w.shape[0] // P, w.shape[1] // P
    per = 32 // k
    a = w.reshape(k, P, m, P).transpose(2, 1, 0, 3).reshape(m // per, per, P, k, P)
    return np.ascontiguousarray(a.transpose(0, 2, 1, 3, 4)).reshape(m // per, P, 4096)


def kernel(**inputs):
    import concourse.bacc as _bacc
    from concourse import mybir as _mybir
    from concourse.bass_utils import run_bass_kernel_spmd as _run

    i = {k: np.asarray(v) for k, v in inputs.items()}
    f = np.float32

    def cols(v):
        return v.reshape(-1, P).T

    def padded(a):
        out = np.zeros((P, 4096), f)
        out[:, :a.shape[1]] = a
        return out[None]

    arr = {"cst": _constants()}
    arr["xT"] = np.ascontiguousarray(np.concatenate([i["x_prompt"].reshape(NP_TOK, D), i["x_sample"].reshape(P, D)])
                                     .T.reshape(KD, P, T).transpose(1, 0, 2))
    c = np.concatenate([i["c_prompt"], i["c_sample"]])
    arr["cT"] = np.ascontiguousarray(c.T.reshape(KD, P, 9).transpose(1, 0, 2)).reshape(P, 72)
    vec = np.zeros((P, NVEC), f)

    def put(name, a):
        o, w = VEC[name]
        vec[:a.shape[0], o:o + w] = a
    for n, src in (("norm_mix", "norm_mix_w"), ("norm_moe", "norm_moe_w"), ("b_ada", "b_ada"), ("s5_d", "s5_d"),
                   ("gdn_norm", "gdn_norm_w"), ("lru_conv_b", "lru_conv_b"), ("lru_b_a", "lru_b_a"),
                   ("lru_b_x", "lru_b_x"), ("lru_lambda", "lru_lambda"), ("ssd_conv_b", "ssd_conv_b"),
                   ("ssd_norm", "ssd_norm_w"), ("s5_re", "s5_a_re"), ("s5_im", "s5_a_im")):
        put(n, cols(i[src][0].reshape(-1)))
    put("norm_final", cols(i["norm_final_w"]))
    for n, src in (("gdn_conv", "gdn_conv_w"), ("lru_conv", "lru_conv_w"), ("ssd_conv", "ssd_conv_w")):
        put(n, cols(i[src][0].reshape(-1)))
    put("ssd_d", cols(np.repeat(i["ssd_d"][0], 64)))
    put("s5_dt", cols(np.repeat(i["s5_log_dt"][0], 64)))
    zero4 = np.zeros(4, f)
    put("alog", np.concatenate([i["gdn_a_log"][0], i["ssd_a_log"][0], zero4])[:, None])
    put("dtb", np.concatenate([i["gdn_dt_bias"][0], i["ssd_dt_bias"][0], zero4])[:, None])
    put("rbias", np.broadcast_to(i["router_bias"], (P, NE)))
    put("lru_h0", i["state_lru"][0].reshape(8, 4, P).transpose(2, 1, 0).reshape(P, 32))
    for n, src in (("s5_x0r", "state_s5_re"), ("s5_x0i", "state_s5_im")):
        put(n, i[src][0].reshape(8, 16, P).transpose(2, 1, 0).reshape(P, 128))
    arr["vec"] = vec
    h = np.concatenate([i["cache_gdn_conv"][0], i["cache_ssd_conv"][0], i["cache_lru_conv"][0]], axis=2)
    arr["hist"] = np.ascontiguousarray(h.reshape(8, 3, 24, P).transpose(3, 2, 0, 1)).reshape(P, 576)
    w = i["w_in"][0]
    o = dict(ua=0, qkv=512, zb=2048, ab=2560, bb=2564, xc=2568, gc=3080, zd=3592, xbc=4104, dt=5128, gate=5136)
    for n, width in (("ua", 512), ("qkv", 1536), ("zb", 512), ("xc", 512), ("gc", 512), ("zd", 512), ("xbc", 1024)):
        arr[n] = _pack(w[:, o[n]:o[n] + width])
    for k in range(4):
        arr["gate%d" % k] = _pack(w[:, o["gate"] + 1024 * k:o["gate"] + 1024 * (k + 1)])
        arr["br%d" % k] = _pack(i["w_branch"][0, k])
    nar = np.concatenate([w[:, o["ab"]:o["ab"] + 4], w[:, o["dt"]:o["dt"] + 8], w[:, o["bb"]:o["bb"] + 4]], axis=1)
    arr["wrows"] = np.ascontiguousarray(nar.reshape(KD, P, 16).transpose(1, 0, 2)).reshape(P, 128)
    arr["wrouter"] = np.ascontiguousarray(i["router_w"].reshape(KD, P, 16).transpose(1, 0, 2)).reshape(P, 128)
    arr["ada"] = _pack(i["w_ada"][0])
    arr["out"] = _pack(i["w_out"][0])
    g = i["s5_w_glu"][0].reshape(4, P, 4, P).transpose(1, 2, 0, 3).reshape(P, 2048)
    arr["glu"] = padded(g)
    for e in range(NE):
        arr["hg%d" % e] = _pack(i["moe_w_gate"][0, e])
        arr["hu%d" % e] = _pack(i["moe_w_up"][0, e])
        arr["down%d" % e] = _pack(i["moe_w_down"][0, e])
    arr["gdn_state"] = np.ascontiguousarray(i["state_gdn"][0].transpose(2, 0, 1, 3)).reshape(1, P, 4096)
    arr["ssd_state"] = np.ascontiguousarray(i["state_ssd"][0].transpose(3, 0, 1, 2)).reshape(1, P, 4096)
    lw = np.zeros((P, 2, 4, P), f)
    for j, n in enumerate(("lru_w_a", "lru_w_x")):
        for b in range(8):
            r = 64 * (b % 2)
            lw[r:r + 64, j, b // 2, r:r + 64] = i[n][0, b]
    arr["lru_w"] = padded(lw.reshape(P, 1024))
    sbc = np.zeros((P, 4, 16, 32), f)
    for j, (n, tr) in enumerate((("s5_b_re", 0), ("s5_b_im", 0), ("s5_c_re", 1), ("s5_c_im", 1))):
        for gr in range(32):
            a = i[n][0, gr]
            a = a.T if tr else a
            r = 64 * (gr % 2)
            sbc[r:r + 64, j, gr // 2, 16 * (gr % 2):16 * (gr % 2) + 16] = a
    arr["s5_bc"] = padded(sbc.reshape(P, 2048))

    nc = _bacc.Bacc("TRN2", target_bir_lowering=False, num_devices=1)
    arrays, aps = {}, {}
    for name, a in arr.items():
        a = np.ascontiguousarray(a)
        arrays["in_" + name] = a
        aps[name] = nc.dram_tensor("in_" + name, a.shape, F32, kind="ExternalInput").ap()
    for name, shape in _outs().items():
        aps[name] = nc.dram_tensor("out_" + name, shape, F32, kind="ExternalOutput").ap()
    build(nc, aps)
    r = _run(nc, [arrays], core_ids=[0]).results[0]
    o = {name: np.asarray(r["out_" + name]) for name in _outs()}
    y = o["yT"].transpose(1, 0, 2).reshape(D, T).T
    ho = o["hist_out"].reshape(P, 24, 9, 3).transpose(2, 3, 1, 0).reshape(9, 3, 24 * P)
    s5 = o["s5_out"].reshape(P, 2, 16, 9).transpose(1, 3, 2, 0).reshape(2, 9, 32, 64)
    lru = o["lru_out"].reshape(P, 4, 9).transpose(2, 1, 0).reshape(9, MIX)
    gp = o["gdn_p"].reshape(P, 1, GH, P).transpose(1, 2, 0, 3)
    gs = o["gdn_s"].reshape(P, NSEQ, GH, P).transpose(1, 2, 0, 3)
    sp_ = o["ssd_p"].reshape(P, 1, SH, 64).transpose(1, 2, 3, 0)
    ss = o["ssd_s"].reshape(P, NSEQ, SH, 64).transpose(1, 2, 3, 0)
    got = [y[:NP_TOK].reshape(1, NP_TOK, D), y[NP_TOK:].reshape(NSEQ, SLEN, D)]
    for a, b, gd, sd in ((0, 1, gp, sp_), (1, 9, gs, ss)):
        got += [s5[0, a:b][None], s5[1, a:b][None], gd[None], ho[a:b, :, 0:1536][None], lru[a:b][None],
                ho[a:b, :, 2560:3072][None], sd[None], ho[a:b, :, 1536:2560][None]]
    return tuple(np.ascontiguousarray(x) for x in got)
```

```python
from contextlib import ExitStack

import numpy as np

import concourse.bass as bass
from concourse import mybir

F32 = mybir.dt.float32
ALU = mybir.AluOpType
ACT = mybir.ActivationFunctionType
AX = mybir.AxisListType

P = 128
D = 1024
KD = D // P
NP_TOK, NSEQ, SLEN = 1024, 8, 16
T = NP_TOK + NSEQ * SLEN
N3 = T // 3
NT = T // P
MIX = D // 2
KM = MIX // P
GH, SH = 4, 8
NE = 16
BLK = 128
NB = -(-(2 * T + NE * (BLK - 1)) // BLK)
EPS = 1e-6
CW = 3 + NP_TOK + NSEQ * (3 + SLEN)
TWO_PI_HI = 6.28125
TWO_PI_LO = float(2 * np.pi - 6.28125)
ROUND = 12582912.0

CST = {}
def _cst(name, n):
    CST[name] = (sum(v[1] for v in CST.values()), n)
_cst("ident", P); _cst("ones", P); _cst("level", 7 * P)
_cst("neg_prompt", P); _cst("neg_sample", P); _cst("last", P); _cst("row", NSEQ); _cst("eps", 1); _cst("tri", 16)
_cst("token", NT); _cst("block", NB); _cst("before", NE)
NCST = sum(v[1] for v in CST.values())

VEC = {}
def _vec(name, n):
    VEC[name] = (sum(v[1] for v in VEC.values()), n)
for _n, _w in (("norm_mix", 8), ("norm_moe", 8), ("norm_final", 8), ("b_ada", 48), ("s5_d", 4), ("gdn_conv", 48),
               ("gdn_norm", 1), ("lru_conv", 16), ("lru_conv_b", 4), ("lru_b_a", 4), ("lru_b_x", 4), ("lru_lambda", 4),
               ("ssd_conv", 32), ("ssd_conv_b", 8), ("ssd_d", 4), ("ssd_norm", 4), ("s5_re", 16), ("s5_im", 16),
               ("s5_dt", 16), ("alog", 1), ("dtb", 1), ("rbias", NE), ("lru_h0", 32), ("s5_x0r", 128), ("s5_x0i", 128)):
    _vec(_n, _w)
NVEC = sum(v[1] for v in VEC.values())

def plan_tiles():
    names = [("ss_mix", 0, 0)]
    names += [("rows", 0, 1)]
    names += [("qkv", m, m % 2) for m in range(12)] + [("zb", m, m % 2) for m in range(KM)]
    names += [("qkn", m, m % 2) for m in range(8)]
    names += [("gdn_ss", m, m % 2) for m in range(4)]
    def merge(k):
        return [x for m in range(KD) for x in (("gate%d" % k, m, 0), ("br%d" % k, m, 1))]
    names += merge(1)
    names += [("xbc", m, m % 2) for m in range(8)] + [("zd", m, m % 2) for m in range(KM)]
    names += [("ssd_ss", 0, 0)]
    names += merge(3)
    names += [("xc", m, m % 2) for m in range(4)] + [("gc", m, m % 2) for m in range(4)]
    names += [x for m in range(4) for x in (("lru_r", m, 0), ("lru_i", m, 1))]
    names += merge(2)
    names += [("ua", m, m % 2) for m in range(4)]
    for i in range(4):
        names += [x for q in range(4) for x in (("bu_re", 4 * i + q, 0), ("bu_im", 4 * i + q, 1))]
    names += [("glu", m, m % 2) for m in range(4)]
    names += merge(0)
    names += [("out", m, m % 2) for m in range(KD)]
    names += [("ss_moe", 0, 0)]
    names += [("ss_final", 0, 0)]
    count, at = [0, 0], {}
    for name, m, s in names:
        at[(name, m)] = (s, count[s])
        count[s] += 1
    return at

FILL = plan_tiles()

def plan_loads():
    loads = [("ada", g, g % 2) for g in range(12)]
    def add(*names):
        for a, g in names:
            loads.append((a, g, (len(loads)) % 2))
    add(("qkv", 0), ("qkv", 1), ("qkv", 2), ("zb", 0), ("gdn_state", 0))
    def merge(k):
        add(("gate%d" % k, 0), ("br%d" % k, 0), ("gate%d" % k, 1))
    merge(1)
    add(("xbc", 0), ("xbc", 1), ("zd", 0), ("ssd_state", 0))
    merge(3)
    add(("xc", 0), ("gc", 0), ("lru_w", 0))
    merge(2)
    add(("ua", 0), ("s5_bc", 0), ("glu", 0))
    merge(0)
    add(("out", 0), ("out", 1))
    return loads

LOADS = plan_loads()
SLOT = {(a, g): s for a, g, s in LOADS}

def slot_count(a, g):
    n = 0
    for x, y, s in LOADS:
        if s == SLOT[(a, g)]:
            n += 1
        if (x, y) == (a, g):
            return n

def last_reader(a, g):
    if a in ("ada", "gdn_state", "ssd_state", "lru_w", "s5_bc"):
        return None
    if a.startswith("br"):
        return (a, KD - 1)
    if a == "glu":
        return (a, 3)
    return (a, 4 * g + 3)


def build(nc, A):
    with ExitStack() as ctx:
        def sb(name, shape):
            return ctx.enter_context(nc.sbuf_tensor(name, shape, F32))

        def sem(name):
            return ctx.enter_context(nc.semaphore(name))

        cst = sb("cst", [P, NCST])
        vec = sb("vec", [P, NVEC])
        mod = sb("mod", [P, 48 * 9])
        amul = sb("amul", [P, 2 * 72])
        cond = sb("cond", [P, 72])
        rows = sb("rows", [P, T])
        hist = sb("hist", [P, 24 * 24])
        hist_out = sb("hist_out", [P, 24 * 27])
        s5c = sb("s5c", [P, 16 * 34])
        s5x = sb("s5x", [P, 2 * 16 * 8])
        s5_out = sb("s5_out", [P, 2 * 16 * 9])
        lru_out = sb("lru_out", [P, 4 * 9])
        lruc = sb("lruc", [P, 32])
        wrows = sb("wrows", [P, KD * 16])
        wrouter = sb("wrouter", [P, KD * 16])
        small = sb("small", [P, 400])
        ARENA = 46080
        arena = sb("arena", [P, ARENA])
        psum = ctx.enter_context(nc.psum_tensor("psum", [P, 8 * 512], F32))

        def cut(start, n):
            assert start + n <= ARENA
            return arena[:, start:start + n]

        W = [cut(0, 4096), cut(4096, 4096)]
        HT = cut(8192, KD * T).rearrange("p (k t) -> p k t", k=KD)
        Y = cut(17408, KM * T).rearrange("p (k t) -> p k t", k=KM)
        R0 = 22016
        MRG0 = 36864
        merged = cut(MRG0, KD * T).rearrange("p (k t) -> p k t", k=KD)
        X = cut(R0, KD * T).rearrange("p (k t) -> p k t", k=KD)

        def bank(b, n=512, w=1):
            return psum[:, 512 * b:512 * b + n]

        def pset(s):
            return psum[:, 1536 * s:1536 * (s + 1)].rearrange("p (b c) -> p b c", b=3)[:, :, 0:N3]

        def tri3(ap):
            return ap.rearrange("p (b c) -> p b c", b=3)

        def c_(name, a=0, n=None):
            o, w = CST[name]
            return cst[:, o + a:o + a + (w if n is None else n)]

        def v_(name, a=0, n=1):
            return vec[:, VEC[name][0] + a:VEC[name][0] + a + n]

        ident, ones = c_("ident"), c_("ones")
        mod3 = mod[:, :].rearrange("p (m s) -> p m s", s=9)
        amul3 = amul[:, :].rearrange("p (w m s) -> p w m s", w=2, s=9)

        def seqs(ap):
            return ap[:, NP_TOK:T].rearrange("p (b t) -> p b t", t=SLEN)

        s_const = sem("s_const"); s_x = sem("s_x"); s_xr = sem("s_xr")
        s_w = [sem("s_w%d" % i) for i in range(2)]
        s_fill = [sem("s_fillA"), sem("s_fillB")]
        s_free = [sem("s_freeA"), sem("s_freeB")]
        s_dve = sem("s_dve"); s_act = sem("s_act")
        s_phase = sem("s_phase")
        s_cond = sem("s_cond"); s_ada = sem("s_ada"); s_mod = sem("s_mod")
        s_sq = sem("s_sq"); s_sq_used = sem("s_sq_used"); s_root = sem("s_root"); s_h = sem("s_h"); s_recip = sem("s_recip")
        s_cb = sem("s_cb"); s_conv = sem("s_conv")
        r_z = sem("r_z"); r_l = sem("r_l"); r_sg = sem("r_sg")
        s_sig = sem("s_sig"); s_acc = sem("s_acc")
        s_out = sem("s_out"); s_pstate = sem("s_pstate")
        c_bc = sem("c_bc"); c_cols = sem("c_cols"); c_diff = sem("c_diff"); c_exp = sem("c_exp")
        c_gram = sem("c_gram"); c_tok = sem("c_tok"); c_ops = sem("c_ops"); c_lk = sem("c_lk"); c_p = sem("c_p")
        c_ps = sem("c_ps"); c_d = sem("c_d"); c_x = sem("c_x"); c_w = sem("c_w"); c_nw = sem("c_nw"); c_u = sem("c_u")
        c_us = sem("c_us"); c_o = sem("c_o"); c_os = sem("c_os"); c_ut = sem("c_ut"); c_um = sem("c_um")
        c_s = sem("c_s"); c_ss = sem("c_ss")
        d_bc = sem("d_bc"); d_diff = sem("d_diff"); d_exp = sem("d_exp"); d_ops = sem("d_ops"); d_y = sem("d_y")
        d_ys = sem("d_ys"); d_bm = sem("d_bm"); d_s = sem("d_s"); d_ss = sem("d_ss"); d_gated = sem("d_gated")
        l_sp = sem("l_sp"); l_col = sem("l_col"); l_a = sem("l_a"); l_m = sem("l_m"); l_b = sem("l_b"); l_done = sem("l_done")
        a_mag = sem("a_mag"); a_th = sem("a_th"); a_sin = sem("a_sin"); a_bs = sem("a_bs"); a_bt = sem("a_bt")
        a_btc = sem("a_btc"); a_u = sem("a_u"); a_x = sem("a_x"); a_y = sem("a_y"); a_ys = sem("a_ys")
        a_yd = sem("a_yd"); a_g = sem("a_g"); a_gs = sem("a_gs")
        m_r = sem("m_r"); m_sc = sem("m_sc"); m_mask = sem("m_mask"); m_maskt = sem("m_maskt"); m_nblk = sem("m_nblk")
        m_start = sem("m_start"); m_pos = sem("m_pos"); m_post = sem("m_post"); m_posi = sem("m_posi"); m_tab = sem("m_tab")
        m_ht = sem("m_ht"); m_htok = sem("m_htok"); m_hst = [sem("m_hst%d" % i) for i in range(2)]; m_zero = sem("m_zero"); m_idz = sem("m_idz")
        m_scat = sem("m_scat"); m_idl = sem("m_idl"); m_idt = sem("m_idt"); m_idx = sem("m_idx")
        e_w = [sem("e_w%d" % i) for i in range(2)]; e_x = [sem("e_x%d" % i) for i in range(2)]
        e_xt = sem("e_xt"); e_xc = sem("e_xc"); e_g = sem("e_g"); e_u = sem("e_u"); e_sg = sem("e_sg"); e_hid = sem("e_hid")
        e_ht = sem("e_ht"); e_htc = sem("e_htc"); e_d = sem("e_d"); e_ya = sem("e_ya"); e_yd = sem("e_yd")
        e_st = [sem("e_st%d" % i) for i in range(2)]
        f_y = [sem("f_y%d" % i) for i in range(2)]; f_f = sem("f_f"); f_t = sem("f_t"); f_x = sem("f_x")

        class Steps:
            def __init__(self, eng, own):
                self.eng, self.own, self.n = eng, own, {}

            def tell(self, ins, s):
                ins.then_inc(s, 1)
                self.n[s.name] = self.n.get(s.name, 0) + 1

            def then(self, ins, s=None):
                s = self.own if s is None else s
                self.tell(ins, s)
                self.eng.wait_ge(s, self.n[s.name])

        def end_phase(eng, n):
            eng.drain().then_inc(s_phase, 1)
            eng.wait_ge(s_phase, 3 * (n + 1))

        def wait_fill(eng, name, m):
            s, k = FILL[(name, m)]
            eng.wait_ge(s_fill[s], k + 1)
            return s

        def freed(eng, name, m):
            s, k = FILL[(name, m)]
            eng.wait_ge(s_free[s], k + 1)

        def wait_load(eng, a, g):
            s = SLOT[(a, g)]
            eng.wait_ge(s_w[s], 16 * slot_count(a, g))
            return W[s]

        block = ctx.enter_context(nc.Block())

        tmp0 = 35840
        QKV = cut(R0, 12 * T).rearrange("p (m t) -> p m t", m=12)
        cb_g = [cut(tmp0, CW), cut(tmp0 + CW + 1, CW)]
        sq_a = [cut(tmp0, T), cut(tmp0 + T, T)]
        rs_a, rt_a = cut(tmp0 + 2 * T, T), cut(tmp0 + 3 * T, T)
        rowt = [cut(tmp0 + (4 + i) * T, T) for i in range(4)]
        (cDT, cEG, cLT, cAT, cQE, cKE, cKB, cVB, cLK, cPS, cX, cXT, cU, cS, cNW) = [
            cut(tmp0 + 512 * i, 512) for i in range(15)]
        cUM = cut(tmp0 + 512 * 15, 1024)
        Rb = R0 + 8 * T
        XBC = cut(R0, 8 * T).rearrange("p (m t) -> p m t", m=8)
        cb_s = [cut(Rb, CW), cut(Rb + CW + 1, CW)]
        sq_s = [cut(Rb, T), cut(Rb + T, T)]
        rs_s, rt_s = cut(Rb + 2 * T, T), cut(Rb + 3 * T, T)
        dDT, dEG = cut(Rb, 1024), cut(Rb + 1024, 1024)
        dXD, dXW = cut(Rb + 2048, 512), cut(Rb + 2560, 512)
        dB, dBM, dH, dTMP = cut(Rb + 3072, 256), cut(Rb + 3328, 256), cut(Rb + 3584, 512), cut(Rb + 4096, 512)
        Rl = R0 + 4 * T
        XF = cut(R0, 4 * T).rearrange("p (m t) -> p m t", m=4)
        cb_l = [cut(Rl, CW), cut(Rl + CW + 1, CW)]
        lt = [cut(Rl + 2400 + i * T, T) for i in range(6)]
        U = XF
        sCOS, sSIN = cut(Rl, T), cut(Rl + T, T)
        st = [cut(Rl + (2 + i) * T, T) for i in range(6)]
        sBT = cut(Rl + 8 * T, 1024)
        sMASK = rows[:, :]
        E0 = 35328
        sq_e = [cut(E0, T), cut(E0 + T, T)]
        rs_e, rt_e = cut(E0 + 2 * T, T), cut(E0 + 3 * T, T)
        res_tmp = cut(31232, P)
        G0 = E0 + 4 * T + P
        scores, rsel, rank, picked, weight, first1, rtmp = [cut(G0 + 144 * i, 144) for i in range(7)]
        grp = cut(G0 + 144 * 7, 36 * 4)
        btab = cut(G0 + 144 * 8, NB * NB)
        cmpA, cmpB = cut(31232, 576), cut(31232 + 576, 576)
        ones_row, mask_row, cum_row = cut(E0, T), cut(E0 + 2 * T, T), cut(E0 + 3 * T, T)
        htok = [cut(17408, D), cut(18432, D)]
        INT = mybir.dt.int32
        w12 = hist[:, 0:18].rearrange("p (k c) -> p k c", k=2)
        posf, posi = hist[:, 20:38], hist[:, 40:58].bitcast(INT)
        idxi = hist[:, 60:60 + NB].bitcast(INT)
        ecol = hist[0:16, 100:110]
        erow = hist[0:1, 120:120 + 8 * NB].rearrange("p (a j) -> p a j", j=NB)
        eint_at = hist[0:1, 540:540 + NB].bitcast(INT).rearrange("p (a j) -> p a j", j=NB)
        eint = hist[0:1, 400:400 + 4 * NB].bitcast(INT).rearrange("p (a j) -> p a j", j=NB)
        islot = cut(G0 + 144 * 8 + NB * NB, BLK)
        WSET = 31232
        wset = cut(0, 12288)
        xg = [cut(12288, D), cut(13312, D)]
        xT = [cut(14336, D), cut(15360, D)]
        esg, ehid, ehT = cut(16384, 512), cut(16896, 512), cut(17408, 512)
        yb = [cut(17920, D), cut(18944, D)]
        yg = [[cut(12288 + 1024 * (2 * i + k), D) for k in range(2)] for i in range(2)]
        ff = [cut(16384, D), cut(17408, D)]
        ftmp = cut(18432, D)
        h_rows = A["h_rows"]
        y_rows = A["y_rows"]
        slot_token = A["slot_token"]
        mg_sig = [cut(R0, T), cut(R0 + T, T)]
        mg_tmp = cut(R0 + 2 * T, T)

        colG, colE, colB = small[:, 0:80], small[:, 96:112], small[:, 112:116]
        colK, colW, colL = small[:, 116:124], small[:, 124:132], small[:, 132:196]
        nexpa = small[0:16, 200:201]

        S5N = ["dt", "mag", "th", "sin", "cos", "den", "fre", "fim", "t0", "t1", "lre", "lim", "c1", "s1"]

        def s5(name, k=0):
            i = (S5N.index(name) if name in S5N else len(S5N) + 2 * k + (name == "pi")) * 16
            return s5c[:, i:i + 16]

        def hd(ap, h):
            return ap.rearrange("p (h t) -> p h t", h=h)

        def over(ap, n):
            return ap.unsqueeze(2).to_broadcast([ap.shape[0], ap.shape[1], n])

        def by(ap, n):
            return ap.unsqueeze(1).to_broadcast([ap.shape[0], n, ap.shape[1]])

        sq_no, sq_reader, root_no = {}, {}, {}
        n_sq = used = 0
        for name, m, terms in ([("ss_mix", 0, KD)] + [("qkn", m, 1) for m in range(8)] +
                               [("gdn_ss", m, 1) for m in range(4)] + [("ssd_ss", 0, KM)] +
                               [("ss_moe", 0, KD), ("ss_final", 0, KD)]):
            root_no[(name, m)] = len(root_no)
            sq_no[(name, m)] = list(range(n_sq, n_sq + terms))
            for i in range(terms):
                if i < terms - 1:
                    used += 1
                    sq_reader[n_sq + i] = (s_sq_used, used)
                else:
                    fs, fk = FILL[(name, m)]
                    sq_reader[n_sq + i] = (s_fill[fs], fk + 1)
            n_sq += terms

        def pe_tile(pe, name, m, w, src, K):
            s, k = FILL[(name, m)]
            if k >= 1:
                pe.wait_ge(s_free[s], k)
            for n in range(3):
                for kk in range(K):
                    last = nc.tensor.matmul(pset(s)[:, n, :], w[:, kk, :], src[:, kk, n * N3:(n + 1) * N3],
                                            start=(kk == 0), stop=(kk == K - 1))
            last.then_inc(s_fill[s], 1)

        def pe_group(pe, name, g, src, K, per):
            w = wait_load(pe, name, g).rearrange("p (m k c) -> p m k c", m=4096 // (K * P), k=K)
            for m in range(per):
                pe_tile(pe, name, per * g + m, w[:, m], src, K)

        def pe_sumsq(pe, name, m, sq):
            s, k = FILL[(name, m)]
            if k >= 1:
                pe.wait_ge(s_free[s], k)
            terms = sq_no[(name, m)]
            for i, q in enumerate(terms):
                pe.wait_ge(s_sq, q + 1)
                for n in range(3):
                    last = nc.tensor.matmul(pset(s)[:, n, :], ones, sq[q % 2][:, n * N3:(n + 1) * N3],
                                            start=(i == 0), stop=(i == len(terms) - 1))
                last.then_inc(s_sq_used if i < len(terms) - 1 else s_fill[s], 1)

        def act_sumsq(act, name, m, sq, srcs):
            for q, src in zip(sq_no[(name, m)], srcs):
                if q >= 2:
                    act.wait_ge(*sq_reader[q - 2])
                nc.scalar.activation(sq[q % 2], src, ACT.Square).then_inc(s_sq, 1)

        def act_root(St, name, m, dst, scale):
            s = wait_fill(St.eng, name, m)
            if root_no[(name, m)] >= 1:
                St.eng.wait_ge(s_recip, root_no[(name, m)])
            nc.scalar.activation(tri3(dst), pset(s), ACT.Sqrt, bias=c_("eps"), scale=scale).then_inc(s_free[s], 1)

        def dve_recip(V, name, m, rs, rt):
            freed(V.eng, name, m)
            V.then(nc.vector.reciprocal(rs, rt), s_recip)

        def dve_norm(V, x, h, aw, sh):
            for k in range(KD):
                V.then(nc.vector.tensor_tensor(h[:, k, :], x[:, k, :], V.rs, ALU.mult))
                nc.vector.tensor_scalar(h[:, k, 0:NP_TOK], h[:, k, 0:NP_TOK], aw[:, k, 0:1], sh[:, k, 0:1],
                                        ALU.mult, ALU.add)
                hs = seqs(h[:, k, :])
                V.then(nc.vector.tensor_tensor(hs, hs, over(aw[:, k, 1:9], SLEN), ALU.mult))
                V.then(nc.vector.tensor_tensor(hs, hs, over(sh[:, k, 1:9], SLEN), ALU.add),
                       s_h if k == KD - 1 else None)

        def cb_seq(c):
            return c[:, 3 + NP_TOK:CW].rearrange("p (b t) -> p b t", t=3 + SLEN)

        def act_conv_in(St, name, m, n, c):
            s = wait_fill(St.eng, name, m)
            if n >= 2:
                St.eng.wait_ge(s_conv, n - 1)
            ps, d = pset(s), c[n % 2]
            nc.scalar.activation(cb_seq(d)[:, :, 0:3], hist[:, 24 * n:24 * (n + 1)].rearrange("p (b t) -> p b t", t=3),
                                 ACT.Copy)
            nc.scalar.activation(d[:, 3:3 + 2 * N3].rearrange("p (b t) -> p b t", b=2), ps[:, 0:2, :], ACT.Copy)
            nc.scalar.activation(d[:, 3 + 2 * N3:3 + NP_TOK], ps[:, 2, 0:NP_TOK - 2 * N3], ACT.Copy)
            St.then(nc.scalar.activation(cb_seq(d)[:, :, 3:3 + SLEN],
                                         ps[:, 2, NP_TOK - 2 * N3:N3].rearrange("p (b t) -> p b t", t=SLEN), ACT.Copy),
                    s_cb)
            St.eng.sem_inc(s_free[s], 1)

        def dve_cb_start(V, c):
            nc.vector.memset(c[0][:, 0:3], 0.0)
            V.then(nc.vector.memset(c[1][:, 0:3], 0.0))

        def dve_conv(V, n, c, dst, wname, wt, ntile, bias=None):
            V.eng.wait_ge(s_cb, n + 1)
            d = c[n % 2]
            ho = hist_out[:, 27 * n:27 * (n + 1)].rearrange("p (b t) -> p b t", t=3)
            nc.vector.tensor_copy(ho[:, 0, :], d[:, NP_TOK:NP_TOK + 3])
            nc.vector.tensor_copy(ho[:, 1:9, :], cb_seq(d)[:, :, SLEN:SLEN + 3])
            ds = seqs(dst)
            for k in range(4):
                a, b, w = d[:, k:k + NP_TOK], cb_seq(d)[:, :, k:k + SLEN], v_(wname, k * ntile + wt)
                if k == 0 and bias is None:
                    nc.vector.tensor_scalar(dst[:, 0:NP_TOK], a, w, None, ALU.mult)
                    V.then(nc.vector.tensor_scalar(ds, b, w, None, ALU.mult))
                elif k == 0:
                    nc.vector.tensor_scalar(dst[:, 0:NP_TOK], a, w, bias, ALU.mult, ALU.add)
                    V.then(nc.vector.tensor_scalar(ds, b, w, bias, ALU.mult, ALU.add))
                else:
                    nc.vector.scalar_tensor_tensor(out=dst[:, 0:NP_TOK], in0=a, scalar=w, in1=dst[:, 0:NP_TOK],
                                                   op0=ALU.mult, op1=ALU.add)
                    V.then(nc.vector.scalar_tensor_tensor(out=ds, in0=b, scalar=w, in1=ds, op0=ALU.mult, op1=ALU.add),
                           s_conv if k == 3 else None)

        MERGES = [1, 3, 2, 0]

        def pe_merge(pe, k):
            g = "gate%d" % k
            for m in range(KD):
                if m % 4 == 0:
                    wg = wait_load(pe, g, m // 4).rearrange("p (m k c) -> p m k c", m=4, k=KD)
                pe_tile(pe, g, m, wg[:, m % 4], HT, KD)
                if m == 0:
                    wb = wait_load(pe, "br%d" % k, 0).rearrange("p (m k c) -> p m k c", m=8, k=KM)
                pe_tile(pe, "br%d" % k, m, wb[:, m], Y, KM)

        def act_merge(act, k):
            at = MERGES.index(k) * KD
            for m in range(KD):
                s = wait_fill(act, "gate%d" % k, m)
                if at + m >= 2:
                    act.wait_ge(s_acc, at + m - 1)
                nc.scalar.activation(tri3(mg_sig[m % 2]), pset(s), ACT.Sigmoid).then_inc(s_free[s], 1)

        def dve_merge(V, k):
            for m in range(KD):
                freed(V.eng, "gate%d" % k, m)
                s = wait_fill(V.eng, "br%d" % k, m)
                dst = merged[:, m, :] if k == MERGES[0] else mg_tmp
                nc.vector.tensor_tensor(tri3(dst), tri3(mg_sig[m % 2]), pset(s), ALU.mult).then_inc(s_free[s], 1)
                freed(V.eng, "br%d" % k, m)
                if k == MERGES[0]:
                    V.eng.sem_inc(s_acc, 1)
                    V.n[s_acc.name] = V.n.get(s_acc.name, 0) + 1
                else:
                    V.then(nc.vector.tensor_tensor(merged[:, m, :], merged[:, m, :], mg_tmp, ALU.add), s_acc)

        def dve_residual(V, name, m, gate, tmp):
            s = wait_fill(V.eng, name, m)
            ps, x = pset(s), X[:, m, :]
            g = mod3[:, gate + m, :]
            xa = x[:, 0:2 * N3].rearrange("p (b t) -> p b t", b=2)
            nc.vector.scalar_tensor_tensor(out=xa, in0=ps[:, 0:2, :], scalar=g[:, 0:1], in1=xa, op0=ALU.mult, op1=ALU.add)
            xb = x[:, 2 * N3:NP_TOK]
            nc.vector.scalar_tensor_tensor(out=xb, in0=ps[:, 2, 0:NP_TOK - 2 * N3], scalar=g[:, 0:1], in1=xb,
                                           op0=ALU.mult, op1=ALU.add)
            t = tmp[:, 0:P].rearrange("p (b t) -> p b t", t=SLEN)
            nc.vector.tensor_tensor(t, ps[:, 2, NP_TOK - 2 * N3:N3].rearrange("p (b t) -> p b t", t=SLEN),
                                    over(g[:, 1:9], SLEN), ALU.mult).then_inc(s_free[s], 1)
            freed(V.eng, name, m)
            V.then(nc.vector.tensor_tensor(seqs(x), seqs(x), t, ALU.add))

        LEV = [7] * 8 + [4]
        LEV0 = [7 * c for c in range(9)]
        NC7 = NT - 1

        def store_block(sp, j):
            sp.wait_ge(e_ya, j + 1)
            sp.wait_ge(e_yd, j + 1)
            sp.dma_start(y_rows[j * BLK:(j + 1) * BLK, :], yb[j % 2]).then_inc(e_st[j % 2], 16)

        @block.sync
        def _(sp):
            for dst, name in ((cst, "cst"), (vec, "vec"), (cond, "cT"), (hist, "hist"), (wrows, "wrows"), (wrouter, "wrouter")):
                sp.dma_start(dst[:, :], A[name]).then_inc(s_const, 16)
            sp.dma_start(X, A["xT"]).then_inc(s_x, 16)
            before = {}
            for a, g, s in LOADS:
                if s in before:
                    pa, pg = before[s]
                    if pa == "ada":
                        sp.wait_ge(s_ada, pg + 1)
                    elif pa == "gdn_state":
                        sp.wait_ge(c_ss, NC7)
                        sp.dma_start(A["gdn_p"], cS).then_inc(s_pstate, 16)
                        sp.wait_ge(c_ss, NC7 + GH)
                        sp.dma_start(A["gdn_s"], W[s]).then_inc(s_pstate, 16)
                        sp.wait_ge(s_pstate, 32)
                    elif pa == "ssd_state":
                        sp.wait_ge(d_ss, NC7)
                        sp.dma_start(A["ssd_p"], dH).then_inc(s_pstate, 16)
                        sp.wait_ge(d_ss, NC7 + NSEQ)
                        sp.dma_start(A["ssd_s"], W[s]).then_inc(s_pstate, 16)
                        sp.wait_ge(s_pstate, 64)
                    elif pa == "lru_w":
                        sp.wait_ge(s_phase, 3 * 11)
                    elif pa == "s5_bc":
                        sp.wait_ge(s_phase, 3 * 13)
                    else:
                        f, k = FILL[last_reader(pa, pg)]
                        sp.wait_ge(s_fill[f], k + 1)
                sp.dma_start(W[s], A[a][g]).then_inc(s_w[s], 16)
                before[s] = (a, g)
                if a == "out" and g == 1:
                    sp.wait_ge(s_phase, 3 * 14)
                    sp.dma_start(X, A["xT"]).then_inc(s_xr, 16)
            sp.wait_ge(m_zero, 1)
            sp.dma_start(slot_token.rearrange("(p j) o -> p (j o)", p=P), cmpB[:, 0:NB]).then_inc(m_idz, 16)
            for c in range(NT):
                sp.wait_ge(m_htok, c + 1)
                sp.dma_start(h_rows[c * P:(c + 1) * P, :], htok[c % 2]).then_inc(m_hst[c % 2], 16)
            sp.wait_ge(m_scat, 16 * 18)
            sp.dma_start(islot[0:NB, :], slot_token.rearrange("(j p) o -> j (p o)", p=BLK)).then_inc(m_idl, 16)
            sp.wait_ge(s_phase, 3 * 16)
            e0 = sp.value_load(eint[:, 0, 0:1], min_val=0, max_val=NE - 1)
            sp.dma_start(wset, A["moe"][bass.ds(e0, 1)].rearrange("a p c -> (a p) c")).then_inc(e_w[1], 16)
            for j in range(NB - 1):
                nxt = sp.value_load(eint[:, 1, j:j + 1], min_val=0, max_val=NE - 1)
                new = sp.value_load(eint[:, 2, j:j + 1], min_val=0, max_val=1)
                other = sp.value_load(eint[:, 3, j:j + 1], min_val=0, max_val=WSET)
                if j:
                    sp.wait_ge(e_d, j)
                sp.dma_start(arena[:, bass.ds(other, 12288)], A["moe"][bass.ds(nxt, 1)].rearrange("a p c -> (a p) c"),
                             cond=(new > 0)).then_inc(e_w[j % 2], 16)
                if j:
                    store_block(sp, j - 1)
            store_block(sp, NB - 2)
            store_block(sp, NB - 1)
            sp.wait_ge(s_phase, 3 * 19)
            sp.dma_start(A["yT"], HT).then_inc(s_out, 16)
            for name, t in (("hist_out", hist_out), ("s5_out", s5_out), ("lru_out", lru_out)):
                sp.dma_start(A[name], t[:, :]).then_inc(s_out, 16)
            sp.wait_ge(s_out, 16 * 4)

        @block.tensor
        def _(pe):
            pe.wait_ge(s_const, 16 * 6)
            pe.wait_ge(s_cond, 1)
            for g in range(12):
                w = wait_load(pe, "ada", g).rearrange("p (m k c) -> p m k c", m=4, k=KD)
                for m in range(4 * g, 4 * g + 4):
                    for k in range(KD):
                        last = nc.tensor.matmul(bank(6)[:, 9 * m:9 * m + 9], w[:, m % 4, k, :], cond[:, 9 * k:9 * k + 9],
                                                start=(k == 0), stop=(k == KD - 1))
                last.then_inc(s_ada, 1)
            pe_sumsq(pe, "ss_mix", 0, sq_a)
            pe.wait_ge(s_h, 1)
            s, k = FILL[("rows", 0)]
            pe.wait_ge(s_free[s], k) if k else None
            wr = wrows[:, :].rearrange("p (k c) -> p k c", k=KD)
            for n in range(3):
                for kk in range(KD):
                    last = nc.tensor.matmul(pset(s)[0:16, n, :], wr[:, kk, :], HT[:, kk, n * N3:(n + 1) * N3],
                                            start=(kk == 0), stop=(kk == KD - 1))
            last.then_inc(s_fill[s], 1)
            end_phase(pe, 0)
            for g in range(3):
                pe_group(pe, "qkv", g, HT, KD, 4)
            pe_group(pe, "zb", 0, HT, KD, 4)
            end_phase(pe, 1)
            for m in range(8):
                pe_sumsq(pe, "qkn", m, sq_a)
            end_phase(pe, 2)

            def sel(r):
                return ident[0:80, r:r + 1].to_broadcast([80, P])

            for c in range(NT):
                t0 = c * P
                sample = c == NC7
                ck = lambda m: QKV[:, m, t0:t0 + P]
                hs = [slice(h * P, (h + 1) * P) for h in range(GH)]
                if c:
                    pe.wait_ge(c_ss, c)
                    pe.wait_ge(c_os, c)
                for h in range(GH):
                    nc.tensor.matmul(bank(0)[:, hs[h]], sel(h), rows[0:80, t0:t0 + P], start=True, stop=True)
                for h in range(GH):
                    nc.tensor.matmul(bank(1)[:, hs[h]], sel(76 + h), rows[0:80, t0:t0 + P], start=True, stop=True)
                nc.tensor.transpose(bank(2)[:, 0:80], rows[0:80, t0:t0 + P], ident[0:80, 0:80]).then_inc(c_bc, 1)
                for h in range(GH):
                    nc.tensor.matmul(bank(3)[:, hs[h]], ck(4 + h), ck(4 + h), start=True, stop=True)
                for h in range(GH):
                    last = nc.tensor.matmul(bank(4)[:, hs[h]], ck(4 + h), ck(h), start=True, stop=True)
                last.then_inc(c_gram, 1)
                for h in range(GH):
                    nc.tensor.transpose(bank(5)[:, hs[h]], ck(4 + h), ident)
                for h in range(GH):
                    last = nc.tensor.transpose(bank(6)[:, hs[h]], ck(8 + h), ident)
                last.then_inc(c_tok, 1)
                pe.wait_ge(c_ops, c + 1)
                for n in range(LEV0[c], LEV0[c] + LEV[c]):
                    pe.wait_ge(c_lk, n + 1)
                    for a in hs:
                        last = nc.tensor.matmul(bank(0)[:, a], cLK[:, a], cX[:, a], start=True, stop=True)
                    last.then_inc(c_p, 1)
                    pe.wait_ge(c_ps, n + 1)
                    for a in hs:
                        nc.tensor.matmul(bank(1)[:, a], cXT[:, a], cPS[:, a], start=True, stop=True)
                    for a in hs:
                        last = nc.tensor.matmul(bank(2)[:, a], cPS[:, a], cXT[:, a], start=True, stop=True)
                    last.then_inc(c_d, 1)
                pe.wait_ge(c_x, LEV0[c] + LEV[c])
                for a in hs:
                    last = nc.tensor.matmul(bank(3)[:, a], cKB[:, a], cXT[:, a], start=True, stop=True)
                last.then_inc(c_w, 1)
                pe.wait_ge(c_nw, c + 1)
                if not sample:
                    for a in hs:
                        nc.tensor.matmul(bank(4)[:, a], cXT[:, a], cVB[:, a], start=True, stop=False)
                        last = nc.tensor.matmul(bank(4)[:, a], cNW[:, a], cS[:, a], start=False, stop=True)
                    last.then_inc(c_u, 1)
                    pe.wait_ge(c_us, c + 1)
                    for a in hs:
                        nc.tensor.matmul(bank(5)[:, a], cS[:, a], cQE[:, a], start=True, stop=False)
                        last = nc.tensor.matmul(bank(5)[:, a], cU[:, a], cAT[:, a], start=False, stop=True)
                    last.then_inc(c_o, 1)
                    for a in hs:
                        last = nc.tensor.matmul(bank(6)[:, a], cKE[:, a], cU[:, a], start=True, stop=True)
                    last.then_inc(c_s, 1)
                else:
                    S0 = wait_load(pe, "gdn_state", 0).rearrange("p (b h v) -> p b h v", b=NSEQ, h=GH)
                    for h in range(GH):
                        nc.tensor.matmul(bank(4)[:, hs[h]], cVB[:, hs[h]], cXT[:, hs[h]], start=True, stop=False)
                        for b in range(NSEQ):
                            a = slice(h * P + SLEN * b, h * P + SLEN * (b + 1))
                            last = nc.tensor.matmul(bank(4)[:, a], S0[:, b, h, :], cNW[:, a],
                                                    start=False, stop=(b == NSEQ - 1))
                    last.then_inc(c_u, 1)
                    pe.wait_ge(c_ut, 1)
                    for a in hs:
                        last = nc.tensor.transpose(bank(7)[:, a], cPS[:, a], ident)
                    last.then_inc(c_u, 1)
                    pe.wait_ge(c_us, c + 1)
                    for h in range(GH):
                        nc.tensor.matmul(bank(5)[:, hs[h]], cU[:, hs[h]], cAT[:, hs[h]], start=True, stop=False)
                        for b in range(NSEQ):
                            a = slice(h * P + SLEN * b, h * P + SLEN * (b + 1))
                            last = nc.tensor.matmul(bank(5)[:, a], S0[:, b, h, :], cQE[:, a],
                                                    start=False, stop=(b == NSEQ - 1))
                    last.then_inc(c_o, 1)
                    for h in range(GH):
                        pe.wait_ge(c_um, h + 1)
                        for j in range(2):
                            last = nc.tensor.matmul(bank(j), cKE[:, hs[h]], cUM[:, 512 * j:512 * (j + 1)],
                                                    start=True, stop=True)
                        last.then_inc(c_s, 1)
            end_phase(pe, 3)
            for m in range(GH):
                pe_sumsq(pe, "gdn_ss", m, sq_a)
            end_phase(pe, 4)
            pe_merge(pe, 1)
            end_phase(pe, 5)
            for g in range(2):
                pe_group(pe, "xbc", g, HT, KD, 4)
            pe_group(pe, "zd", 0, HT, KD, 4)
            end_phase(pe, 6)
            for c in range(NT):
                t0 = c * P
                sample = c == NC7
                xk = lambda m: XBC[:, m, t0:t0 + P]
                if c:
                    pe.wait_ge(d_ss, c)
                    pe.wait_ge(d_ys, c)
                for h in range(SH):
                    nc.tensor.matmul(bank(h // 4)[:, (h % 4) * P:(h % 4 + 1) * P], sel(4 + h), rows[0:80, t0:t0 + P],
                                     start=True, stop=True)
                nc.tensor.transpose(bank(2)[:, 0:80], rows[0:80, t0:t0 + P], ident[0:80, 0:80])
                for g in range(2):
                    nc.tensor.matmul(bank(3)[:, g * P:(g + 1) * P], xk(4 + g), xk(6 + g), start=True, stop=True)
                for g in range(2):
                    nc.tensor.transpose(bank(4)[:, g * P:(g + 1) * P], xk(4 + g), ident)
                for m in range(KM):
                    last = nc.tensor.transpose(bank(5)[:, m * P:(m + 1) * P], xk(m), ident)
                last.then_inc(d_bc, 1)
                pe.wait_ge(d_ops, c + 1)
                if sample:
                    H0 = wait_load(pe, "ssd_state", 0).rearrange("p (b h d) -> p b h d", b=NSEQ, h=SH)
                for h in range(SH):
                    q0, o0 = 64 * (h % 2), 6 * 512 + (h // 2) * P
                    y = psum[q0:q0 + 64, o0:o0 + P]
                    nc.tensor.matmul(y, dXD[:, 64 * h:64 * h + 64], dDT[:, h * P:(h + 1) * P], start=True, stop=False)
                    if not sample:
                        last = nc.tensor.matmul(y, dH[:, 64 * h:64 * h + 64], dEG[:, h * P:(h + 1) * P],
                                                start=False, stop=True)
                    else:
                        for b in range(NSEQ):
                            last = nc.tensor.matmul(psum[q0:q0 + 64, o0 + SLEN * b:o0 + SLEN * (b + 1)], H0[:, b, h, :],
                                                    dEG[:, h * P + SLEN * b:h * P + SLEN * (b + 1)],
                                                    start=False, stop=(b == NSEQ - 1))
                last.then_inc(d_y, 1)
                for b in range(NSEQ if sample else 1):
                    if sample:
                        pe.wait_ge(d_bm, b + 1)
                    bt = dBM if sample else dB
                    for g in range(2):
                        last = nc.tensor.matmul(bank(7)[:, 256 * g:256 * (g + 1)], bt[:, g * P:(g + 1) * P],
                                                dXW[:, 256 * g:256 * (g + 1)], start=True, stop=True)
                    last.then_inc(d_s, 1)
            end_phase(pe, 7)
            pe_sumsq(pe, "ssd_ss", 0, sq_s)
            end_phase(pe, 8)
            pe_merge(pe, 3)
            end_phase(pe, 9)
            pe_group(pe, "xc", 0, HT, KD, 4)
            pe_group(pe, "gc", 0, HT, KD, 4)
            wl = wait_load(pe, "lru_w", 0)[:, 0:1024].rearrange("p (w m c) -> p w m c", w=2, m=4)
            for m in range(4):
                pe.wait_ge(s_conv, 20 + m + 1)
                for w, name in ((0, "lru_r"), (1, "lru_i")):
                    s, k = FILL[(name, m)]
                    pe.wait_ge(s_free[s], k)
                    for n in range(3):
                        last = nc.tensor.matmul(pset(s)[:, n, :], wl[:, w, m, :], XF[:, m, n * N3:(n + 1) * N3],
                                                start=True, stop=True)
                    last.then_inc(s_fill[s], 1)
            end_phase(pe, 10)
            pe_merge(pe, 2)
            end_phase(pe, 11)
            pe_group(pe, "ua", 0, HT, KD, 4)
            bc = wait_load(pe, "s5_bc", 0)
            pe.wait_ge(a_bs, 1)
            for w in range(2):
                for i in range(4):
                    last = nc.tensor.transpose(bank(6 + w)[:, i * P:(i + 1) * P],
                                               bc[:, 512 * w + P * i:512 * w + P * (i + 1)], ident)
            last.then_inc(a_bt, 1)
            pe.wait_ge(a_btc, 1)
            pe.wait_ge(a_u, 4)
            cc = bc[:, 1024:2048].rearrange("p (w j c) -> p w j c", w=2, c=32)
            for j in range(16):
                i, q = divmod(j, 4)
                for w, name in ((0, "bu_re"), (1, "bu_im")):
                    s, k = FILL[(name, j)]
                    pe.wait_ge(s_free[s], k)
                    for n in range(3):
                        last = nc.tensor.matmul(pset(s)[:, n, :],
                                                sBT[32 * q:32 * q + 32, 512 * w + P * i:512 * w + P * i + P],
                                                U[32 * q:32 * q + 32, i, n * N3:(n + 1) * N3], start=True, stop=True)
                    last.then_inc(s_fill[s], 1)
                pe.wait_ge(a_x, j + 1)
                for n in range(3):
                    b = 3 * j + n
                    if b >= 2:
                        pe.wait_ge(a_ys, b - 1)
                    dst = psum[32 * q:32 * q + 32, 512 * (6 + b % 2):512 * (6 + b % 2) + N3]
                    nc.tensor.matmul(dst, cc[:, 0, j, :], st[2][:, n * N3:(n + 1) * N3], start=True, stop=False)
                    nc.tensor.matmul(dst, cc[:, 1, j, :], st[3][:, n * N3:(n + 1) * N3],
                                     start=False, stop=True).then_inc(a_y, 1)
            wg = wait_load(pe, "glu", 0).rearrange("p (m k c) -> p m k c", m=8, k=KM)
            pe.wait_ge(a_g, 4)
            for m in range(4):
                pe_tile(pe, "glu", m, wg[:, m], U, KM)
            end_phase(pe, 12)
            pe_merge(pe, 0)
            end_phase(pe, 13)
            pe_group(pe, "out", 0, merged, KD, 4)
            pe_group(pe, "out", 1, merged, KD, 4)
            end_phase(pe, 14)
            pe_sumsq(pe, "ss_moe", 0, sq_e)
            pe.wait_ge(s_h, 2)
            wr = wrouter[:, :].rearrange("p (k c) -> p k c", k=KD)
            for c in range(NT):
                for k in range(KD):
                    last = nc.tensor.matmul(bank(7)[:, 16 * c:16 * c + 16], HT[:, k, c * P:(c + 1) * P], wr[:, k, :],
                                            start=(k == 0), stop=(k == KD - 1))
            last.then_inc(m_r, 1)
            for c in range(NT):
                if c >= 2:
                    pe.wait_ge(m_htok, c - 1)
                for k in range(KD):
                    last = nc.tensor.transpose(bank(2 * (c % 2) + k // 4)[:, P * (k % 4):P * (k % 4 + 1)],
                                               HT[:, k, c * P:(c + 1) * P], ident)
                last.then_inc(m_ht, 1)
            pe.wait_ge(m_mask, 1)
            for c in range(NT):
                last = nc.tensor.transpose(psum[0:16, 2048 + P * c:2048 + P * (c + 1)], picked[:, 16 * c:16 * c + 16], ident)
            last.then_inc(m_maskt, 1)
            pe.wait_ge(m_nblk, 1)
            nc.tensor.matmul(bank(7)[0:16, 200:201], c_("before")[0:16], ecol[:, 1:2], start=True, stop=True).then_inc(m_start, 1)
            pe.wait_ge(m_pos, 1)
            for c in range(NT):
                nc.tensor.transpose(bank(7)[:, 16 * c:16 * c + 16], cum_row[0:16, c * P:(c + 1) * P], ident[0:16, 0:16])
            nc.tensor.matmul(bank(7)[0:1, 256:256 + NB], ones[0:16, 0:1], cmpB[0:16, 0:NB],
                             start=True, stop=True).then_inc(m_post, 1)
            pe.wait_ge(m_idl, 16)
            nc.tensor.transpose(bank(4)[:, 0:NB], islot[0:NB, :], ident[0:NB, 0:NB]).then_inc(m_idt, 1)
            end_phase(pe, 15)
            def turn_block(j):
                pe.wait_ge(e_x[j % 2], 16 * (j // 2 + 1))
                if j:
                    pe.wait_ge(e_xc, j)
                for k in range(KD):
                    last = nc.tensor.transpose(bank(2 + k // 4)[:, P * (k % 4):P * (k % 4 + 1)],
                                               xg[j % 2][:, k * P:(k + 1) * P], ident)
                last.then_inc(e_xt, 1)

            turn_block(0)
            for j in range(NB):
                at = pe.value_load(eint_at[:, 0, j:j + 1], min_val=0, max_val=WSET)
                pe.wait_ge(e_w[(j + 1) % 2], 16 * ((j + 1) // 2 + (1 if j % 2 == 0 else 0)))
                if j >= 1:
                    pass
                pe.wait_ge(e_xc, j + 1)
                x = xT[j % 2]
                if j:
                    pe.wait_ge(e_hid, j)
                for w, s in ((0, e_g), (1, e_u)):
                    for k in range(KD):
                        last = nc.tensor.matmul(bank(w), x[:, k * P:(k + 1) * P],
                                                arena[:, bass.ds(at + (4096 * w + 512 * k), 512)],
                                                start=(k == 0), stop=(k == KD - 1))
                    last.then_inc(s, 1)
                if j + 1 < NB:
                    turn_block(j + 1)
                pe.wait_ge(e_hid, j + 1)
                for k in range(4):
                    last = nc.tensor.transpose(bank(4)[:, k * P:(k + 1) * P], ehid[:, k * P:(k + 1) * P], ident)
                last.then_inc(e_ht, 1)
                pe.wait_ge(e_htc, j + 1)
                if j:
                    pe.wait_ge(e_ya, j)
                    pe.wait_ge(e_yd, j)
                for n in range(2):
                    for k in range(4):
                        last = nc.tensor.matmul(bank(6 + n), ehT[:, k * P:(k + 1) * P],
                                                arena[:, bass.ds(at + (8192 + 1024 * k + 512 * n), 512)],
                                                start=(k == 0), stop=(k == 3))
                last.then_inc(e_d, 1)
            end_phase(pe, 16)
            for c in range(NT):
                pe.wait_ge(f_f, c + 1)
                if c >= 2:
                    pe.wait_ge(f_x, c - 1)
                for k in range(KD):
                    last = nc.tensor.transpose(bank(2 * (c % 2) + k // 4)[:, P * (k % 4):P * (k % 4 + 1)],
                                               ff[c % 2][:, k * P:(k + 1) * P], ident)
                last.then_inc(f_t, 1)
            end_phase(pe, 17)
            pe_sumsq(pe, "ss_final", 0, sq_e)
            end_phase(pe, 18)

        @block.scalar
        def _(act):
            S = Steps(act, s_act)
            act.wait_ge(s_const, 16 * 6)
            act.wait_ge(s_x, 16)
            S.then(nc.scalar.activation(cond[:, :], cond[:, :], ACT.Silu), s_cond)
            act_sumsq(act, "ss_mix", 0, sq_a, [X[:, k, :] for k in range(KD)])
            act_root(S, "ss_mix", 0, rt_a, 1.0 / D)
            S.then(nc.scalar.activation(nexpa, v_("alog")[0:16], ACT.Exp))
            act.wait_ge(r_z, 1)
            S.then(nc.scalar.activation(rowt[1][0:16], rowt[0][0:16], ACT.Abs))
            S.then(nc.scalar.activation(rowt[1][0:16], rowt[1][0:16], ACT.Exp, scale=-1.0))
            S.then(nc.scalar.activation(rowt[1][0:16], rowt[1][0:16], ACT.Ln, bias=ones[0:16, 0:1]), r_l)
            S.then(nc.scalar.activation(rows[64:80, :], rowt[0][0:16], ACT.Sigmoid))
            end_phase(act, 0)
            for m in range(12):
                act_conv_in(S, "qkv", m, m, cb_g)
                if m:
                    act.wait_ge(s_conv, m)
                    nc.scalar.activation(QKV[:, m - 1, :], QKV[:, m - 1, :], ACT.Silu)
            act.wait_ge(s_conv, 12)
            nc.scalar.activation(QKV[:, 11, :], QKV[:, 11, :], ACT.Silu)
            for m in range(KM):
                s = wait_fill(act, "zb", m)
                nc.scalar.activation(tri3(Y[:, m, :]), pset(s), ACT.Silu).then_inc(s_free[s], 1)
            end_phase(act, 1)
            for m in range(8):
                act_sumsq(act, "qkn", m, sq_a, [QKV[:, m, :]])
                act_root(S, "qkn", m, rt_a, 1.0)
            end_phase(act, 2)
            for c in range(NT):
                sample = c == NC7
                act.wait_ge(c_cols, c + 1)
                nc.scalar.activation(colE, colG[:, 0:16], ACT.Exp)
                act.wait_ge(c_diff, c + 1)
                nc.scalar.activation(cEG, bank(0), ACT.Exp)
                nc.scalar.activation(cDT, cDT, ACT.Exp).then_inc(c_exp, 1)
                for n in range(LEV0[c], LEV0[c] + LEV[c]):
                    act.wait_ge(c_p, n + 1)
                    nc.scalar.activation(cPS, bank(0), ACT.Copy).then_inc(c_ps, 1)
                act.wait_ge(c_u, c + (2 if sample else 1))
                nc.scalar.activation(cU, bank(7 if sample else 4), ACT.Copy).then_inc(c_us, 1)
            end_phase(act, 3)
            for m in range(GH):
                act_sumsq(act, "gdn_ss", m, sq_a, [QKV[:, m, :]])
                act_root(S, "gdn_ss", m, rt_a, 1.0 / P)
            end_phase(act, 4)
            act_merge(act, 1)
            end_phase(act, 5)
            for m in range(8):
                act_conv_in(S, "xbc", m, 12 + m, cb_s)
                if m:
                    act.wait_ge(s_conv, 12 + m)
                    nc.scalar.activation(XBC[:, m - 1, :], XBC[:, m - 1, :], ACT.Silu)
            act.wait_ge(s_conv, 20)
            nc.scalar.activation(XBC[:, 7, :], XBC[:, 7, :], ACT.Silu)
            for m in range(KM):
                s = wait_fill(act, "zd", m)
                nc.scalar.activation(tri3(Y[:, m, :]), pset(s), ACT.Silu).then_inc(s_free[s], 1)
            end_phase(act, 6)
            for c in range(NT):
                act.wait_ge(d_diff, c + 1)
                nc.scalar.activation(dDT, dDT, ACT.Exp)
                nc.scalar.activation(dEG, psum[:, 0:1024], ACT.Exp).then_inc(d_exp, 1)
            act.wait_ge(s_pstate, 16 * 4)
            end_phase(act, 7)
            act.wait_ge(d_gated, KM)
            act_sumsq(act, "ssd_ss", 0, sq_s, [XBC[:, m, :] for m in range(KM)])
            act_root(S, "ssd_ss", 0, rt_s, 1.0 / MIX)
            end_phase(act, 8)
            act_merge(act, 3)
            end_phase(act, 9)
            lam = v_("lru_lambda", 0, 4)
            S.then(nc.scalar.activation(lruc[:, 8:12], lam, ACT.Abs))
            S.then(nc.scalar.activation(lruc[:, 8:12], lruc[:, 8:12], ACT.Exp, scale=-1.0))
            S.then(nc.scalar.activation(lruc[:, 8:12], lruc[:, 8:12], ACT.Ln, bias=ones[:, 0:1]), l_sp)
            for m in range(4):
                act_conv_in(S, "xc", m, 20 + m, cb_l)
            for m in range(4):
                s = wait_fill(act, "gc", m)
                nc.scalar.activation(tri3(Y[:, m, :]), pset(s), ACT.Gelu_apprx_tanh).then_inc(s_free[s], 1)
            act.wait_ge(l_col, 1)
            for m in range(4):
                s = wait_fill(act, "lru_r", m)
                if m:
                    act.wait_ge(l_done, m)
                nc.scalar.activation(tri3(lt[0]), pset(s), ACT.Sigmoid, bias=v_("lru_b_a", m)).then_inc(s_free[s], 1)
                freed(act, "lru_r", m)
                s = wait_fill(act, "lru_i", m)
                nc.scalar.activation(tri3(lt[1]), pset(s), ACT.Sigmoid, bias=v_("lru_b_x", m)).then_inc(s_free[s], 1)
                nc.scalar.activation(lt[2], lt[0], ACT.Exp, scale=lruc[:, 4 + m:5 + m])
                nc.scalar.activation(lt[3], lt[0], ACT.Tanh, scale=lruc[:, m:m + 1]).then_inc(l_a, 1)
                act.wait_ge(l_m, m + 1)
                nc.scalar.activation(lt[4], lt[4], ACT.Sqrt).then_inc(l_b, 1)
            end_phase(act, 10)
            act_merge(act, 2)
            end_phase(act, 11)
            S.then(nc.scalar.activation(s5("dt"), v_("s5_dt", 0, 16), ACT.Exp), a_mag)
            act.wait_ge(a_th, 1)
            nc.scalar.activation(s5("mag"), s5("mag"), ACT.Exp)
            nc.scalar.activation(s5("sin"), s5("sin"), ACT.Sin)
            nc.scalar.activation(s5("cos"), s5("cos"), ACT.Sin).then_inc(a_sin, 1)
            for m in range(4):
                s = wait_fill(act, "ua", m)
                nc.scalar.activation(tri3(U[:, m, :]), pset(s), ACT.Copy).then_inc(s_free[s], 1)
                freed(act, "ua", m)
                act.sem_inc(a_u, 1)
            for j in range(16):
                i, q = divmod(j, 4)
                for n in range(3):
                    b = 3 * j + n
                    act.wait_ge(a_y, b + 1)
                    nc.scalar.activation(Y[32 * q:32 * q + 32, i, n * N3:(n + 1) * N3],
                                         psum[32 * q:32 * q + 32, 512 * (6 + b % 2):512 * (6 + b % 2) + N3],
                                         ACT.Copy).then_inc(a_ys, 1)
            for m in range(4):
                act.wait_ge(a_yd, m + 1)
                nc.scalar.activation(U[:, m, :], Y[:, m, :], ACT.Gelu_apprx_tanh).then_inc(a_g, 1)
            for m in range(4):
                s = wait_fill(act, "glu", m)
                nc.scalar.activation(tri3(st[m]), pset(s), ACT.Sigmoid).then_inc(s_free[s], 1)
            end_phase(act, 12)
            act_merge(act, 0)
            end_phase(act, 13)
            end_phase(act, 14)
            act_sumsq(act, "ss_moe", 0, sq_e, [X[:, k, :] for k in range(KD)])
            act_root(S, "ss_moe", 0, rt_e, 1.0 / D)
            act.wait_ge(m_r, 1)
            nc.scalar.activation(scores, bank(7)[:, 0:144], ACT.Sigmoid).then_inc(m_sc, 1)
            for c in range(NT):
                act.wait_ge(m_ht, c + 1)
                if c >= 2:
                    act.wait_ge(m_hst[c % 2], 16 * (c // 2))
                nc.scalar.activation(htok[c % 2], psum[:, 1024 * (c % 2):1024 * (c % 2 + 1)], ACT.Copy).then_inc(m_htok, 1)
            act.wait_ge(m_hst[0], 16 * 5)
            act.wait_ge(m_hst[1], 16 * 4)
            end_phase(act, 15)
            def act_turned(j):
                act.wait_ge(e_xt, j + 1)
                if j >= 2:
                    act.wait_ge(e_u, j - 1)
                nc.scalar.activation(xT[j % 2], psum[:, 1024:2048], ACT.Copy).then_inc(e_xc, 1)
            act_turned(0)
            for j in range(NB):
                act.wait_ge(e_g, j + 1)
                if j:
                    act.wait_ge(e_hid, j)
                nc.scalar.activation(esg, bank(0), ACT.Silu).then_inc(e_sg, 1)
                if j + 1 < NB:
                    act_turned(j + 1)
                act.wait_ge(e_d, j + 1)
                if j >= 2:
                    act.wait_ge(e_st[j % 2], 16 * (j // 2))
                nc.scalar.activation(yb[j % 2][:, 0:512], bank(6), ACT.Copy).then_inc(e_ya, 1)
            for i in range(2):
                act.wait_ge(e_st[i], 16 * (NB // 2))
            end_phase(act, 16)
            end_phase(act, 17)
            act_sumsq(act, "ss_final", 0, sq_e, [X[:, k, :] for k in range(KD)])
            act_root(S, "ss_final", 0, rt_e, 1.0 / D)
            end_phase(act, 18)

        @block.gpsimd
        def _(pool):
            pool.wait_ge(s_const, 16 * 6)
            pool.wait_ge(m_idz, 16)
            pool.wait_ge(m_posi, 1)
            for k in range(2):
                for c in range(NT):
                    pool.indirect_dma_start(out=slot_token, out_offset=bass.IndirectOffsetOnAxis(
                        ap=posi[:, NT * k + c:NT * k + c + 1], axis=0),
                        in_=c_("token", c, 1), in_offset=None).then_inc(m_scat, 16)
            pool.wait_ge(s_phase, 3 * 16)
            for j in range(NB):
                if j >= 2:
                    pool.wait_ge(e_xt, j - 1)
                pool.indirect_dma_start(out=xg[j % 2], out_offset=None, in_=h_rows, in_offset=bass.IndirectOffsetOnAxis(
                    ap=idxi[:, j:j + 1], axis=0)).then_inc(e_x[j % 2], 16)
            pool.wait_ge(s_phase, 3 * 17)
            for c in range(NT):
                if c >= 2:
                    pool.wait_ge(f_f, c - 1)
                for k in range(2):
                    pool.indirect_dma_start(out=yg[c % 2][k], out_offset=None, in_=y_rows,
                                            in_offset=bass.IndirectOffsetOnAxis(
                                                ap=posi[:, NT * k + c:NT * k + c + 1], axis=0)).then_inc(f_y[c % 2], 16)

        @block.vector
        def _(dve):
            V = Steps(dve, s_dve)
            tt, ts, stt = nc.vector.tensor_tensor, nc.vector.tensor_scalar, nc.vector.scalar_tensor_tensor

            dve.wait_ge(s_const, 16 * 6)
            dve.wait_ge(s_ada, 12)
            V.then(tt(mod3, bank(6)[:, 0:432].rearrange("p (m s) -> p m s", s=9), over(v_("b_ada", 0, 48), 9), ALU.add))
            for w, scale, nw in ((0, 8, "norm_mix"), (1, 32, "norm_moe")):
                V.then(ts(amul3[:, w], mod3[:, scale:scale + 8, :], 1.0, None, ALU.add))
                V.then(tt(amul3[:, w], amul3[:, w], over(v_(nw, 0, 8), 9), ALU.mult))
            dve.wait_ge(s_x, 16)
            dve_recip(V, "ss_mix", 0, rs_a, rt_a)
            V.rs = rs_a
            dve_norm(V, X, HT, amul3[:, 0], mod3[:, 0:8, :])
            V.then(nc.vector.memset(rows[0:64, :], 0.0))
            s = wait_fill(dve, "rows", 0)
            ts(tri3(rowt[0][0:16]), pset(s)[0:16], v_("dtb")[0:16], None, ALU.add).then_inc(s_free[s], 1)
            freed(dve, "rows", 0)
            dve.sem_inc(r_z, 1)
            dve.wait_ge(r_l, 1)
            V.then(stt(out=rowt[3][0:16], in0=rowt[0][0:16], scalar=0.0, in1=rowt[1][0:16], op0=ALU.max, op1=ALU.add))
            V.then(nc.vector.tensor_copy(rows[32:48, :], rowt[3][0:16]))
            V.then(ts(rowt[2][0:16], rowt[3][0:16], nexpa, -1.0, ALU.mult, ALU.mult))
            V.then(nc.vector.memset(rowt[1][0:16], 1.0))
            V.then(nc.vector.memset(rowt[1][0:16, 0:NP_TOK:P], 0.0))
            V.then(nc.vector.memset(rowt[1][0:16, NP_TOK:T:SLEN], 0.0))
            V.then(nc.vector.tensor_tensor_scan(rows[0:16, :], rowt[1][0:16], rowt[2][0:16], 0.0, ALU.mult, ALU.add))
            end_phase(dve, 0)
            dve_cb_start(V, cb_g)
            for m in range(12):
                dve_conv(V, m, cb_g, QKV[:, m, :], "gdn_conv", m, 12)
            end_phase(dve, 1)
            for m in range(8):
                dve_recip(V, "qkn", m, rs_a, rt_a)
                V.then(stt(out=QKV[:, m, :], in0=QKV[:, m, :], scalar=(P ** -0.5 if m < 4 else 1.0), in1=rs_a,
                           op0=ALU.mult, op1=ALU.mult))
            end_phase(dve, 2)
            V.then(nc.vector.memset(cS, 0.0))
            for c in range(NT):
                t0 = c * P
                sample = c == NC7
                dve.wait_ge(c_bc, c + 1)
                V.then(nc.vector.tensor_copy(colG, bank(2)[:, 0:80]), c_cols)
                V.then(tt(hd(cDT, 4), hd(bank(0), 4), over(colG[:, 0:4], P), ALU.subtract))
                V.then(tt(hd(cDT, 4), hd(cDT, 4), by(c_("neg_sample" if sample else "neg_prompt"), 4), ALU.add), c_diff)
                dve.wait_ge(c_exp, c + 1)
                dve.wait_ge(c_gram, c + 1)
                V.then(tt(cLT, cDT, bank(3), ALU.mult))
                V.then(tt(cLT, cLT, bank(1), ALU.mult))
                V.then(tt(cAT, cDT, bank(4), ALU.mult))
                V.then(tt(hd(cQE, 4), QKV[:, 0:4, t0:t0 + P], hd(cEG, 4), ALU.mult))
                V.then(tt(colB, colG[:, 76:80], colE[:, 0:4], ALU.mult))
                if sample:
                    V.then(tt(hd(cUM[:, 0:512], 4), hd(cDT, 4), by(c_("last"), 4), ALU.mult))
                    V.then(nc.vector.reduce_sum(colK[:, 0:4], hd(cUM[:, 0:512], 4), axis=AX.X))
                else:
                    V.then(nc.vector.tensor_copy(colK[:, 0:4], hd(cDT, 4)[:, :, P - 1]))
                dve.wait_ge(c_tok, c + 1)
                V.then(tt(hd(cKE, 4), hd(bank(5), 4), over(colK[:, 0:4], P), ALU.mult))
                V.then(tt(hd(cKB, 4), hd(bank(5), 4), over(colB, P), ALU.mult))
                V.then(tt(hd(cVB, 4), hd(bank(6), 4), over(colG[:, 76:80], P), ALU.mult))
                V.then(nc.vector.tensor_copy(hd(cX, 4), by(ident, 4)))
                V.then(nc.vector.tensor_copy(hd(cXT, 4), by(ident, 4)), c_ops)
                for lv in range(LEV[c]):
                    n = LEV0[c] + lv
                    V.then(tt(hd(cLK, 4), hd(cLT, 4), by(c_("level", P * lv, P), 4), ALU.mult), c_lk)
                    dve.wait_ge(c_d, n + 1)
                    V.then(tt(cX, cX, bank(1), ALU.subtract))
                    V.then(tt(cXT, cXT, bank(2), ALU.subtract), c_x)
                dve.wait_ge(c_w, c + 1)
                V.then(ts(cNW, bank(3), -1.0, None, ALU.mult), c_nw)
                if sample:
                    dve.wait_ge(c_u, c + 1)
                    V.then(nc.vector.tensor_copy(cPS, bank(4)), c_ut)
                dve.wait_ge(c_o, c + 1)
                V.then(nc.vector.tensor_copy(QKV[:, 0:4, t0:t0 + P], hd(bank(5), 4)), c_os)
                if not sample:
                    dve.wait_ge(c_s, c + 1)
                    V.then(tt(hd(cS, 4), hd(cS, 4), hd(cEG, 4)[:, :, P - 1:P].to_broadcast([P, 4, P]), ALU.mult))
                    V.then(tt(cS, cS, bank(6), ALU.add), c_ss)
                else:
                    S0 = wait_load(dve, "gdn_state", 0).rearrange("p (b h v) -> p b h v", b=NSEQ, h=GH)
                    dve.wait_ge(c_us, c + 1)
                    for h in range(GH):
                        V.then(tt(hd(cUM, 8), by(cU[:, h * P:(h + 1) * P], 8), over(c_("row"), P), ALU.mult), c_um)
                        dve.wait_ge(c_s, c + h + 1)
                        V.then(tt(S0[:, :, h, :], S0[:, :, h, :],
                                  over(cEG[:, h * P + SLEN - 1:(h + 1) * P:SLEN], P), ALU.mult))
                        V.then(tt(S0[:, :, h, :], S0[:, :, h, :], hd(psum[:, 0:1024], 8), ALU.add), c_ss)
            end_phase(dve, 3)
            for m in range(GH):
                dve_recip(V, "gdn_ss", m, rs_a, rt_a)
                V.then(stt(out=QKV[:, m, :], in0=QKV[:, m, :], scalar=v_("gdn_norm"), in1=rs_a, op0=ALU.mult, op1=ALU.mult))
                V.then(tt(Y[:, m, :], Y[:, m, :], QKV[:, m, :], ALU.mult))
            dve.wait_ge(s_pstate, 32)
            end_phase(dve, 4)
            dve_merge(V, 1)
            end_phase(dve, 5)
            dve_cb_start(V, cb_s)
            for m in range(8):
                dve_conv(V, 12 + m, cb_s, XBC[:, m, :], "ssd_conv", m, 8, bias=v_("ssd_conv_b", m))
            end_phase(dve, 6)
            V.then(nc.vector.memset(dH, 0.0))
            for c in range(NT):
                t0 = c * P
                sample = c == NC7
                dve.wait_ge(d_bc, c + 1)
                V.then(nc.vector.tensor_copy(colG, bank(2)[:, 0:80]))
                V.then(tt(hd(dDT, 8), hd(psum[:, 0:1024], 8), over(colG[:, 4:12], P), ALU.subtract))
                V.then(tt(hd(dDT, 8), hd(dDT, 8), by(c_("neg_sample" if sample else "neg_prompt"), 8), ALU.add), d_diff)
                V.then(nc.vector.tensor_copy(dB, bank(4)[:, 0:256]))
                V.then(tt(hd(dXD, 8), hd(bank(5), 8), over(colG[:, 36:44], 64), ALU.mult))
                dve.wait_ge(d_exp, c + 1)
                if sample:
                    for g in range(2):
                        V.then(tt(hd(dTMP, 4), hd(dDT[:, 512 * g:512 * (g + 1)], 4), by(c_("last"), 4), ALU.mult))
                        V.then(nc.vector.reduce_sum(colK[:, 4 * g:4 * g + 4], hd(dTMP, 4), axis=AX.X))
                    V.then(nc.vector.tensor_copy(hd(colL, 8), hd(dEG, 8)[:, :, SLEN - 1:P:SLEN]))
                else:
                    V.then(nc.vector.tensor_copy(colK, hd(dDT, 8)[:, :, P - 1]))
                    V.then(nc.vector.tensor_copy(colL[:, 0:8], hd(dEG, 8)[:, :, P - 1]))
                V.then(tt(colW, colK, colG[:, 36:44], ALU.mult))
                V.then(tt(hd(dXW, 8), hd(bank(5), 8), over(colW, 64), ALU.mult))
                d4 = dDT.rearrange("p (g h t) -> p g h t", g=2, h=4)
                e4 = dEG.rearrange("p (g h t) -> p g h t", g=2, h=4)
                V.then(tt(d4, d4, hd(bank(3)[:, 0:256], 2).unsqueeze(2).to_broadcast([P, 2, 4, P]), ALU.mult))
                V.then(tt(e4, e4, XBC[:, 6:8, t0:t0 + P].unsqueeze(2).to_broadcast([P, 2, 4, P]), ALU.mult), d_ops)
                dve.wait_ge(d_y, c + 1)
                for m in range(KM):
                    V.then(stt(out=XBC[:, m, t0:t0 + P], in0=XBC[:, m, t0:t0 + P], scalar=v_("ssd_d", m),
                               in1=bank(6)[:, m * P:(m + 1) * P], op0=ALU.mult, op1=ALU.add),
                           d_ys if m == KM - 1 else None)
                if not sample:
                    dve.wait_ge(d_s, c + 1)
                    V.then(tt(hd(dH, 8), hd(dH, 8), over(colL[:, 0:8], 64), ALU.mult))
                    V.then(tt(dH, dH, bank(7), ALU.add), d_ss)
                else:
                    H0 = wait_load(dve, "ssd_state", 0).rearrange("p (b h d) -> p b h d", b=NSEQ, h=SH)
                    for b in range(NSEQ):
                        V.then(ts(dBM, dB, c_("row", b, 1), None, ALU.mult), d_bm)
                        dve.wait_ge(d_s, c + b + 1)
                        V.then(tt(H0[:, b], H0[:, b], over(hd(colL, 8)[:, :, b], 64), ALU.mult))
                        V.then(tt(H0[:, b], H0[:, b], hd(bank(7), 8), ALU.add), d_ss)
            end_phase(dve, 7)
            for m in range(KM):
                V.then(tt(XBC[:, m, :], XBC[:, m, :], Y[:, m, :], ALU.mult), d_gated)
            dve_recip(V, "ssd_ss", 0, rs_s, rt_s)
            for m in range(KM):
                V.then(stt(out=Y[:, m, :], in0=XBC[:, m, :], scalar=v_("ssd_norm", m), in1=rs_s, op0=ALU.mult, op1=ALU.mult))
            end_phase(dve, 8)
            dve_merge(V, 3)
            end_phase(dve, 9)
            lam = v_("lru_lambda", 0, 4)
            V.then(ts(lruc[:, 12:16], lam, -1.0, 0.0, ALU.mult, ALU.max))
            dve.wait_ge(l_sp, 1)
            V.then(tt(lruc[:, 12:16], lruc[:, 12:16], lruc[:, 8:12], ALU.add))
            V.then(ts(lruc[:, 0:4], lruc[:, 12:16], 8.0, None, ALU.mult))
            V.then(ts(lruc[:, 4:8], lruc[:, 12:16], -8.0, None, ALU.mult), l_col)
            dve_cb_start(V, cb_l)
            for m in range(4):
                dve_conv(V, 20 + m, cb_l, XF[:, m, :], "lru_conv", m, 4, bias=v_("lru_conv_b", m))
            lo = lru_out[:, :].rearrange("p (m b) -> p m b", b=9)
            for m in range(4):
                a, b = lt[2], lt[5]
                first = slice(NP_TOK, T, SLEN)
                dve.wait_ge(l_a, m + 1)
                V.then(tt(lt[4], a, a, ALU.mult))
                V.then(stt(out=lt[4], in0=lt[4], scalar=1.0, in1=lt[3], op0=ALU.add, op1=ALU.mult), l_m)
                V.then(tt(b, lt[1], XF[:, m, :], ALU.mult))
                dve.wait_ge(l_b, m + 1)
                V.then(tt(b, b, lt[4], ALU.mult))
                V.then(tt(lruc[:, 16:24], a[:, first], v_("lru_h0", 8 * m, 8), ALU.mult))
                V.then(tt(b[:, first], b[:, first], lruc[:, 16:24], ALU.add))
                V.then(nc.vector.memset(a[:, first], 0.0))
                V.then(nc.vector.tensor_tensor_scan(b, a, b, 0.0, ALU.mult, ALU.add))
                V.then(nc.vector.tensor_copy(lo[:, m, 0:1], b[:, NP_TOK - 1:NP_TOK]))
                V.then(nc.vector.tensor_copy(lo[:, m, 1:9], b[:, NP_TOK + SLEN - 1:T:SLEN]))
                freed(dve, "gc", m)
                V.then(tt(Y[:, m, :], Y[:, m, :], b, ALU.mult), l_done)
            end_phase(dve, 10)
            dve_merge(V, 2)
            end_phase(dve, 11)
            are, aim = v_("s5_re", 0, 16), v_("s5_im", 0, 16)
            dve.wait_ge(a_mag, 1)
            V.then(tt(s5("mag"), are, s5("dt"), ALU.mult))
            V.then(tt(s5("th"), aim, s5("dt"), ALU.mult))

            def reduce_angle(dst, shift):
                V.then(ts(s5("t1"), s5("th"), shift, None, ALU.add))
                V.then(ts(s5("t0"), s5("t1"), float(1 / (2 * np.pi)), ROUND, ALU.mult, ALU.add))
                V.then(ts(s5("t0"), s5("t0"), ROUND, None, ALU.subtract))
                V.then(stt(out=s5("t1"), in0=s5("t0"), scalar=-TWO_PI_HI, in1=s5("t1"), op0=ALU.mult, op1=ALU.add))
                V.then(stt(out=s5("t1"), in0=s5("t0"), scalar=-TWO_PI_LO, in1=s5("t1"), op0=ALU.mult, op1=ALU.add))
                V.then(ts(dst, s5("t1"), 3.141592, -3.141592, ALU.min, ALU.max))

            reduce_angle(s5("sin"), 0.0)
            reduce_angle(s5("cos"), float(np.pi / 2))
            dve.sem_inc(a_th, 1)
            dve.wait_ge(a_sin, 1)
            V.then(tt(s5("lre"), s5("mag"), s5("cos"), ALU.mult))
            V.then(tt(s5("lim"), s5("mag"), s5("sin"), ALU.mult))
            V.then(tt(s5("den"), are, are, ALU.mult))
            V.then(tt(s5("t0"), aim, aim, ALU.mult))
            V.then(tt(s5("den"), s5("den"), s5("t0"), ALU.add))
            V.then(nc.vector.reciprocal(s5("den"), s5("den")))
            V.then(ts(s5("t0"), s5("lre"), -1.0, None, ALU.add))
            V.then(tt(s5("fre"), s5("t0"), are, ALU.mult))
            V.then(tt(s5("t1"), s5("lim"), aim, ALU.mult))
            V.then(tt(s5("fre"), s5("fre"), s5("t1"), ALU.add))
            V.then(tt(s5("fre"), s5("fre"), s5("den"), ALU.mult))
            V.then(tt(s5("fim"), s5("lim"), are, ALU.mult))
            V.then(tt(s5("t1"), s5("t0"), aim, ALU.mult))
            V.then(tt(s5("fim"), s5("fim"), s5("t1"), ALU.subtract))
            V.then(tt(s5("fim"), s5("fim"), s5("den"), ALU.mult))
            V.then(nc.vector.tensor_copy(s5("pr", 0), s5("cos")))
            V.then(nc.vector.tensor_copy(s5("pi", 0), s5("sin")))
            for k in range(9):
                V.then(tt(s5("t0"), s5("pi", k), s5("pi", k), ALU.mult))
                V.then(tt(s5("pr", k + 1), s5("pr", k), s5("pr", k), ALU.mult))
                V.then(tt(s5("pr", k + 1), s5("pr", k + 1), s5("t0"), ALU.subtract))
                V.then(tt(s5("t0"), s5("pr", k), s5("pi", k), ALU.mult))
                V.then(ts(s5("pi", k + 1), s5("t0"), 2.0, None, ALU.mult))
            x0 = [v_("s5_x0r", 0, 128).rearrange("p (j b) -> p j b", b=8),
                  v_("s5_x0i", 0, 128).rearrange("p (j b) -> p j b", b=8)]
            xs = [s5x[:, 128 * w:128 * (w + 1)].rearrange("p (j b) -> p j b", b=8) for w in range(2)]
            xt = small[:, 256:384].rearrange("p (j b) -> p j b", b=8)
            V.then(tt(xs[0], x0[0], over(s5("lre"), 8), ALU.mult))
            V.then(tt(xt, x0[1], over(s5("lim"), 8), ALU.mult))
            V.then(tt(xs[0], xs[0], xt, ALU.subtract))
            V.then(tt(xs[1], x0[1], over(s5("lre"), 8), ALU.mult))
            V.then(tt(xt, x0[0], over(s5("lim"), 8), ALU.mult))
            V.then(tt(xs[1], xs[1], xt, ALU.add))
            bc = wait_load(dve, "s5_bc", 0)
            br, bi = [bc[:, 512 * w:512 * (w + 1)].rearrange("p (j c) -> p j c", c=32) for w in range(2)]
            t = [x[:, 0:512].rearrange("p (j c) -> p j c", c=32) for x in st[0:4]]
            V.then(tt(t[0], br, over(s5("fre"), 32), ALU.mult))
            V.then(tt(t[1], bi, over(s5("fim"), 32), ALU.mult))
            V.then(tt(t[2], bi, over(s5("fre"), 32), ALU.mult))
            V.then(tt(t[3], br, over(s5("fim"), 32), ALU.mult))
            V.then(tt(br, t[0], t[1], ALU.subtract))
            V.then(tt(bi, t[2], t[3], ALU.add), a_bs)
            dve.wait_ge(a_bt, 1)
            V.then(nc.vector.tensor_copy(sBT, psum[:, 6 * 512:8 * 512]), a_btc)
            V.then(nc.vector.memset(sMASK, 1.0))
            V.then(nc.vector.memset(sMASK[:, NP_TOK:T:SLEN], 0.0))
            so = s5_out[:, :].rearrange("p (w j b) -> p w j b", w=2, b=9)
            first = slice(NP_TOK, T, SLEN)
            for j in range(16):
                V.then(nc.vector.memset(sCOS[:, 0:1], 1.0))
                V.then(nc.vector.memset(sSIN[:, 0:1], 0.0))
                for k in range(10):
                    n = 1 << k
                    pr, pi = s5("pr", k)[:, j:j + 1], s5("pi", k)[:, j:j + 1]
                    ts(st[0][:, 0:n], sSIN[:, 0:n], pi, None, ALU.mult)
                    V.then(ts(st[1][:, 0:n], sCOS[:, 0:n], pi, None, ALU.mult))
                    stt(out=sCOS[:, n:2 * n], in0=sCOS[:, 0:n], scalar=pr, in1=st[0][:, 0:n], op0=ALU.mult, op1=ALU.subtract)
                    V.then(stt(out=sSIN[:, n:2 * n], in0=sSIN[:, 0:n], scalar=pr, in1=st[1][:, 0:n],
                               op0=ALU.mult, op1=ALU.add))
                nc.vector.tensor_copy(seqs(sCOS), by(sCOS[:, 0:SLEN], 8))
                V.then(nc.vector.tensor_copy(seqs(sSIN), by(sSIN[:, 0:SLEN], 8)))
                sA, sB = wait_fill(dve, "bu_re", j), wait_fill(dve, "bu_im", j)
                c3, s3 = tri3(sCOS), tri3(sSIN)
                tt(tri3(st[0]), pset(sA), c3, ALU.mult)
                V.then(tt(tri3(st[1]), pset(sB), s3, ALU.mult))
                V.then(tt(st[4], st[0], st[1], ALU.add))
                tt(tri3(st[0]), pset(sA), s3, ALU.mult).then_inc(s_free[sA], 1)
                tt(tri3(st[1]), pset(sB), c3, ALU.mult).then_inc(s_free[sB], 1)
                freed(dve, "bu_re", j)
                freed(dve, "bu_im", j)
                V.then(tt(st[5], st[1], st[0], ALU.subtract))
                tt(st[4][:, first], st[4][:, first], xs[0][:, j, :], ALU.add)
                tt(st[5][:, first], st[5][:, first], xs[1][:, j, :], ALU.add)
                V.then(ts(st[0], sMASK, s5("mag")[:, j:j + 1], None, ALU.mult))
                nc.vector.tensor_tensor_scan(st[4], st[0], st[4], 0.0, ALU.mult, ALU.add)
                V.then(nc.vector.tensor_tensor_scan(st[5], st[0], st[5], 0.0, ALU.mult, ALU.add))
                tt(st[0], st[4], sCOS, ALU.mult)
                V.then(tt(st[1], st[5], sSIN, ALU.mult))
                if j:
                    dve.wait_ge(a_y, 3 * j)
                V.then(tt(st[2], st[0], st[1], ALU.subtract))
                tt(st[0], st[4], sSIN, ALU.mult)
                V.then(tt(st[1], st[5], sCOS, ALU.mult))
                V.then(stt(out=st[3], in0=st[0], scalar=-1.0, in1=st[1], op0=ALU.mult, op1=ALU.subtract), a_x)
                nc.vector.tensor_copy(so[:, 0, j, 0:1], st[2][:, NP_TOK - 1:NP_TOK])
                nc.vector.tensor_copy(so[:, 0, j, 1:9], st[2][:, NP_TOK + SLEN - 1:T:SLEN])
                ts(so[:, 1, j, 0:1], st[3][:, NP_TOK - 1:NP_TOK], -1.0, None, ALU.mult)
                V.then(ts(so[:, 1, j, 1:9], st[3][:, NP_TOK + SLEN - 1:T:SLEN], -1.0, None, ALU.mult))
            for m in range(4):
                dve.wait_ge(a_ys, 12 * (m + 1))
                V.then(stt(out=Y[:, m, :], in0=U[:, m, :], scalar=v_("s5_d", m), in1=Y[:, m, :], op0=ALU.mult, op1=ALU.add),
                       a_yd)
            for m in range(4):
                freed(dve, "glu", m)
                V.then(tt(Y[:, m, :], U[:, m, :], st[m], ALU.mult), a_gs)
            end_phase(dve, 12)
            dve_merge(V, 0)
            end_phase(dve, 13)
            dve.wait_ge(s_xr, 16)
            for m in range(KD):
                dve_residual(V, "out", m, 16, res_tmp)
            end_phase(dve, 14)
            dve_recip(V, "ss_moe", 0, rs_e, rt_e)
            V.rs = rs_e
            dve_norm(V, X, HT, amul3[:, 1], mod3[:, 24:32, :])
            V.then(nc.vector.memset(cmpB[:, 0:NB], 0.0), m_zero)
            V.then(nc.vector.memset(ones_row[0:16], 1.0))
            dve.wait_ge(m_idz, 16)
            dve.wait_ge(m_sc, 1)
            V.then(tt(hd(rsel, 9), hd(scores, 9), by(v_("rbias", 0, NE), 9), ALU.add))

            def ranks(dst, src, n):
                s4 = src.rearrange("p (n j) -> p n j", j=4)
                si, sj = s4.unsqueeze(2).to_broadcast([P, n, 4, 4]), s4.unsqueeze(3).to_broadcast([P, n, 4, 4])
                ca = cmpA[:, 0:16 * n].rearrange("p (n j i) -> p n j i", j=4, i=4)
                cb_ = cmpB[:, 0:16 * n].rearrange("p (n j i) -> p n j i", j=4, i=4)
                V.then(tt(ca, si, sj, ALU.is_gt))
                V.then(tt(cb_, si, sj, ALU.is_equal))
                V.then(tt(cmpB[:, 0:16 * n].rearrange("p (n x) -> p n x", x=16),
                          cmpB[:, 0:16 * n].rearrange("p (n x) -> p n x", x=16), by(c_("tri"), n), ALU.mult))
                V.then(tt(cmpA[:, 0:16 * n], cmpA[:, 0:16 * n], cmpB[:, 0:16 * n], ALU.add))
                V.then(nc.vector.reduce_sum(dst.rearrange("p (n j) -> p n j", j=4), ca, axis=AX.X))

            ranks(rank, rsel, 36)
            V.then(ts(picked, rank, 1.5, None, ALU.is_lt))
            V.then(tt(rtmp, picked, rsel, ALU.mult))
            V.then(nc.vector.reduce_sum(grp[:, 0:36], hd(rtmp, 36), axis=AX.X))
            ranks(grp[:, 36:72], grp[:, 0:36], 9)
            V.then(ts(grp[:, 36:72], grp[:, 36:72], 0.5, None, ALU.is_lt))
            V.then(tt(hd(picked, 36), hd(picked, 36), over(grp[:, 36:72], 4), ALU.mult), m_mask)
            V.then(ts(first1, rank, 0.5, None, ALU.is_lt))
            V.then(tt(first1, first1, picked, ALU.mult))
            V.then(tt(weight, scores, picked, ALU.mult))
            V.then(nc.vector.reduce_sum(grp[:, 72:81], hd(weight, 9), axis=AX.X))
            V.then(nc.vector.reciprocal(grp[:, 72:81], grp[:, 72:81]))
            V.then(tt(hd(weight, 9), hd(weight, 9), over(grp[:, 72:81], NE), ALU.mult))

            def pick_both(dst, src):
                V.then(tt(rtmp, src, first1, ALU.mult))
                V.then(nc.vector.reduce_sum(dst[:, 0, :], hd(rtmp, 9), axis=AX.X))
                V.then(tt(rsel, src, picked, ALU.mult))
                V.then(tt(rsel, rsel, rtmp, ALU.subtract))
                V.then(nc.vector.reduce_sum(dst[:, 1, :], hd(rsel, 9), axis=AX.X))

            pick_both(w12, weight)
            dve.wait_ge(m_maskt, 1)
            V.then(nc.vector.tensor_copy(mask_row[0:16], psum[0:16, 2048:2048 + T]))
            V.then(nc.vector.tensor_tensor_scan(cum_row[0:16], ones_row[0:16], mask_row[0:16], 0.0, ALU.mult, ALU.add))
            V.then(ts(ecol[:, 0:1], cum_row[0:16, T - 1:T], 1.0 / BLK, (BLK - 1.0) / BLK - 0.498, ALU.mult, ALU.add))
            V.then(ts(ecol[:, 0:1], ecol[:, 0:1], ROUND, None, ALU.add))
            V.then(ts(ecol[:, 1:2], ecol[:, 0:1], ROUND, None, ALU.subtract), m_nblk)
            dve.wait_ge(m_start, 1)
            V.then(tt(ecol[:, 2:3], bank(7)[0:16, 200:201], ecol[:, 1:2], ALU.add))
            V.then(ts(ecol[:, 3:4], bank(7)[0:16, 200:201], float(BLK), -1.0, ALU.mult, ALU.add))
            V.then(ts(cum_row[0:16], cum_row[0:16], ecol[:, 3:4], None, ALU.add))
            V.then(ts(cmpB[0:16, 0:NB], c_("block")[0:16], ecol[:, 2:3], None, ALU.is_ge), m_pos)
            dve.wait_ge(m_post, 1)
            V.then(nc.vector.tensor_copy(cmpA[:, 0:144], bank(7)[:, 0:144]))
            V.then(ts(erow[:, 0, :], bank(7)[0:1, 256:256 + NB], NE - 1.0, None, ALU.min))
            pick_both(posf.rearrange("p (k c) -> p k c", k=2), cmpA[:, 0:144])
            V.then(nc.vector.tensor_copy(posi, posf), m_posi)
            ei, ej = erow[:, 0, :], erow[:, 0, :]
            big = btab[0:1].rearrange("p (j i) -> p j i", i=NB)
            V.then(tt(big, ei.unsqueeze(1).to_broadcast([1, NB, NB]), ej.unsqueeze(2).to_broadcast([1, NB, NB]), ALU.is_le))
            V.then(stt(out=big, in0=big, scalar=100.0, in1=ei.unsqueeze(1).to_broadcast([1, NB, NB]),
                       op0=ALU.mult, op1=ALU.add))
            V.then(nc.vector.tensor_reduce(erow[:, 1, :], big, AX.X, ALU.min))
            V.then(ts(erow[:, 1, :], erow[:, 1, :], NE - 1.0, None, ALU.min))
            V.then(nc.vector.memset(erow[:, 2, :], 1.0))
            V.then(tt(erow[:, 2, 1:NB], erow[:, 0, 1:NB], erow[:, 0, 0:NB - 1], ALU.not_equal))
            V.then(nc.vector.memset(erow[:, 4, :], 1.0))
            V.then(nc.vector.tensor_tensor_scan(erow[:, 3, :], erow[:, 4, :], erow[:, 2, :], 0.0, ALU.mult, ALU.add))
            V.then(ts(erow[:, 4, :], erow[:, 3, :], 0.5, -0.25, ALU.mult, ALU.add))
            V.then(ts(erow[:, 4, :], erow[:, 4, :], ROUND, None, ALU.add))
            V.then(ts(erow[:, 4, :], erow[:, 4, :], ROUND, None, ALU.subtract))
            V.then(stt(out=erow[:, 4, :], in0=erow[:, 4, :], scalar=-2.0, in1=erow[:, 3, :], op0=ALU.mult, op1=ALU.add))
            V.then(ts(erow[:, 3, :], erow[:, 4, :], float(WSET), None, ALU.mult))
            V.then(ts(erow[:, 5, :], erow[:, 3, :], -1.0, float(WSET), ALU.mult, ALU.add))
            V.then(nc.vector.tensor_copy(eint, erow[:, 0:4, :]))
            V.then(nc.vector.tensor_copy(eint_at[:, 0, :], erow[:, 5, :]), m_tab)
            dve.wait_ge(m_idt, 1)
            V.then(nc.vector.tensor_copy(idxi, bank(4)[:, 0:NB]), m_idx)
            end_phase(dve, 15)
            for j in range(NB):
                dve.wait_ge(e_sg, j + 1)
                dve.wait_ge(e_u, j + 1)
                if j:
                    dve.wait_ge(e_ht, j)
                tt(ehid, esg, bank(1), ALU.mult).then_inc(e_hid, 1)
                dve.wait_ge(e_ht, j + 1)
                nc.vector.tensor_copy(ehT, bank(4)).then_inc(e_htc, 1)
                dve.wait_ge(e_d, j + 1)
                if j >= 2:
                    dve.wait_ge(e_st[j % 2], 16 * (j // 2))
                nc.vector.tensor_copy(yb[j % 2][:, 512:1024], bank(7)).then_inc(e_yd, 1)
            end_phase(dve, 16)
            for c in range(NT):
                for k in range(2):
                    dve.wait_ge(f_y[c % 2], 32 * (c // 2 + 1))
                if c >= 2:
                    dve.wait_ge(f_t, c - 1)
                V.then(ts(ff[c % 2], yg[c % 2][0], w12[:, 0, c:c + 1], None, ALU.mult))
                V.then(stt(out=ff[c % 2], in0=yg[c % 2][1], scalar=w12[:, 1, c:c + 1], in1=ff[c % 2],
                           op0=ALU.mult, op1=ALU.add), f_f)
                dve.wait_ge(f_t, c + 1)
                p8 = psum[:, 1024 * (c % 2):1024 * (c % 2 + 1)]
                xc = X[:, :, c * P:(c + 1) * P]
                if c < NT - 1:
                    V.then(tt(hd(ftmp, 8), hd(p8, 8), over(mod3[:, 40:48, 0], P), ALU.mult))
                else:
                    V.then(tt(ftmp.rearrange("p (k b t) -> p k b t", k=8, b=8), p8.rearrange("p (k b t) -> p k b t", k=8, b=8),
                              mod3[:, 40:48, 1:9].unsqueeze(3).to_broadcast([P, 8, 8, SLEN]), ALU.mult))
                V.then(tt(xc, xc, hd(ftmp, 8), ALU.add), f_x)
            end_phase(dve, 17)
            dve_recip(V, "ss_final", 0, rs_e, rt_e)
            for k in range(KD):
                V.then(stt(out=HT[:, k, :], in0=X[:, k, :], scalar=v_("norm_final", k), in1=rs_e, op0=ALU.mult, op1=ALU.mult))
            end_phase(dve, 18)


def _outs():
    return {"yT": (P, KD, T), "hist_out": (P, 24 * 27), "s5_out": (P, 288), "lru_out": (P, 36),
            "gdn_p": (P, 512), "gdn_s": (P, 4096), "ssd_p": (P, 512), "ssd_s": (P, 4096)}


def _constants():
    c = np.zeros((P, NCST), np.float32)

    def put(name, a):
        o, w = CST[name]
        c[:, o:o + w] = a
    s, t = np.arange(P)[:, None], np.arange(P)[None, :]
    put("ident", np.eye(P))
    put("ones", 1.0)
    put("level", np.concatenate([(s >> (k + 1) == t >> (k + 1)) & ((s >> k) & 1 == 0) & ((t >> k) & 1 == 1)
                                 for k in range(7)], axis=1))
    put("neg_prompt", np.where(t >= s, 0.0, -1e30))
    put("neg_sample", np.where((t >= s) & (t // SLEN == s // SLEN), 0.0, -1e30))
    put("last", np.broadcast_to(t % SLEN == SLEN - 1, (P, P)))
    put("row", s // SLEN == np.arange(NSEQ)[None, :])
    put("eps", EPS)
    put("token", s + P * np.arange(NT)[None, :])
    put("block", np.broadcast_to(np.arange(NB), (P, NB)))
    put("before", s < np.arange(NE)[None, :])
    j, i = np.arange(16) // 4, np.arange(16) % 4
    put("tri", np.broadcast_to(i < j, (P, 16)))
    return c


def _pack(w):
    k, m = w.shape[0] // P, w.shape[1] // P
    per = 32 // k
    a = w.reshape(k, P, m, P).transpose(2, 1, 0, 3).reshape(m // per, per, P, k, P)
    return np.ascontiguousarray(a.transpose(0, 2, 1, 3, 4)).reshape(m // per, P, 4096)


def kernel(**inputs):
    import concourse.bacc as _bacc
    from concourse import mybir as _mybir
    from concourse.bass_utils import run_bass_kernel_spmd as _run

    i = {k: np.asarray(v) for k, v in inputs.items()}
    f = np.float32

    def cols(v):
        return v.reshape(-1, P).T

    def padded(a):
        out = np.zeros((P, 4096), f)
        out[:, :a.shape[1]] = a
        return out[None]

    arr = {"cst": _constants()}
    arr["xT"] = np.ascontiguousarray(np.concatenate([i["x_prompt"].reshape(NP_TOK, D), i["x_sample"].reshape(P, D)])
                                     .T.reshape(KD, P, T).transpose(1, 0, 2))
    c = np.concatenate([i["c_prompt"], i["c_sample"]])
    arr["cT"] = np.ascontiguousarray(c.T.reshape(KD, P, 9).transpose(1, 0, 2)).reshape(P, 72)
    vec = np.zeros((P, NVEC), f)

    def put(name, a):
        o, w = VEC[name]
        vec[:a.shape[0], o:o + w] = a
    for n, src in (("norm_mix", "norm_mix_w"), ("norm_moe", "norm_moe_w"), ("b_ada", "b_ada"), ("s5_d", "s5_d"),
                   ("gdn_norm", "gdn_norm_w"), ("lru_conv_b", "lru_conv_b"), ("lru_b_a", "lru_b_a"),
                   ("lru_b_x", "lru_b_x"), ("lru_lambda", "lru_lambda"), ("ssd_conv_b", "ssd_conv_b"),
                   ("ssd_norm", "ssd_norm_w"), ("s5_re", "s5_a_re"), ("s5_im", "s5_a_im")):
        put(n, cols(i[src][0].reshape(-1)))
    put("norm_final", cols(i["norm_final_w"]))
    for n, src in (("gdn_conv", "gdn_conv_w"), ("lru_conv", "lru_conv_w"), ("ssd_conv", "ssd_conv_w")):
        put(n, cols(i[src][0].reshape(-1)))
    put("ssd_d", cols(np.repeat(i["ssd_d"][0], 64)))
    put("s5_dt", cols(np.repeat(i["s5_log_dt"][0], 64)))
    zero4 = np.zeros(4, f)
    put("alog", np.concatenate([i["gdn_a_log"][0], i["ssd_a_log"][0], zero4])[:, None])
    put("dtb", np.concatenate([i["gdn_dt_bias"][0], i["ssd_dt_bias"][0], zero4])[:, None])
    put("rbias", np.broadcast_to(i["router_bias"], (P, NE)))
    put("lru_h0", i["state_lru"][0].reshape(8, 4, P).transpose(2, 1, 0).reshape(P, 32))
    for n, src in (("s5_x0r", "state_s5_re"), ("s5_x0i", "state_s5_im")):
        put(n, i[src][0].reshape(8, 16, P).transpose(2, 1, 0).reshape(P, 128))
    arr["vec"] = vec
    h = np.concatenate([i["cache_gdn_conv"][0], i["cache_ssd_conv"][0], i["cache_lru_conv"][0]], axis=2)
    arr["hist"] = np.ascontiguousarray(h.reshape(8, 3, 24, P).transpose(3, 2, 0, 1)).reshape(P, 576)
    w = i["w_in"][0]
    o = dict(ua=0, qkv=512, zb=2048, ab=2560, bb=2564, xc=2568, gc=3080, zd=3592, xbc=4104, dt=5128, gate=5136)
    for n, width in (("ua", 512), ("qkv", 1536), ("zb", 512), ("xc", 512), ("gc", 512), ("zd", 512), ("xbc", 1024)):
        arr[n] = _pack(w[:, o[n]:o[n] + width])
    for k in range(4):
        arr["gate%d" % k] = _pack(w[:, o["gate"] + 1024 * k:o["gate"] + 1024 * (k + 1)])
        arr["br%d" % k] = _pack(i["w_branch"][0, k])
    nar = np.concatenate([w[:, o["ab"]:o["ab"] + 4], w[:, o["dt"]:o["dt"] + 8], w[:, o["bb"]:o["bb"] + 4]], axis=1)
    arr["wrows"] = np.ascontiguousarray(nar.reshape(KD, P, 16).transpose(1, 0, 2)).reshape(P, 128)
    arr["wrouter"] = np.ascontiguousarray(i["router_w"].reshape(KD, P, 16).transpose(1, 0, 2)).reshape(P, 128)
    arr["ada"] = _pack(i["w_ada"][0])
    arr["out"] = _pack(i["w_out"][0])
    g = i["s5_w_glu"][0].reshape(4, P, 4, P).transpose(1, 2, 0, 3).reshape(P, 2048)
    arr["glu"] = padded(g)
    arr["moe"] = np.concatenate([i[n][0].reshape(NE, -1, P, wd).transpose(0, 2, 1, 3).reshape(NE, P, 4096)
                                 for n, wd in (("moe_w_gate", 512), ("moe_w_up", 512), ("moe_w_down", 1024))], axis=2)
    arr["gdn_state"] = np.ascontiguousarray(i["state_gdn"][0].transpose(2, 0, 1, 3)).reshape(1, P, 4096)
    arr["ssd_state"] = np.ascontiguousarray(i["state_ssd"][0].transpose(3, 0, 1, 2)).reshape(1, P, 4096)
    lw = np.zeros((P, 2, 4, P), f)
    for j, n in enumerate(("lru_w_a", "lru_w_x")):
        for b in range(8):
            r = 64 * (b % 2)
            lw[r:r + 64, j, b // 2, r:r + 64] = i[n][0, b]
    arr["lru_w"] = padded(lw.reshape(P, 1024))
    sbc = np.zeros((P, 4, 16, 32), f)
    for j, (n, tr) in enumerate((("s5_b_re", 0), ("s5_b_im", 0), ("s5_c_re", 1), ("s5_c_im", 1))):
        for gr in range(32):
            a = i[n][0, gr]
            a = a.T if tr else a
            r = 64 * (gr % 2)
            sbc[r:r + 64, j, gr // 2, 16 * (gr % 2):16 * (gr % 2) + 16] = a
    arr["s5_bc"] = padded(sbc.reshape(P, 2048))

    nc = _bacc.Bacc("TRN2", target_bir_lowering=False, num_devices=1)
    arrays, aps = {}, {}
    for name, a in arr.items():
        a = np.ascontiguousarray(a)
        arrays["in_" + name] = a
        aps[name] = nc.dram_tensor("in_" + name, a.shape, F32, kind="ExternalInput").ap()
    for name, shape in _outs().items():
        aps[name] = nc.dram_tensor("out_" + name, shape, F32, kind="ExternalOutput").ap()
    for name, shape in (("h_rows", (T, D)), ("y_rows", (NB * BLK, D)), ("slot_token", (NB * BLK, 1))):
        aps[name] = nc.dram_tensor(name, shape, F32, kind="Internal").ap()
    build(nc, aps)
    r = _run(nc, [arrays], core_ids=[0]).results[0]
    o = {name: np.asarray(r["out_" + name]) for name in _outs()}
    y = o["yT"].transpose(1, 0, 2).reshape(D, T).T
    ho = o["hist_out"].reshape(P, 24, 9, 3).transpose(2, 3, 1, 0).reshape(9, 3, 24 * P)
    s5 = o["s5_out"].reshape(P, 2, 16, 9).transpose(1, 3, 2, 0).reshape(2, 9, 32, 64)
    lru = o["lru_out"].reshape(P, 4, 9).transpose(2, 1, 0).reshape(9, MIX)
    gp = o["gdn_p"].reshape(P, 1, GH, P).transpose(1, 2, 0, 3)
    gs = o["gdn_s"].reshape(P, NSEQ, GH, P).transpose(1, 2, 0, 3)
    sp_ = o["ssd_p"].reshape(P, 1, SH, 64).transpose(1, 2, 3, 0)
    ss = o["ssd_s"].reshape(P, NSEQ, SH, 64).transpose(1, 2, 3, 0)
    got = [y[:NP_TOK].reshape(1, NP_TOK, D), y[NP_TOK:].reshape(NSEQ, SLEN, D)]
    for a, b, gd, sd in ((0, 1, gp, sp_), (1, 9, gs, ss)):
        got += [s5[0, a:b][None], s5[1, a:b][None], gd[None], ho[a:b, :, 0:1536][None], lru[a:b][None],
                ho[a:b, :, 2560:3072][None], sd[None], ho[a:b, :, 1536:2560][None]]
    return tuple(np.ascontiguousarray(x) for x in got)
```

```python
from contextlib import ExitStack

import numpy as np

import concourse.bass as bass
from concourse import mybir

F32 = mybir.dt.float32
ALU = mybir.AluOpType
ACT = mybir.ActivationFunctionType
AX = mybir.AxisListType

P = 128
D = 1024
KD = D // P
NP_TOK, NSEQ, SLEN = 1024, 8, 16
T = NP_TOK + NSEQ * SLEN
N3 = T // 3
NT = T // P
MIX = D // 2
KM = MIX // P
GH, SH = 4, 8
NE = 16
BLK = 128
NB = -(-(2 * T + NE * (BLK - 1)) // BLK)
EPS = 1e-6
Q5 = 8
NQ = T // Q5
NQP = NP_TOK // Q5
CW = 3 + NP_TOK + NSEQ * (3 + SLEN)
TWO_PI_HI = 6.28125
TWO_PI_LO = float(2 * np.pi - 6.28125)
ROUND = 12582912.0

CST = {}
def _cst(name, n):
    CST[name] = (sum(v[1] for v in CST.values()), n)
_cst("ident", P); _cst("ones", P); _cst("level", 7 * P)
_cst("neg_prompt", P); _cst("neg_sample", P); _cst("last", P); _cst("row", NSEQ); _cst("eps", 1); _cst("tri", 16)
_cst("token", NT); _cst("block", NB); _cst("before", NE)
NCST = sum(v[1] for v in CST.values())

VEC = {}
def _vec(name, n):
    VEC[name] = (sum(v[1] for v in VEC.values()), n)
for _n, _w in (("norm_mix", 8), ("norm_moe", 8), ("norm_final", 8), ("b_ada", 48), ("s5_d", 16), ("gdn_conv", 48),
               ("gdn_norm", 1), ("lru_conv", 16), ("lru_conv_b", 4), ("lru_b_a", 4), ("lru_b_x", 4), ("lru_lambda", 4),
               ("ssd_conv", 32), ("ssd_conv_b", 8), ("ssd_d", 4), ("ssd_norm", 4), ("s5_re", 16), ("s5_im", 16),
               ("s5_dt", 16), ("alog", 1), ("dtb", 1), ("rbias", NE), ("lru_h0", 32), ("s5_x0r", 128), ("s5_x0i", 128)):
    _vec(_n, _w)
NVEC = sum(v[1] for v in VEC.values())

def plan_tiles():
    names = [("ss_mix", 0, 0)]
    names += [("rows", 0, 1)]
    names += [("qkv", 0, 0), ("qkv", 1, 1)]
    for m in range(2, 10):
        names += [("qkv", m, 0), ("qkn", m - 2, 1)]
    names += [("qkv", 10, 0), ("qkv", 11, 1)]
    names += [("gdn_ss", 0, 0), ("zb", 0, 1), ("gdn_ss", 1, 0), ("zb", 1, 1), ("gdn_ss", 2, 0), ("zb", 2, 1),
              ("zb", 3, 0), ("gdn_ss", 3, 1)]
    def merge(k):
        return [x for m in range(KD) for x in (("gate%d" % k, m, 0), ("br%d" % k, m, 1))]
    names += merge(1)
    names += [("xbc", m, m % 2) for m in range(8)] + [("zd", m, m % 2) for m in range(KM)]
    names += [("ssd_ss", 0, 0)]
    names += merge(3)
    names += [("xc", m, m % 2) for m in range(4)] + [("gc", m, m % 2) for m in range(4)]
    names += [x for m in range(4) for x in (("lru_r", m, 0), ("lru_i", m, 1))]
    names += merge(2)
    names += [("ua", m, m % 2) for m in range(4)]
    names += [("glu", m, m % 2) for m in range(4)]
    names += merge(0)
    names += [("out", m, m % 2) for m in range(KD)]
    names += [("ss_moe", 0, 0)]
    names += [("ss_final", 0, 0)]
    count, at = [0, 0], {}
    for name, m, s in names:
        at[(name, m)] = (s, count[s])
        count[s] += 1
    return at

FILL = plan_tiles()

def plan_loads():
    loads = []
    def add(*names):
        for a, g in names:
            loads.append((a, g, (len(loads)) % 2))
    add(("qkv", 0), ("qkv", 1), ("qkv", 2), ("zb", 0), ("gdn_state", 0))
    def merge(k):
        add(("gate%d" % k, 0), ("br%d" % k, 0), ("gate%d" % k, 1))
    merge(1)
    add(("xbc", 0), ("xbc", 1), ("zd", 0), ("ssd_state", 0))
    merge(3)
    add(("xc", 0), ("gc", 0), ("lru_w", 0))
    merge(2)
    add(("ua", 0), ("s5_bc", 0), ("glu", 0))
    merge(0)
    add(("out", 0), ("out", 1))
    return loads

LOADS = plan_loads()
ADA_SLOT = [0, 1, 2, 3, 4, 5, 0, 1, 4, 5, 0, 1]
ADA_EARLY = 4
SLOT = {(a, g): s for a, g, s in LOADS}

def slot_count(a, g):
    n = 0
    for x, y, s in LOADS:
        if s == SLOT[(a, g)]:
            n += 1
        if (x, y) == (a, g):
            return n

def last_reader(a, g):
    if a in ("gdn_state", "ssd_state", "lru_w", "s5_bc"):
        return None
    if a.startswith("br"):
        return (a, KD - 1)
    if a == "glu":
        return (a, 3)
    return (a, 4 * g + 3)


def build(nc, A):
    with ExitStack() as ctx:
        def sb(name, shape):
            return ctx.enter_context(nc.sbuf_tensor(name, shape, F32))

        def sem(name):
            return ctx.enter_context(nc.semaphore(name))

        cst = sb("cst", [P, NCST])
        vec = sb("vec", [P, NVEC])
        mod = sb("mod", [P, 48 * 9])
        amul = sb("amul", [P, 2 * 72])
        cond = sb("cond", [P, 72])
        rows = sb("rows", [P, T])
        hist = sb("hist", [P, 24 * 24])
        hist_out = sb("hist_out", [P, 24 * 27])
        s5c = sb("s5c", [P, 16 * 34])
        s5p = sb("s5p", [P, 2 * 16 * (Q5 + 1)])
        s5_out = sb("s5_out", [P, 2 * 16 * 9])
        lru_out = sb("lru_out", [P, 4 * 9])
        lruc = sb("lruc", [P, 32])
        wrows = sb("wrows", [P, KD * 16])
        wrouter = sb("wrouter", [P, KD * 16])
        small = sb("small", [P, 400])
        ARENA = 46080
        arena = sb("arena", [P, ARENA])
        psum = ctx.enter_context(nc.psum_tensor("psum", [P, 8 * 512], F32))

        def cut(start, n):
            assert start + n <= ARENA
            return arena[:, start:start + n]

        W = [cut(0, 4096), cut(4096, 4096)]
        AW = [cut(at, 4096) for at in (0, 4096, 8192, 12288, 17408, 31232)]
        HT = cut(8192, KD * T).rearrange("p (k t) -> p k t", k=KD)
        Y = cut(17408, KM * T).rearrange("p (k t) -> p k t", k=KM)
        R0 = 22016
        MRG0 = 36864
        merged = cut(MRG0, KD * T).rearrange("p (k t) -> p k t", k=KD)
        X = cut(R0, KD * T).rearrange("p (k t) -> p k t", k=KD)

        def bank(b, n=512, w=1):
            return psum[:, 512 * b:512 * b + n]

        def pset(s):
            return psum[:, 1536 * s:1536 * (s + 1)].rearrange("p (b c) -> p b c", b=3)[:, :, 0:N3]

        def tri3(ap):
            return ap.rearrange("p (b c) -> p b c", b=3)

        def c_(name, a=0, n=None):
            o, w = CST[name]
            return cst[:, o + a:o + a + (w if n is None else n)]

        def v_(name, a=0, n=1):
            return vec[:, VEC[name][0] + a:VEC[name][0] + a + n]

        ident, ones = c_("ident"), c_("ones")
        mod3 = mod[:, :].rearrange("p (m s) -> p m s", s=9)
        amul3 = amul[:, :].rearrange("p (w m s) -> p w m s", w=2, s=9)

        def seqs(ap):
            return ap[:, NP_TOK:T].rearrange("p (b t) -> p b t", t=SLEN)

        s_const = sem("s_const"); s_x = sem("s_x"); s_xr = sem("s_xr")
        s_w = [sem("s_w%d" % i) for i in range(2)]
        s_fill = [sem("s_fillA"), sem("s_fillB")]
        s_free = [sem("s_freeA"), sem("s_freeB")]
        s_dve = sem("s_dve"); s_act = sem("s_act")
        s_phase = sem("s_phase")
        s_aw = [sem("s_aw%d" % i) for i in range(6)]
        s_cond = sem("s_cond"); s_ada = sem("s_ada"); s_mod = sem("s_mod")
        s_sq = sem("s_sq"); s_sq_used = sem("s_sq_used"); s_root = sem("s_root"); s_h = sem("s_h"); s_recip = sem("s_recip")
        s_cb = sem("s_cb"); s_conv = sem("s_conv")
        r_z = sem("r_z"); r_l = sem("r_l"); r_sg = sem("r_sg")
        s_sig = sem("s_sig"); s_acc = sem("s_acc")
        s_out = sem("s_out"); s_pstate = sem("s_pstate")
        c_bc = sem("c_bc"); c_cols = sem("c_cols"); c_diff = sem("c_diff"); c_exp = sem("c_exp")
        c_gram = sem("c_gram"); c_tok = sem("c_tok"); c_ops = sem("c_ops"); c_lk = sem("c_lk"); c_p = sem("c_p")
        c_ps = sem("c_ps"); c_d = sem("c_d"); c_x = sem("c_x"); c_w = sem("c_w"); c_nw = sem("c_nw"); c_u = sem("c_u")
        c_us = sem("c_us"); c_o = sem("c_o"); c_os = sem("c_os"); c_ut = sem("c_ut"); c_um = sem("c_um")
        c_s = sem("c_s"); c_ss = sem("c_ss")
        d_bc = sem("d_bc"); d_diff = sem("d_diff"); d_exp = sem("d_exp"); d_ops = sem("d_ops"); d_y = sem("d_y")
        d_ys = sem("d_ys"); d_bm = sem("d_bm"); d_s = sem("d_s"); d_ss = sem("d_ss"); d_gated = sem("d_gated")
        l_sp = sem("l_sp"); l_col = sem("l_col"); l_a = sem("l_a"); l_m = sem("l_m"); l_b = sem("l_b"); l_done = sem("l_done")
        a_mag = sem("a_mag"); a_th = sem("a_th"); a_sin = sem("a_sin"); a_u = sem("a_u"); a_wb = sem("a_wb")
        a_wt = sem("a_wt"); a_wc = sem("a_wc"); a_uc = sem("a_uc"); a_v = sem("a_v"); a_ve = sem("a_ve")
        a_ca = sem("a_ca"); a_k = sem("a_k"); a_dd = sem("a_dd"); a_s = sem("a_s"); a_y = sem("a_y")
        a_g = sem("a_g"); a_gs = sem("a_gs"); a_mask = sem("a_mask"); a_fin = sem("a_fin")
        m_r = sem("m_r"); m_sc = sem("m_sc"); m_mask = sem("m_mask"); m_maskt = sem("m_maskt"); m_nblk = sem("m_nblk")
        m_start = sem("m_start"); m_pos = sem("m_pos"); m_post = sem("m_post"); m_posi = sem("m_posi"); m_tab = sem("m_tab")
        m_ht = sem("m_ht"); m_htok = sem("m_htok"); m_hst = [sem("m_hst%d" % i) for i in range(2)]; m_zero = sem("m_zero"); m_idz = sem("m_idz")
        m_scat = sem("m_scat"); m_idl = sem("m_idl"); m_idt = sem("m_idt"); m_idx = sem("m_idx")
        e_w = [sem("e_w%d" % i) for i in range(2)]; e_x = [sem("e_x%d" % i) for i in range(2)]
        e_xt = sem("e_xt"); e_xc = sem("e_xc"); e_g = sem("e_g"); e_u = sem("e_u"); e_sg = sem("e_sg"); e_hid = sem("e_hid")
        e_ht = sem("e_ht"); e_htc = sem("e_htc"); e_d = sem("e_d"); e_ya = sem("e_ya"); e_yd = sem("e_yd")
        e_st = [sem("e_st%d" % i) for i in range(2)]
        f_y = [sem("f_y%d" % i) for i in range(2)]; f_f = sem("f_f"); f_t = sem("f_t"); f_x = sem("f_x")

        class Steps:
            def __init__(self, eng, own):
                self.eng, self.own, self.n = eng, own, {}

            def tell(self, ins, s):
                ins.then_inc(s, 1)
                self.n[s.name] = self.n.get(s.name, 0) + 1

            def then(self, ins, s=None):
                s = self.own if s is None else s
                self.tell(ins, s)
                self.eng.wait_ge(s, self.n[s.name])

        def end_phase(eng, n):
            eng.drain().then_inc(s_phase, 1)
            eng.wait_ge(s_phase, 3 * (n + 1))

        def wait_fill(eng, name, m):
            s, k = FILL[(name, m)]
            eng.wait_ge(s_fill[s], k + 1)
            return s

        def freed(eng, name, m):
            s, k = FILL[(name, m)]
            eng.wait_ge(s_free[s], k + 1)

        def wait_load(eng, a, g):
            s = SLOT[(a, g)]
            eng.wait_ge(s_w[s], 16 * slot_count(a, g))
            return W[s]

        block = ctx.enter_context(nc.Block())

        tmp0 = 35840
        QKV = cut(R0, 12 * T).rearrange("p (m t) -> p m t", m=12)
        cb_g = [cut(tmp0, CW), cut(tmp0 + CW + 1, CW)]
        sq_a = [cut(tmp0, T), cut(tmp0 + T, T)]
        rs_a, rt_a = cut(tmp0 + 2 * T, T), cut(tmp0 + 3 * T, T)
        tq = tmp0 + 2 * (CW + 1)
        sq_g, rs_g, rt_g = [cut(tq, T), cut(tq + T, T)], cut(tq + 2 * T, T), cut(tq + 3 * T, T)
        rowt = [cut(tmp0 + (4 + i) * T, T) for i in range(4)]
        (cDT, cEG, cLT, cAT, cQE, cKE, cKB, cVB, cLK0, cLK1, cPS, cU, cS, cNW) = [
            cut(tmp0 + 512 * i, 512) for i in range(14)]
        cLK = [cLK0, cLK1]
        cXX = cut(tmp0 + 512 * 14, 1024)
        cUM = cut(tmp0 + 512 * 16, 1024)
        gX = [cXX[:, 512 * (h // 2) + P * (h % 2):512 * (h // 2) + P * (h % 2 + 1)] for h in range(GH)]
        gXT = [cXX[:, 512 * (h // 2) + P * (h % 2 + 2):512 * (h // 2) + P * (h % 2 + 3)] for h in range(GH)]
        Rb = R0 + 8 * T
        XBC = cut(R0, 8 * T).rearrange("p (m t) -> p m t", m=8)
        cb_s = [cut(Rb, CW), cut(Rb + CW + 1, CW)]
        sq_s = [cut(Rb, T), cut(Rb + T, T)]
        rs_s, rt_s = cut(Rb + 2 * T, T), cut(Rb + 3 * T, T)
        dDT, dEG = cut(Rb, 1024), cut(Rb + 1024, 1024)
        dXD, dXW = cut(Rb + 2048, 512), cut(Rb + 2560, 512)
        dB, dBM, dH, dTMP = cut(Rb + 3072, 256), cut(Rb + 3328, 256), cut(Rb + 3584, 512), cut(Rb + 4096, 512)
        Rl = R0 + 4 * T
        XF = cut(R0, 4 * T).rearrange("p (m t) -> p m t", m=4)
        cb_l = [cut(Rl, CW), cut(Rl + CW + 1, CW)]
        lt = [cut(Rl + 2400 + i * T, T) for i in range(6)]
        U = XF
        NS = 4 * NQ
        sV = [cut(Rl + i * NS, NS) for i in range(2)]
        sZ = [cut(Rl + (2 + i) * NS, NS) for i in range(2)]
        sCOS, sSIN, sR = cut(Rl + 4 * NS, NS), cut(Rl + 5 * NS, NS), cut(Rl + 6 * NS, NS)
        sT = cut(Rl + 7 * NS, 2 * NS)
        sT2 = [sT[:, 0:NS], sT[:, NS:2 * NS]]
        Rs = Rl + 9 * NS
        CAW = 2 * 4 * (Q5 + 1) * 32
        sCA = [cut(at, CAW).rearrange("p (w q l c) -> p w q l c", w=2, q=4, c=32) for at in (Rs, 17408)]
        sUC = [cut(at, T).rearrange("p (q h n) -> p q h n", q=4, h=2) for at in (Rs + CAW, 17408 + CAW)]
        sDD = cut(Rs + CAW + T, 1024).rearrange("p (q l c) -> p q l c", q=4, c=32)
        sMASK = cut(Rs + CAW + T + 1024, NQ)
        sID4, sDIAG = [cut(Rs + CAW + T + 1024 + NQ + P * i, P)[0:32] for i in range(2)]
        assert Rs + CAW + T + 1024 + NQ + 2 * P <= MRG0
        sB4 = rows[:, 0:1024].rearrange("p (w q r c) -> p w q r c", w=2, q=4, c=32)
        sLAST = [small[:, 256 + 36 * w:292 + 36 * w].rearrange("p (q b) -> p q b", b=9) for w in range(4)]
        st = [cut(Rl + i * T, T) for i in range(4)]
        E0 = 35328
        sq_e = [cut(E0, T), cut(E0 + T, T)]
        rs_e, rt_e = cut(E0 + 2 * T, T), cut(E0 + 3 * T, T)
        res_tmp = cut(31232, P)
        G0 = E0 + 4 * T + P
        scores, rsel, rank, picked, weight, first1, rtmp = [cut(G0 + 144 * i, 144) for i in range(7)]
        grp = cut(G0 + 144 * 7, 36 * 4)
        btab = cut(G0 + 144 * 8, NB * NB)
        cmpA, cmpB = cut(31232, 576), cut(31232 + 576, 576)
        ones_row, mask_row, cum_row = cut(E0, T), cut(E0 + 2 * T, T), cut(E0 + 3 * T, T)
        htok = [cut(17408, D), cut(18432, D)]
        INT = mybir.dt.int32
        w12 = hist[:, 0:18].rearrange("p (k c) -> p k c", k=2)
        posf, posi = hist[:, 20:38], hist[:, 40:58].bitcast(INT)
        idxi = hist[:, 60:60 + NB].bitcast(INT)
        ecol = hist[0:16, 100:110]
        erow = hist[0:1, 120:120 + 8 * NB].rearrange("p (a j) -> p a j", j=NB)
        eint_at = hist[0:1, 540:540 + NB].bitcast(INT).rearrange("p (a j) -> p a j", j=NB)
        eint = hist[0:1, 400:400 + 4 * NB].bitcast(INT).rearrange("p (a j) -> p a j", j=NB)
        islot = cut(G0 + 144 * 8 + NB * NB, BLK)
        WSET = 31232
        wset = cut(0, 12288)
        xg = [cut(12288, D), cut(13312, D)]
        xT = [cut(14336, D), cut(15360, D)]
        esg, ehid, ehT = cut(16384, 512), cut(16896, 512), cut(17408, 512)
        yb = [cut(17920, D), cut(18944, D)]
        yg = [[cut(12288 + 1024 * (2 * i + k), D) for k in range(2)] for i in range(2)]
        ff = [cut(16384, D), cut(17408, D)]
        ftmp = cut(18432, D)
        h_rows = A["h_rows"]
        y_rows = A["y_rows"]
        slot_token = A["slot_token"]
        mg_sig = [cut(R0, T), cut(R0 + T, T)]
        mg_tmp = cut(R0 + 2 * T, T)

        colG, colE, colB = small[:, 0:80], small[:, 96:112], small[:, 112:116]
        colK, colW, colL = small[:, 116:124], small[:, 124:132], small[:, 132:196]
        nexpa = small[0:16, 200:201]

        S5N = ["dt", "mag", "th", "sin", "cos", "den", "fre", "fim", "t0", "t1", "lre", "lim", "c1", "s1"]

        def s5(name, k=0):
            i = (S5N.index(name) if name in S5N else len(S5N) + 2 * k + (name == "pi")) * 16
            return s5c[:, i:i + 16]

        def hd(ap, h):
            return ap.rearrange("p (h t) -> p h t", h=h)

        def over(ap, n):
            return ap.unsqueeze(2).to_broadcast([ap.shape[0], ap.shape[1], n])

        def by(ap, n):
            return ap.unsqueeze(1).to_broadcast([ap.shape[0], n, ap.shape[1]])

        sq_no, sq_reader, root_no = {}, {}, {}
        n_sq = used = 0
        for name, m, terms in ([("ss_mix", 0, KD)] + [("qkn", m, 1) for m in range(8)] +
                               [("gdn_ss", m, 1) for m in range(4)] + [("ssd_ss", 0, KM)] +
                               [("ss_moe", 0, KD), ("ss_final", 0, KD)]):
            root_no[(name, m)] = len(root_no)
            sq_no[(name, m)] = list(range(n_sq, n_sq + terms))
            for i in range(terms):
                if i < terms - 1:
                    used += 1
                    sq_reader[n_sq + i] = (s_sq_used, used)
                else:
                    fs, fk = FILL[(name, m)]
                    sq_reader[n_sq + i] = (s_fill[fs], fk + 1)
            n_sq += terms

        def pe_tile(pe, name, m, w, src, K):
            s, k = FILL[(name, m)]
            if k >= 1:
                pe.wait_ge(s_free[s], k)
            for n in range(3):
                for kk in range(K):
                    last = nc.tensor.matmul(pset(s)[:, n, :], w[:, kk, :], src[:, kk, n * N3:(n + 1) * N3],
                                            start=(kk == 0), stop=(kk == K - 1))
            last.then_inc(s_fill[s], 1)

        def pe_group(pe, name, g, src, K, per):
            w = wait_load(pe, name, g).rearrange("p (m k c) -> p m k c", m=4096 // (K * P), k=K)
            for m in range(per):
                pe_tile(pe, name, per * g + m, w[:, m], src, K)

        def pe_sumsq(pe, name, m, sq):
            s, k = FILL[(name, m)]
            if k >= 1:
                pe.wait_ge(s_free[s], k)
            terms = sq_no[(name, m)]
            for i, q in enumerate(terms):
                pe.wait_ge(s_sq, q + 1)
                for n in range(3):
                    last = nc.tensor.matmul(pset(s)[:, n, :], ones, sq[q % 2][:, n * N3:(n + 1) * N3],
                                            start=(i == 0), stop=(i == len(terms) - 1))
                last.then_inc(s_sq_used if i < len(terms) - 1 else s_fill[s], 1)

        def act_sumsq(act, name, m, sq, srcs):
            for q, src in zip(sq_no[(name, m)], srcs):
                if q >= 2:
                    act.wait_ge(*sq_reader[q - 2])
                nc.scalar.activation(sq[q % 2], src, ACT.Square).then_inc(s_sq, 1)

        def act_root(St, name, m, dst, scale):
            s = wait_fill(St.eng, name, m)
            if root_no[(name, m)] >= 1:
                St.eng.wait_ge(s_recip, root_no[(name, m)])
            nc.scalar.activation(tri3(dst), pset(s), ACT.Sqrt, bias=c_("eps"), scale=scale).then_inc(s_free[s], 1)

        def dve_recip(V, name, m, rs, rt):
            freed(V.eng, name, m)
            V.then(nc.vector.reciprocal(rs, rt), s_recip)

        def dve_norm(V, x, h, aw, sh):
            for k in range(KD):
                V.then(nc.vector.tensor_tensor(h[:, k, :], x[:, k, :], V.rs, ALU.mult))
                nc.vector.tensor_scalar(h[:, k, 0:NP_TOK], h[:, k, 0:NP_TOK], aw[:, k, 0:1], sh[:, k, 0:1],
                                        ALU.mult, ALU.add)
                hs = seqs(h[:, k, :])
                V.then(nc.vector.tensor_tensor(hs, hs, over(aw[:, k, 1:9], SLEN), ALU.mult))
                V.then(nc.vector.tensor_tensor(hs, hs, over(sh[:, k, 1:9], SLEN), ALU.add),
                       s_h if k == KD - 1 else None)

        def cb_seq(c):
            return c[:, 3 + NP_TOK:CW].rearrange("p (b t) -> p b t", t=3 + SLEN)

        def act_conv_in(St, name, m, n, c):
            s = wait_fill(St.eng, name, m)
            if n >= 2:
                St.eng.wait_ge(s_conv, n - 1)
            ps, d = pset(s), c[n % 2]
            nc.scalar.activation(cb_seq(d)[:, :, 0:3], hist[:, 24 * n:24 * (n + 1)].rearrange("p (b t) -> p b t", t=3),
                                 ACT.Copy)
            nc.scalar.activation(d[:, 3:3 + 2 * N3].rearrange("p (b t) -> p b t", b=2), ps[:, 0:2, :], ACT.Copy)
            nc.scalar.activation(d[:, 3 + 2 * N3:3 + NP_TOK], ps[:, 2, 0:NP_TOK - 2 * N3], ACT.Copy)
            St.then(nc.scalar.activation(cb_seq(d)[:, :, 3:3 + SLEN],
                                         ps[:, 2, NP_TOK - 2 * N3:N3].rearrange("p (b t) -> p b t", t=SLEN), ACT.Copy),
                    s_cb)
            St.eng.sem_inc(s_free[s], 1)

        def dve_cb_start(V, c):
            nc.vector.memset(c[0][:, 0:3], 0.0)
            V.then(nc.vector.memset(c[1][:, 0:3], 0.0))

        def dve_conv(V, n, c, dst, wname, wt, ntile, bias=None):
            V.eng.wait_ge(s_cb, n + 1)
            d = c[n % 2]
            ho = hist_out[:, 27 * n:27 * (n + 1)].rearrange("p (b t) -> p b t", t=3)
            nc.vector.tensor_copy(ho[:, 0, :], d[:, NP_TOK:NP_TOK + 3])
            nc.vector.tensor_copy(ho[:, 1:9, :], cb_seq(d)[:, :, SLEN:SLEN + 3])
            ds = seqs(dst)
            for k in range(4):
                a, b, w = d[:, k:k + NP_TOK], cb_seq(d)[:, :, k:k + SLEN], v_(wname, k * ntile + wt)
                if k == 0 and bias is None:
                    nc.vector.tensor_scalar(dst[:, 0:NP_TOK], a, w, None, ALU.mult)
                    V.then(nc.vector.tensor_scalar(ds, b, w, None, ALU.mult))
                elif k == 0:
                    nc.vector.tensor_scalar(dst[:, 0:NP_TOK], a, w, bias, ALU.mult, ALU.add)
                    V.then(nc.vector.tensor_scalar(ds, b, w, bias, ALU.mult, ALU.add))
                else:
                    nc.vector.scalar_tensor_tensor(out=dst[:, 0:NP_TOK], in0=a, scalar=w, in1=dst[:, 0:NP_TOK],
                                                   op0=ALU.mult, op1=ALU.add)
                    V.then(nc.vector.scalar_tensor_tensor(out=ds, in0=b, scalar=w, in1=ds, op0=ALU.mult, op1=ALU.add),
                           s_conv if k == 3 else None)

        MERGES = [1, 3, 2, 0]

        def pe_merge(pe, k):
            g = "gate%d" % k
            for m in range(KD):
                if m % 4 == 0:
                    wg = wait_load(pe, g, m // 4).rearrange("p (m k c) -> p m k c", m=4, k=KD)
                pe_tile(pe, g, m, wg[:, m % 4], HT, KD)
                if m == 0:
                    wb = wait_load(pe, "br%d" % k, 0).rearrange("p (m k c) -> p m k c", m=8, k=KM)
                pe_tile(pe, "br%d" % k, m, wb[:, m], Y, KM)

        def act_merge(act, k):
            at = MERGES.index(k) * KD
            for m in range(KD):
                s = wait_fill(act, "gate%d" % k, m)
                if at + m >= 2:
                    act.wait_ge(s_acc, at + m - 1)
                nc.scalar.activation(tri3(mg_sig[m % 2]), pset(s), ACT.Sigmoid).then_inc(s_free[s], 1)

        def dve_merge(V, k):
            for m in range(KD):
                freed(V.eng, "gate%d" % k, m)
                s = wait_fill(V.eng, "br%d" % k, m)
                dst = merged[:, m, :] if k == MERGES[0] else mg_tmp
                nc.vector.tensor_tensor(tri3(dst), tri3(mg_sig[m % 2]), pset(s), ALU.mult).then_inc(s_free[s], 1)
                freed(V.eng, "br%d" % k, m)
                if k == MERGES[0]:
                    V.eng.sem_inc(s_acc, 1)
                    V.n[s_acc.name] = V.n.get(s_acc.name, 0) + 1
                else:
                    V.then(nc.vector.tensor_tensor(merged[:, m, :], merged[:, m, :], mg_tmp, ALU.add), s_acc)

        def dve_residual(V, name, m, gate, tmp):
            s = wait_fill(V.eng, name, m)
            ps, x = pset(s), X[:, m, :]
            g = mod3[:, gate + m, :]
            xa = x[:, 0:2 * N3].rearrange("p (b t) -> p b t", b=2)
            nc.vector.scalar_tensor_tensor(out=xa, in0=ps[:, 0:2, :], scalar=g[:, 0:1], in1=xa, op0=ALU.mult, op1=ALU.add)
            xb = x[:, 2 * N3:NP_TOK]
            nc.vector.scalar_tensor_tensor(out=xb, in0=ps[:, 2, 0:NP_TOK - 2 * N3], scalar=g[:, 0:1], in1=xb,
                                           op0=ALU.mult, op1=ALU.add)
            t = tmp[:, 0:P].rearrange("p (b t) -> p b t", t=SLEN)
            nc.vector.tensor_tensor(t, ps[:, 2, NP_TOK - 2 * N3:N3].rearrange("p (b t) -> p b t", t=SLEN),
                                    over(g[:, 1:9], SLEN), ALU.mult).then_inc(s_free[s], 1)
            freed(V.eng, name, m)
            V.then(nc.vector.tensor_tensor(seqs(x), seqs(x), t, ALU.add))

        LEV = [7] * 8 + [4]
        LEV0 = [7 * c for c in range(9)]
        NC7 = NT - 1

        def store_block(sp, j):
            sp.wait_ge(e_ya, j + 1)
            sp.wait_ge(e_yd, j + 1)
            sp.dma_start(y_rows[j * BLK:(j + 1) * BLK, :], yb[j % 2]).then_inc(e_st[j % 2], 16)

        @block.sync
        def _(sp):
            for dst, name in ((cst, "cst"), (vec, "vec"), (cond, "cT"), (hist, "hist"), (wrows, "wrows"), (wrouter, "wrouter")):
                sp.dma_start(dst[:, :], A[name]).then_inc(s_const, 16)
            for g, a in enumerate(ADA_SLOT):
                if g == ADA_EARLY:
                    sp.dma_start(X, A["xT"]).then_inc(s_x, 16)
                if a in ADA_SLOT[:g]:
                    sp.wait_ge(s_ada, g - ADA_SLOT[:g][::-1].index(a))
                sp.dma_start(AW[a], A["ada"][g]).then_inc(s_aw[a], 16)
            before = {a: ("ada", g) for g, a in enumerate(ADA_SLOT) if a < 2}
            for a, g, s in LOADS:
                if s in before:
                    pa, pg = before[s]
                    if pa == "ada":
                        sp.wait_ge(s_ada, pg + 1)
                    elif pa == "gdn_state":
                        sp.wait_ge(c_ss, NC7)
                        sp.dma_start(A["gdn_p"], cS).then_inc(s_pstate, 16)
                        sp.wait_ge(c_ss, NC7 + GH)
                        sp.dma_start(A["gdn_s"], W[s]).then_inc(s_pstate, 16)
                        sp.wait_ge(s_pstate, 32)
                    elif pa == "ssd_state":
                        sp.wait_ge(d_ss, NC7)
                        sp.dma_start(A["ssd_p"], dH).then_inc(s_pstate, 16)
                        sp.wait_ge(d_ss, NC7 + NSEQ)
                        sp.dma_start(A["ssd_s"], W[s]).then_inc(s_pstate, 16)
                        sp.wait_ge(s_pstate, 64)
                    elif pa == "lru_w":
                        sp.wait_ge(s_phase, 3 * 10)
                    elif pa == "s5_bc":
                        sp.wait_ge(s_phase, 3 * 12)
                    else:
                        f, k = FILL[last_reader(pa, pg)]
                        sp.wait_ge(s_fill[f], k + 1)
                sp.dma_start(W[s], A[a][g]).then_inc(s_w[s], 16)
                before[s] = (a, g)
                if a == "out" and g == 1:
                    sp.wait_ge(s_phase, 3 * 13)
                    sp.dma_start(X, A["xT"]).then_inc(s_xr, 16)
            sp.wait_ge(m_zero, 1)
            sp.dma_start(slot_token.rearrange("(p j) o -> p (j o)", p=P), cmpB[:, 0:NB]).then_inc(m_idz, 16)
            for c in range(NT):
                sp.wait_ge(m_htok, c + 1)
                sp.dma_start(h_rows[c * P:(c + 1) * P, :], htok[c % 2]).then_inc(m_hst[c % 2], 16)
            sp.wait_ge(m_scat, 16 * 18)
            sp.dma_start(islot[0:NB, :], slot_token.rearrange("(j p) o -> j (p o)", p=BLK)).then_inc(m_idl, 16)
            sp.wait_ge(s_phase, 3 * 15)
            e0 = sp.value_load(eint[:, 0, 0:1], min_val=0, max_val=NE - 1)
            sp.dma_start(wset, A["moe"][bass.ds(e0, 1)].rearrange("a p c -> (a p) c")).then_inc(e_w[1], 16)
            for j in range(NB - 1):
                nxt = sp.value_load(eint[:, 1, j:j + 1], min_val=0, max_val=NE - 1)
                new = sp.value_load(eint[:, 2, j:j + 1], min_val=0, max_val=1)
                other = sp.value_load(eint[:, 3, j:j + 1], min_val=0, max_val=WSET)
                if j:
                    sp.wait_ge(e_d, j)
                sp.dma_start(arena[:, bass.ds(other, 12288)], A["moe"][bass.ds(nxt, 1)].rearrange("a p c -> (a p) c"),
                             cond=(new > 0)).then_inc(e_w[j % 2], 16)
                if j:
                    store_block(sp, j - 1)
            store_block(sp, NB - 2)
            store_block(sp, NB - 1)
            sp.wait_ge(s_phase, 3 * 18)
            sp.dma_start(A["yT"], HT).then_inc(s_out, 16)
            for name, t in (("hist_out", hist_out), ("s5_out", s5_out), ("lru_out", lru_out)):
                sp.dma_start(A[name], t[:, :]).then_inc(s_out, 16)
            sp.wait_ge(s_out, 16 * 4)

        @block.tensor
        def _(pe):
            pe.wait_ge(s_const, 16 * 6)
            pe.wait_ge(s_cond, 1)
            for g, a in enumerate(ADA_SLOT):
                if g == ADA_EARLY:
                    pe_sumsq(pe, "ss_mix", 0, sq_a)
                pe.wait_ge(s_aw[a], 16 * ADA_SLOT[:g + 1].count(a))
                w = AW[a].rearrange("p (m k c) -> p m k c", m=4, k=KD)
                for m in range(4 * g, 4 * g + 4):
                    for k in range(KD):
                        last = nc.tensor.matmul(bank(6 if g < ADA_EARLY else 7)[:, 9 * m:9 * m + 9], w[:, m % 4, k, :],
                                                cond[:, 9 * k:9 * k + 9], start=(k == 0), stop=(k == KD - 1))
                last.then_inc(s_ada, 1)
            pe.wait_ge(s_h, 1)
            s, k = FILL[("rows", 0)]
            pe.wait_ge(s_free[s], k) if k else None
            wr = wrows[:, :].rearrange("p (k c) -> p k c", k=KD)
            for n in range(3):
                for kk in range(KD):
                    last = nc.tensor.matmul(pset(s)[0:16, n, :], wr[:, kk, :], HT[:, kk, n * N3:(n + 1) * N3],
                                            start=(kk == 0), stop=(kk == KD - 1))
            last.then_inc(s_fill[s], 1)
            end_phase(pe, 0)
            for m in range(12):
                w = wait_load(pe, "qkv", m // 4).rearrange("p (m k c) -> p m k c", m=4, k=KD)
                pe_tile(pe, "qkv", m, w[:, m % 4], HT, KD)
                if 2 <= m < 10:
                    pe_sumsq(pe, "qkn", m - 2, sq_g)
            end_phase(pe, 1)

            def sel(r):
                return ident[0:80, r:r + 1].to_broadcast([80, P])

            for c in range(NT):
                t0 = c * P
                sample = c == NC7
                ck = lambda m: QKV[:, m, t0:t0 + P]
                hs = [slice(h * P, (h + 1) * P) for h in range(GH)]
                if c:
                    pe.wait_ge(c_ss, c)
                    pe.wait_ge(c_os, c)
                for h in range(GH):
                    nc.tensor.matmul(bank(0)[:, hs[h]], sel(h), rows[0:80, t0:t0 + P], start=True, stop=True)
                for h in range(GH):
                    nc.tensor.matmul(bank(1)[:, hs[h]], sel(76 + h), rows[0:80, t0:t0 + P], start=True, stop=True)
                nc.tensor.transpose(bank(2)[:, 0:80], rows[0:80, t0:t0 + P], ident[0:80, 0:80]).then_inc(c_bc, 1)
                for h in range(GH):
                    nc.tensor.matmul(bank(3)[:, hs[h]], ck(4 + h), ck(4 + h), start=True, stop=True)
                for h in range(GH):
                    last = nc.tensor.matmul(bank(4)[:, hs[h]], ck(4 + h), ck(h), start=True, stop=True)
                last.then_inc(c_gram, 1)
                for h in range(GH):
                    nc.tensor.transpose(bank(5)[:, hs[h]], ck(4 + h), ident)
                for h in range(GH):
                    last = nc.tensor.transpose(bank(6)[:, hs[h]], ck(8 + h), ident)
                last.then_inc(c_tok, 1)
                pe.wait_ge(c_ops, c + 1)
                for lv in range(LEV[c]):
                    n = LEV0[c] + lv
                    pe.wait_ge(c_lk, n + 1)
                    for f in range(2):
                        if lv:
                            pe.wait_ge(c_x, 2 * n - 1 + f)
                        for e in range(2):
                            h = 2 * f + e
                            last = nc.tensor.matmul(bank(7 * f)[:, hs[e]], cLK[lv % 2][:, hs[h]], gX[h],
                                                    start=True, stop=True)
                        last.then_inc(c_p, 1)
                    for f in range(2):
                        pe.wait_ge(c_ps, 2 * n + 1 + f)
                        for e in range(2):
                            h = 2 * f + e
                            nc.tensor.matmul(bank(1 + f)[:, hs[e]], gXT[h], cPS[:, hs[h]], start=True, stop=True)
                            last = nc.tensor.matmul(bank(1 + f)[:, hs[2 + e]], cPS[:, hs[h]], gXT[h],
                                                    start=True, stop=True)
                        last.then_inc(c_d, 1)
                pe.wait_ge(c_x, 2 * (LEV0[c] + LEV[c]))
                for h in range(GH):
                    last = nc.tensor.matmul(bank(3)[:, hs[h]], cKB[:, hs[h]], gXT[h], start=True, stop=True)
                last.then_inc(c_w, 1)
                pe.wait_ge(c_nw, c + 1)
                if not sample:
                    for h, a in enumerate(hs):
                        nc.tensor.matmul(bank(4)[:, a], gXT[h], cVB[:, a], start=True, stop=False)
                        last = nc.tensor.matmul(bank(4)[:, a], cNW[:, a], cS[:, a], start=False, stop=True)
                    last.then_inc(c_u, 1)
                    pe.wait_ge(c_us, c + 1)
                    for a in hs:
                        nc.tensor.matmul(bank(5)[:, a], cS[:, a], cQE[:, a], start=True, stop=False)
                        last = nc.tensor.matmul(bank(5)[:, a], cU[:, a], cAT[:, a], start=False, stop=True)
                    last.then_inc(c_o, 1)
                    for a in hs:
                        last = nc.tensor.matmul(bank(6)[:, a], cKE[:, a], cU[:, a], start=True, stop=True)
                    last.then_inc(c_s, 1)
                else:
                    S0 = wait_load(pe, "gdn_state", 0).rearrange("p (b h v) -> p b h v", b=NSEQ, h=GH)
                    for h in range(GH):
                        nc.tensor.matmul(bank(4)[:, hs[h]], cVB[:, hs[h]], gXT[h], start=True, stop=False)
                        for b in range(NSEQ):
                            a = slice(h * P + SLEN * b, h * P + SLEN * (b + 1))
                            last = nc.tensor.matmul(bank(4)[:, a], S0[:, b, h, :], cNW[:, a],
                                                    start=False, stop=(b == NSEQ - 1))
                    last.then_inc(c_u, 1)
                    pe.wait_ge(c_ut, 1)
                    for a in hs:
                        last = nc.tensor.transpose(bank(7)[:, a], cPS[:, a], ident)
                    last.then_inc(c_u, 1)
                    pe.wait_ge(c_us, c + 1)
                    for h in range(GH):
                        nc.tensor.matmul(bank(5)[:, hs[h]], cU[:, hs[h]], cAT[:, hs[h]], start=True, stop=False)
                        for b in range(NSEQ):
                            a = slice(h * P + SLEN * b, h * P + SLEN * (b + 1))
                            last = nc.tensor.matmul(bank(5)[:, a], S0[:, b, h, :], cQE[:, a],
                                                    start=False, stop=(b == NSEQ - 1))
                    last.then_inc(c_o, 1)
                    for h in range(GH):
                        pe.wait_ge(c_um, h + 1)
                        for j in range(2):
                            last = nc.tensor.matmul(bank(j), cKE[:, hs[h]], cUM[:, 512 * j:512 * (j + 1)],
                                                    start=True, stop=True)
                        last.then_inc(c_s, 1)
            end_phase(pe, 2)
            wz = wait_load(pe, "zb", 0).rearrange("p (m k c) -> p m k c", m=4, k=KD)
            for m in range(3):
                pe_sumsq(pe, "gdn_ss", m, sq_a)
                pe_tile(pe, "zb", m, wz[:, m], HT, KD)
            pe_tile(pe, "zb", 3, wz[:, 3], HT, KD)
            pe_sumsq(pe, "gdn_ss", 3, sq_a)
            end_phase(pe, 3)
            pe_merge(pe, 1)
            end_phase(pe, 4)
            for g in range(2):
                pe_group(pe, "xbc", g, HT, KD, 4)
            pe_group(pe, "zd", 0, HT, KD, 4)
            end_phase(pe, 5)
            for c in range(NT):
                t0 = c * P
                sample = c == NC7
                xk = lambda m: XBC[:, m, t0:t0 + P]
                if c:
                    pe.wait_ge(d_ss, c)
                    pe.wait_ge(d_ys, c)
                for h in range(SH):
                    nc.tensor.matmul(bank(h // 4)[:, (h % 4) * P:(h % 4 + 1) * P], sel(4 + h), rows[0:80, t0:t0 + P],
                                     start=True, stop=True)
                nc.tensor.transpose(bank(2)[:, 0:80], rows[0:80, t0:t0 + P], ident[0:80, 0:80])
                for g in range(2):
                    nc.tensor.matmul(bank(3)[:, g * P:(g + 1) * P], xk(4 + g), xk(6 + g), start=True, stop=True)
                for g in range(2):
                    nc.tensor.transpose(bank(4)[:, g * P:(g + 1) * P], xk(4 + g), ident)
                for m in range(KM):
                    last = nc.tensor.transpose(bank(5)[:, m * P:(m + 1) * P], xk(m), ident)
                last.then_inc(d_bc, 1)
                pe.wait_ge(d_ops, c + 1)
                if sample:
                    H0 = wait_load(pe, "ssd_state", 0).rearrange("p (b h d) -> p b h d", b=NSEQ, h=SH)
                for h in range(SH):
                    q0, o0 = 64 * (h % 2), 6 * 512 + (h // 2) * P
                    y = psum[q0:q0 + 64, o0:o0 + P]
                    nc.tensor.matmul(y, dXD[:, 64 * h:64 * h + 64], dDT[:, h * P:(h + 1) * P], start=True, stop=False)
                    if not sample:
                        last = nc.tensor.matmul(y, dH[:, 64 * h:64 * h + 64], dEG[:, h * P:(h + 1) * P],
                                                start=False, stop=True)
                    else:
                        for b in range(NSEQ):
                            last = nc.tensor.matmul(psum[q0:q0 + 64, o0 + SLEN * b:o0 + SLEN * (b + 1)], H0[:, b, h, :],
                                                    dEG[:, h * P + SLEN * b:h * P + SLEN * (b + 1)],
                                                    start=False, stop=(b == NSEQ - 1))
                last.then_inc(d_y, 1)
                for b in range(NSEQ if sample else 1):
                    if sample:
                        pe.wait_ge(d_bm, b + 1)
                    bt = dBM if sample else dB
                    for g in range(2):
                        last = nc.tensor.matmul(bank(7)[:, 256 * g:256 * (g + 1)], bt[:, g * P:(g + 1) * P],
                                                dXW[:, 256 * g:256 * (g + 1)], start=True, stop=True)
                    last.then_inc(d_s, 1)
            end_phase(pe, 6)
            pe_sumsq(pe, "ssd_ss", 0, sq_s)
            end_phase(pe, 7)
            pe_merge(pe, 3)
            end_phase(pe, 8)
            pe_group(pe, "xc", 0, HT, KD, 4)
            pe_group(pe, "gc", 0, HT, KD, 4)
            wl = wait_load(pe, "lru_w", 0)[:, 0:1024].rearrange("p (w m c) -> p w m c", w=2, m=4)
            for m in range(4):
                pe.wait_ge(s_conv, 20 + m + 1)
                for w, name in ((0, "lru_r"), (1, "lru_i")):
                    s, k = FILL[(name, m)]
                    pe.wait_ge(s_free[s], k)
                    for n in range(3):
                        last = nc.tensor.matmul(pset(s)[:, n, :], wl[:, w, m, :], XF[:, m, n * N3:(n + 1) * N3],
                                                start=True, stop=True)
                    last.then_inc(s_fill[s], 1)
            end_phase(pe, 9)
            pe_merge(pe, 2)
            end_phase(pe, 10)
            pe_group(pe, "ua", 0, HT, KD, 4)
            bc = wait_load(pe, "s5_bc", 0)
            pe.wait_ge(a_u, 4)
            wb = bc[:, 2048:4096]
            for i in range(4):
                pe.wait_ge(a_wb, i + 1)
                if i:
                    pe.wait_ge(a_ve, i)
                for k in range(16):
                    last = nc.tensor.transpose(psum[:, 1024 + k * P:1024 + (k + 1) * P], wb[:, k * P:(k + 1) * P], ident)
                last.then_inc(a_wt, 1)
                pe.wait_ge(a_wc, i + 1)
                pe.wait_ge(a_uc, i + 1)
                for w in range(2):
                    for q in range(4):
                        dst = bank(2 + 2 * w + q // 2)[:, NQ * (q % 2):NQ * (q % 2 + 1)]
                        for h in range(2):
                            o = 1024 * w + 256 * q + 128 * h
                            last = nc.tensor.matmul(dst, wb[:, o:o + P], sUC[i % 2][:, q, h, :],
                                                    start=(h == 0), stop=(h == 1))
                last.then_inc(a_v, 1)
                pe.wait_ge(a_ca, i + 1)
                if i:
                    pe.wait_ge(a_dd, i)
                for q in range(4):
                    dst = psum[:, 256 * q:256 * (q + 1)]
                    for w in range(2):
                        nc.tensor.matmul(dst, sB4[:, w, q, :, :],
                                         sCA[i % 2][:, w, q, 0:Q5, :], start=(w == 0), stop=False)
                    last = nc.tensor.matmul(dst[:, 0:32], sID4, sDIAG[:, 32 * q:32 * q + 32], start=False, stop=True)
                last.then_inc(a_k, 1)
                pe.wait_ge(a_dd, i + 1)
                pe.wait_ge(a_s, i + 1)
                for q in range(4):
                    j = 4 * i + q
                    if j >= 2:
                        pe.wait_ge(a_g, j - 1)
                    for h in range(2):
                        dst = bank(6 + j % 2)[:, NQ * h:NQ * (h + 1)]
                        for w in range(2):
                            nc.tensor.matmul(dst, sCA[i % 2][:, w, q, 4 * h + 1:4 * h + 5, :],
                                             sV[w][:, NQ * q:NQ * (q + 1)], start=(w == 0), stop=False)
                        last = nc.tensor.matmul(dst, sDD[:, q, 4 * h:4 * h + 4, :], sUC[i % 2][:, q, 1, :],
                                                start=False, stop=(h == 0))
                    last = nc.tensor.matmul(dst, sDD[:, q, 0:4, :], sUC[i % 2][:, q, 0, :], start=False, stop=True)
                    last.then_inc(a_y, 1)
            wg = wait_load(pe, "glu", 0).rearrange("p (m k c) -> p m k c", m=8, k=KM)
            pe.wait_ge(a_g, 16)
            for m in range(4):
                pe_tile(pe, "glu", m, wg[:, m], U, KM)
            end_phase(pe, 11)
            pe_merge(pe, 0)
            end_phase(pe, 12)
            pe_group(pe, "out", 0, merged, KD, 4)
            pe_group(pe, "out", 1, merged, KD, 4)
            end_phase(pe, 13)
            pe_sumsq(pe, "ss_moe", 0, sq_e)
            pe.wait_ge(s_h, 2)
            wr = wrouter[:, :].rearrange("p (k c) -> p k c", k=KD)
            for c in range(NT):
                for k in range(KD):
                    last = nc.tensor.matmul(bank(7)[:, 16 * c:16 * c + 16], HT[:, k, c * P:(c + 1) * P], wr[:, k, :],
                                            start=(k == 0), stop=(k == KD - 1))
            last.then_inc(m_r, 1)
            for c in range(NT):
                if c >= 2:
                    pe.wait_ge(m_htok, c - 1)
                for k in range(KD):
                    last = nc.tensor.transpose(bank(2 * (c % 2) + k // 4)[:, P * (k % 4):P * (k % 4 + 1)],
                                               HT[:, k, c * P:(c + 1) * P], ident)
                last.then_inc(m_ht, 1)
            pe.wait_ge(m_mask, 1)
            for c in range(NT):
                last = nc.tensor.transpose(psum[0:16, 2048 + P * c:2048 + P * (c + 1)], picked[:, 16 * c:16 * c + 16], ident)
            last.then_inc(m_maskt, 1)
            pe.wait_ge(m_nblk, 1)
            nc.tensor.matmul(bank(7)[0:16, 200:201], c_("before")[0:16], ecol[:, 1:2], start=True, stop=True).then_inc(m_start, 1)
            pe.wait_ge(m_pos, 1)
            for c in range(NT):
                nc.tensor.transpose(bank(7)[:, 16 * c:16 * c + 16], cum_row[0:16, c * P:(c + 1) * P], ident[0:16, 0:16])
            nc.tensor.matmul(bank(7)[0:1, 256:256 + NB], ones[0:16, 0:1], cmpB[0:16, 0:NB],
                             start=True, stop=True).then_inc(m_post, 1)
            pe.wait_ge(m_idl, 16)
            nc.tensor.transpose(bank(4)[:, 0:NB], islot[0:NB, :], ident[0:NB, 0:NB]).then_inc(m_idt, 1)
            end_phase(pe, 14)
            def turn_block(j):
                pe.wait_ge(e_x[j % 2], 16 * (j // 2 + 1))
                if j:
                    pe.wait_ge(e_xc, j)
                for k in range(KD):
                    last = nc.tensor.transpose(bank(2 + k // 4)[:, P * (k % 4):P * (k % 4 + 1)],
                                               xg[j % 2][:, k * P:(k + 1) * P], ident)
                last.then_inc(e_xt, 1)

            turn_block(0)
            for j in range(NB):
                at = pe.value_load(eint_at[:, 0, j:j + 1], min_val=0, max_val=WSET)
                pe.wait_ge(e_w[(j + 1) % 2], 16 * ((j + 1) // 2 + (1 if j % 2 == 0 else 0)))
                if j >= 1:
                    pass
                pe.wait_ge(e_xc, j + 1)
                x = xT[j % 2]
                if j:
                    pe.wait_ge(e_hid, j)
                for w, s in ((0, e_g), (1, e_u)):
                    for k in range(KD):
                        last = nc.tensor.matmul(bank(w), x[:, k * P:(k + 1) * P],
                                                arena[:, bass.ds(at + (4096 * w + 512 * k), 512)],
                                                start=(k == 0), stop=(k == KD - 1))
                    last.then_inc(s, 1)
                if j + 1 < NB:
                    turn_block(j + 1)
                pe.wait_ge(e_hid, j + 1)
                for k in range(4):
                    last = nc.tensor.transpose(bank(4)[:, k * P:(k + 1) * P], ehid[:, k * P:(k + 1) * P], ident)
                last.then_inc(e_ht, 1)
                pe.wait_ge(e_htc, j + 1)
                if j:
                    pe.wait_ge(e_ya, j)
                    pe.wait_ge(e_yd, j)
                for n in range(2):
                    for k in range(4):
                        last = nc.tensor.matmul(bank(6 + n), ehT[:, k * P:(k + 1) * P],
                                                arena[:, bass.ds(at + (8192 + 1024 * k + 512 * n), 512)],
                                                start=(k == 0), stop=(k == 3))
                last.then_inc(e_d, 1)
            end_phase(pe, 15)
            for c in range(NT):
                pe.wait_ge(f_f, c + 1)
                if c >= 2:
                    pe.wait_ge(f_x, c - 1)
                for k in range(KD):
                    last = nc.tensor.transpose(bank(2 * (c % 2) + k // 4)[:, P * (k % 4):P * (k % 4 + 1)],
                                               ff[c % 2][:, k * P:(k + 1) * P], ident)
                last.then_inc(f_t, 1)
            end_phase(pe, 16)
            pe_sumsq(pe, "ss_final", 0, sq_e)
            end_phase(pe, 17)

        @block.scalar
        def _(act):
            S = Steps(act, s_act)
            act.wait_ge(s_const, 16 * 6)
            S.then(nc.scalar.activation(cond[:, :], cond[:, :], ACT.Silu), s_cond)
            act.wait_ge(s_x, 16)
            act_sumsq(act, "ss_mix", 0, sq_a, [X[:, k, :] for k in range(KD)])
            act_root(S, "ss_mix", 0, rt_a, 1.0 / D)
            S.then(nc.scalar.activation(nexpa, v_("alog")[0:16], ACT.Exp))
            act.wait_ge(r_z, 1)
            S.then(nc.scalar.activation(rowt[1][0:16], rowt[0][0:16], ACT.Abs))
            S.then(nc.scalar.activation(rowt[1][0:16], rowt[1][0:16], ACT.Exp, scale=-1.0))
            S.then(nc.scalar.activation(rowt[1][0:16], rowt[1][0:16], ACT.Ln, bias=ones[0:16, 0:1]), r_l)
            S.then(nc.scalar.activation(rows[64:80, :], rowt[0][0:16], ACT.Sigmoid))
            end_phase(act, 0)
            for m in range(13):
                if m < 12:
                    act_conv_in(S, "qkv", m, m, cb_g)
                if 2 <= m < 10:
                    act_root(S, "qkn", m - 2, rt_g, 1.0)
                if m:
                    act.wait_ge(s_conv, m)
                    S.then(nc.scalar.activation(QKV[:, m - 1, :], QKV[:, m - 1, :], ACT.Silu))
                    if m <= 8:
                        act_sumsq(act, "qkn", m - 1, sq_g, [QKV[:, m - 1, :]])
            end_phase(act, 1)
            for c in range(NT):
                sample = c == NC7
                act.wait_ge(c_cols, c + 1)
                nc.scalar.activation(colE, colG[:, 0:16], ACT.Exp)
                act.wait_ge(c_diff, c + 1)
                nc.scalar.activation(cEG, bank(0), ACT.Exp)
                nc.scalar.activation(cDT, cDT, ACT.Exp).then_inc(c_exp, 1)
                for n in range(2 * LEV0[c], 2 * (LEV0[c] + LEV[c])):
                    f = n % 2
                    act.wait_ge(c_p, n + 1)
                    nc.scalar.activation(cPS[:, 256 * f:256 * (f + 1)], bank(7 * f)[:, 0:256], ACT.Copy).then_inc(c_ps, 1)
                act.wait_ge(c_u, c + (2 if sample else 1))
                nc.scalar.activation(cU, bank(7 if sample else 4), ACT.Copy).then_inc(c_us, 1)
            end_phase(act, 2)
            def act_z(m):
                s = wait_fill(act, "zb", m)
                nc.scalar.activation(tri3(Y[:, m, :]), pset(s), ACT.Silu).then_inc(s_free[s], 1)

            act_sumsq(act, "gdn_ss", 0, sq_a, [QKV[:, 0, :]])
            for m in range(GH):
                act_root(S, "gdn_ss", m, rt_a, 1.0 / P)
                if m < 3:
                    act_sumsq(act, "gdn_ss", m + 1, sq_a, [QKV[:, m + 1, :]])
                    act_z(m)
                if m == 2:
                    act_z(3)
            end_phase(act, 3)
            act_merge(act, 1)
            end_phase(act, 4)
            for m in range(8):
                act_conv_in(S, "xbc", m, 12 + m, cb_s)
                if m:
                    act.wait_ge(s_conv, 12 + m)
                    nc.scalar.activation(XBC[:, m - 1, :], XBC[:, m - 1, :], ACT.Silu)
            act.wait_ge(s_conv, 20)
            nc.scalar.activation(XBC[:, 7, :], XBC[:, 7, :], ACT.Silu)
            for m in range(KM):
                s = wait_fill(act, "zd", m)
                nc.scalar.activation(tri3(Y[:, m, :]), pset(s), ACT.Silu).then_inc(s_free[s], 1)
            end_phase(act, 5)
            for c in range(NT):
                act.wait_ge(d_diff, c + 1)
                nc.scalar.activation(dDT, dDT, ACT.Exp)
                nc.scalar.activation(dEG, psum[:, 0:1024], ACT.Exp).then_inc(d_exp, 1)
            act.wait_ge(s_pstate, 16 * 4)
            end_phase(act, 6)
            act.wait_ge(d_gated, KM)
            act_sumsq(act, "ssd_ss", 0, sq_s, [XBC[:, m, :] for m in range(KM)])
            act_root(S, "ssd_ss", 0, rt_s, 1.0 / MIX)
            end_phase(act, 7)
            act_merge(act, 3)
            end_phase(act, 8)
            lam = v_("lru_lambda", 0, 4)
            S.then(nc.scalar.activation(lruc[:, 8:12], lam, ACT.Abs))
            S.then(nc.scalar.activation(lruc[:, 8:12], lruc[:, 8:12], ACT.Exp, scale=-1.0))
            S.then(nc.scalar.activation(lruc[:, 8:12], lruc[:, 8:12], ACT.Ln, bias=ones[:, 0:1]), l_sp)
            for m in range(4):
                act_conv_in(S, "xc", m, 20 + m, cb_l)
            for m in range(4):
                s = wait_fill(act, "gc", m)
                nc.scalar.activation(tri3(Y[:, m, :]), pset(s), ACT.Gelu_apprx_tanh).then_inc(s_free[s], 1)
            act.wait_ge(l_col, 1)
            for m in range(4):
                s = wait_fill(act, "lru_r", m)
                if m:
                    act.wait_ge(l_done, m)
                nc.scalar.activation(tri3(lt[0]), pset(s), ACT.Sigmoid, bias=v_("lru_b_a", m)).then_inc(s_free[s], 1)
                freed(act, "lru_r", m)
                s = wait_fill(act, "lru_i", m)
                nc.scalar.activation(tri3(lt[1]), pset(s), ACT.Sigmoid, bias=v_("lru_b_x", m)).then_inc(s_free[s], 1)
                nc.scalar.activation(lt[2], lt[0], ACT.Exp, scale=lruc[:, 4 + m:5 + m])
                nc.scalar.activation(lt[3], lt[0], ACT.Tanh, scale=lruc[:, m:m + 1]).then_inc(l_a, 1)
                act.wait_ge(l_m, m + 1)
                nc.scalar.activation(lt[4], lt[4], ACT.Sqrt).then_inc(l_b, 1)
            end_phase(act, 9)
            act_merge(act, 2)
            end_phase(act, 10)
            S.then(nc.scalar.activation(s5("dt"), v_("s5_dt", 0, 16), ACT.Exp), a_mag)
            act.wait_ge(a_th, 1)
            nc.scalar.activation(s5("mag"), s5("mag"), ACT.Exp)
            nc.scalar.activation(s5("sin"), s5("sin"), ACT.Sin)
            nc.scalar.activation(s5("cos"), s5("cos"), ACT.Sin).then_inc(a_sin, 1)
            for m in range(4):
                s = wait_fill(act, "ua", m)
                nc.scalar.activation(tri3(U[:, m, :]), pset(s), ACT.Copy).then_inc(s_free[s], 1)
                freed(act, "ua", m)
                act.sem_inc(a_u, 1)

            def act_chunks(i):
                if i >= 2:
                    act.wait_ge(a_y, 4 * (i - 1))
                u = U[:, i, :].rearrange("p (n k) -> p k n", k=Q5)
                for q in range(4):
                    for k in range(4):
                        last = None
                        for h in range(2):
                            last = nc.scalar.activation(sUC[i % 2][32 * k:32 * k + 32, q, h, :],
                                                        u[32 * q:32 * q + 32, Q5 - 1 - 4 * h - k, :], ACT.Copy)
                last.then_inc(a_uc, 1)

            act_chunks(0)
            act.wait_ge(a_mask, 1)
            for i in range(4):
                act.wait_ge(a_wt, i + 1)
                wb = wait_load(act, "s5_bc", 0)[:, 2048:4096]
                nc.scalar.activation(wb[:, 0:1024], psum[:, 1024:2048], ACT.Copy)
                nc.scalar.activation(wb[:, 1024:2048], psum[:, 2048:3072], ACT.Copy).then_inc(a_wc, 1)
                if i < 3:
                    act_chunks(i + 1)
                act.wait_ge(a_v, i + 1)
                for w, x0 in ((0, "s5_x0r"), (1, "s5_x0i")):
                    v = sV[w].rearrange("p (b q n) -> p b q n", b=2, q=2)
                    ps = psum[:, 1024 * (w + 1):1024 * (w + 2)].rearrange("p (b c) -> p b c", b=2)[:, :, 0:2 * NQ]
                    ps = ps.rearrange("p b (q n) -> p b q n", q=2)
                    for b in range(2):
                        nc.scalar.activation(v[:, b, :, 1:NQP], ps[:, b, :, 0:NQP - 1], ACT.Copy)
                        nc.scalar.activation(v[:, b, :, NQP + 1:NQ:2], ps[:, b, :, NQP:NQ:2], ACT.Copy)
                        nc.scalar.activation(sLAST[w][:, 2 * b:2 * b + 2, :], ps[:, b, :, NQP - 1:NQ:2], ACT.Copy)
                    v = hd(sV[w], 4)
                    nc.scalar.activation(v[:, :, 0:1], sMASK[:, 0:1].unsqueeze(1).to_broadcast([P, 4, 1]), ACT.Copy)
                    last = nc.scalar.activation(v[:, :, NQP:NQ:2], v_(x0, 32 * i, 32).rearrange("p (q b) -> p q b", b=8),
                                                ACT.Copy)
                last.then_inc(a_ve, 1)
                act.wait_ge(a_k, i + 1)
                for k in range(4):
                    r = slice(32 * k, 32 * k + 32)
                    last = nc.scalar.activation(sDD[r, :, 3 - k:Q5, :],
                                                psum[r, 0:1024].rearrange("p (q l c) -> p q l c", q=4, c=32)[:, :, 0:5 + k, :],
                                                ACT.Copy)
                last.then_inc(a_dd, 1)
                for q in range(4):
                    j = 4 * i + q
                    act.wait_ge(a_y, j + 1)
                    u = U[:, i, :].rearrange("p (n k) -> p k n", k=Q5)
                    for k in range(4):
                        last = nc.scalar.activation(u[32 * q:32 * q + 32, k:Q5:4, :],
                                                    hd(bank(6 + j % 2)[32 * k:32 * k + 32, 0:2 * NQ], 2),
                                                    ACT.Gelu_apprx_tanh)
                    last.then_inc(a_g, 1)
            act.wait_ge(a_fin, 4)
            for m in range(4):
                s = wait_fill(act, "glu", m)
                nc.scalar.activation(tri3(st[m]), pset(s), ACT.Sigmoid).then_inc(s_free[s], 1)
            end_phase(act, 11)
            act_merge(act, 0)
            end_phase(act, 12)
            end_phase(act, 13)
            act_sumsq(act, "ss_moe", 0, sq_e, [X[:, k, :] for k in range(KD)])
            act_root(S, "ss_moe", 0, rt_e, 1.0 / D)
            act.wait_ge(m_r, 1)
            nc.scalar.activation(scores, bank(7)[:, 0:144], ACT.Sigmoid).then_inc(m_sc, 1)
            for c in range(NT):
                act.wait_ge(m_ht, c + 1)
                if c >= 2:
                    act.wait_ge(m_hst[c % 2], 16 * (c // 2))
                nc.scalar.activation(htok[c % 2], psum[:, 1024 * (c % 2):1024 * (c % 2 + 1)], ACT.Copy).then_inc(m_htok, 1)
            act.wait_ge(m_hst[0], 16 * 5)
            act.wait_ge(m_hst[1], 16 * 4)
            end_phase(act, 14)
            def act_turned(j):
                act.wait_ge(e_xt, j + 1)
                if j >= 2:
                    act.wait_ge(e_u, j - 1)
                nc.scalar.activation(xT[j % 2], psum[:, 1024:2048], ACT.Copy).then_inc(e_xc, 1)
            act_turned(0)
            for j in range(NB):
                act.wait_ge(e_g, j + 1)
                if j:
                    act.wait_ge(e_hid, j)
                nc.scalar.activation(esg, bank(0), ACT.Silu).then_inc(e_sg, 1)
                if j + 1 < NB:
                    act_turned(j + 1)
                act.wait_ge(e_d, j + 1)
                if j >= 2:
                    act.wait_ge(e_st[j % 2], 16 * (j // 2))
                nc.scalar.activation(yb[j % 2][:, 0:512], bank(6), ACT.Copy).then_inc(e_ya, 1)
            for i in range(2):
                act.wait_ge(e_st[i], 16 * (NB // 2))
            end_phase(act, 15)
            end_phase(act, 16)
            act_sumsq(act, "ss_final", 0, sq_e, [X[:, k, :] for k in range(KD)])
            act_root(S, "ss_final", 0, rt_e, 1.0 / D)
            end_phase(act, 17)

        @block.gpsimd
        def _(pool):
            pool.wait_ge(s_const, 16 * 6)
            pool.wait_ge(m_idz, 16)
            pool.wait_ge(m_posi, 1)
            for k in range(2):
                for c in range(NT):
                    pool.indirect_dma_start(out=slot_token, out_offset=bass.IndirectOffsetOnAxis(
                        ap=posi[:, NT * k + c:NT * k + c + 1], axis=0),
                        in_=c_("token", c, 1), in_offset=None).then_inc(m_scat, 16)
            pool.wait_ge(s_phase, 3 * 15)
            for j in range(NB):
                if j >= 2:
                    pool.wait_ge(e_xt, j - 1)
                pool.indirect_dma_start(out=xg[j % 2], out_offset=None, in_=h_rows, in_offset=bass.IndirectOffsetOnAxis(
                    ap=idxi[:, j:j + 1], axis=0)).then_inc(e_x[j % 2], 16)
            pool.wait_ge(s_phase, 3 * 16)
            for c in range(NT):
                if c >= 2:
                    pool.wait_ge(f_f, c - 1)
                for k in range(2):
                    pool.indirect_dma_start(out=yg[c % 2][k], out_offset=None, in_=y_rows,
                                            in_offset=bass.IndirectOffsetOnAxis(
                                                ap=posi[:, NT * k + c:NT * k + c + 1], axis=0)).then_inc(f_y[c % 2], 16)

        @block.vector
        def _(dve):
            V = Steps(dve, s_dve)
            tt, ts, stt = nc.vector.tensor_tensor, nc.vector.tensor_scalar, nc.vector.scalar_tensor_tensor

            dve.wait_ge(s_const, 16 * 6)
            def dve_mod(b, m0, m1, w, scale, nw):
                V.then(tt(mod3[:, m0:m1], bank(b)[:, 9 * m0:9 * m1].rearrange("p (m s) -> p m s", s=9),
                          over(v_("b_ada", m0, m1 - m0), 9), ALU.add))
                V.then(ts(amul3[:, w], mod3[:, scale:scale + 8, :], 1.0, None, ALU.add))
                V.then(tt(amul3[:, w], amul3[:, w], over(v_(nw, 0, 8), 9), ALU.mult))

            dve.wait_ge(s_ada, ADA_EARLY)
            dve_mod(6, 0, 16, 0, 8, "norm_mix")
            dve.wait_ge(s_x, 16)
            dve_recip(V, "ss_mix", 0, rs_a, rt_a)
            V.rs = rs_a
            dve_norm(V, X, HT, amul3[:, 0], mod3[:, 0:8, :])
            dve.wait_ge(s_ada, len(ADA_SLOT))
            dve_mod(7, 16, 48, 1, 32, "norm_moe")
            V.then(nc.vector.memset(rows[0:64, :], 0.0))
            s = wait_fill(dve, "rows", 0)
            ts(tri3(rowt[0][0:16]), pset(s)[0:16], v_("dtb")[0:16], None, ALU.add).then_inc(s_free[s], 1)
            freed(dve, "rows", 0)
            dve.sem_inc(r_z, 1)
            dve.wait_ge(r_l, 1)
            V.then(stt(out=rowt[3][0:16], in0=rowt[0][0:16], scalar=0.0, in1=rowt[1][0:16], op0=ALU.max, op1=ALU.add))
            V.then(nc.vector.tensor_copy(rows[32:48, :], rowt[3][0:16]))
            V.then(ts(rowt[2][0:16], rowt[3][0:16], nexpa, -1.0, ALU.mult, ALU.mult))
            V.then(nc.vector.memset(rowt[1][0:16], 1.0))
            V.then(nc.vector.memset(rowt[1][0:16, 0:NP_TOK:P], 0.0))
            V.then(nc.vector.memset(rowt[1][0:16, NP_TOK:T:SLEN], 0.0))
            V.then(nc.vector.tensor_tensor_scan(rows[0:16, :], rowt[1][0:16], rowt[2][0:16], 0.0, ALU.mult, ALU.add))
            end_phase(dve, 0)
            dve_cb_start(V, cb_g)
            for m in range(12):
                dve_conv(V, m, cb_g, QKV[:, m, :], "gdn_conv", m, 12)
                if 2 <= m < 10:
                    n = m - 2
                    dve_recip(V, "qkn", n, rs_g, rt_g)
                    V.then(stt(out=QKV[:, n, :], in0=QKV[:, n, :], scalar=(P ** -0.5 if n < 4 else 1.0), in1=rs_g,
                               op0=ALU.mult, op1=ALU.mult))
            end_phase(dve, 1)
            V.then(nc.vector.memset(cS, 0.0))
            for c in range(NT):
                t0 = c * P
                sample = c == NC7
                dve.wait_ge(c_bc, c + 1)
                V.then(nc.vector.tensor_copy(colG, bank(2)[:, 0:80]), c_cols)
                V.then(tt(hd(cDT, 4), hd(bank(0), 4), over(colG[:, 0:4], P), ALU.subtract))
                V.then(tt(hd(cDT, 4), hd(cDT, 4), by(c_("neg_sample" if sample else "neg_prompt"), 4), ALU.add), c_diff)
                dve.wait_ge(c_exp, c + 1)
                dve.wait_ge(c_gram, c + 1)
                V.then(tt(cLT, cDT, bank(3), ALU.mult))
                V.then(tt(cLT, cLT, bank(1), ALU.mult))
                V.then(tt(cAT, cDT, bank(4), ALU.mult))
                V.then(tt(hd(cQE, 4), QKV[:, 0:4, t0:t0 + P], hd(cEG, 4), ALU.mult))
                V.then(tt(colB, colG[:, 76:80], colE[:, 0:4], ALU.mult))
                if sample:
                    V.then(tt(hd(cUM[:, 0:512], 4), hd(cDT, 4), by(c_("last"), 4), ALU.mult))
                    V.then(nc.vector.reduce_sum(colK[:, 0:4], hd(cUM[:, 0:512], 4), axis=AX.X))
                else:
                    V.then(nc.vector.tensor_copy(colK[:, 0:4], hd(cDT, 4)[:, :, P - 1]))
                dve.wait_ge(c_tok, c + 1)
                V.then(tt(hd(cKE, 4), hd(bank(5), 4), over(colK[:, 0:4], P), ALU.mult))
                V.then(tt(hd(cKB, 4), hd(bank(5), 4), over(colB, P), ALU.mult))
                V.then(tt(hd(cVB, 4), hd(bank(6), 4), over(colG[:, 76:80], P), ALU.mult))
                V.then(nc.vector.tensor_copy(hd(cXX, 8), by(ident, 8)), c_ops)
                level = lambda lv: V.then(tt(hd(cLK[lv % 2], 4), hd(cLT, 4), by(c_("level", P * lv, P), 4), ALU.mult), c_lk)
                level(0)
                for lv in range(LEV[c]):
                    n = LEV0[c] + lv
                    if lv + 1 < LEV[c]:
                        level(lv + 1)
                    for f in range(2):
                        dve.wait_ge(c_d, 2 * n + 1 + f)
                        x = cXX[:, 512 * f:512 * (f + 1)]
                        tt(x, x, bank(1 + f), ALU.subtract).then_inc(c_x, 1)
                dve.wait_ge(c_w, c + 1)
                V.then(ts(cNW, bank(3), -1.0, None, ALU.mult), c_nw)
                if sample:
                    dve.wait_ge(c_u, c + 1)
                    V.then(nc.vector.tensor_copy(cPS, bank(4)), c_ut)
                dve.wait_ge(c_o, c + 1)
                V.then(nc.vector.tensor_copy(QKV[:, 0:4, t0:t0 + P], hd(bank(5), 4)), c_os)
                if not sample:
                    dve.wait_ge(c_s, c + 1)
                    V.then(tt(hd(cS, 4), hd(cS, 4), hd(cEG, 4)[:, :, P - 1:P].to_broadcast([P, 4, P]), ALU.mult))
                    V.then(tt(cS, cS, bank(6), ALU.add), c_ss)
                else:
                    S0 = wait_load(dve, "gdn_state", 0).rearrange("p (b h v) -> p b h v", b=NSEQ, h=GH)
                    dve.wait_ge(c_us, c + 1)
                    for h in range(GH):
                        V.then(tt(hd(cUM, 8), by(cU[:, h * P:(h + 1) * P], 8), over(c_("row"), P), ALU.mult), c_um)
                        dve.wait_ge(c_s, c + h + 1)
                        V.then(tt(S0[:, :, h, :], S0[:, :, h, :],
                                  over(cEG[:, h * P + SLEN - 1:(h + 1) * P:SLEN], P), ALU.mult))
                        V.then(tt(S0[:, :, h, :], S0[:, :, h, :], hd(psum[:, 0:1024], 8), ALU.add), c_ss)
            end_phase(dve, 2)
            for m in range(GH):
                dve_recip(V, "gdn_ss", m, rs_a, rt_a)
                V.then(stt(out=QKV[:, m, :], in0=QKV[:, m, :], scalar=v_("gdn_norm"), in1=rs_a, op0=ALU.mult, op1=ALU.mult))
                freed(dve, "zb", m)
                V.then(tt(Y[:, m, :], Y[:, m, :], QKV[:, m, :], ALU.mult))
            dve.wait_ge(s_pstate, 32)
            end_phase(dve, 3)
            dve_merge(V, 1)
            end_phase(dve, 4)
            dve_cb_start(V, cb_s)
            for m in range(8):
                dve_conv(V, 12 + m, cb_s, XBC[:, m, :], "ssd_conv", m, 8, bias=v_("ssd_conv_b", m))
            end_phase(dve, 5)
            V.then(nc.vector.memset(dH, 0.0))
            for c in range(NT):
                t0 = c * P
                sample = c == NC7
                dve.wait_ge(d_bc, c + 1)
                V.then(nc.vector.tensor_copy(colG, bank(2)[:, 0:80]))
                V.then(tt(hd(dDT, 8), hd(psum[:, 0:1024], 8), over(colG[:, 4:12], P), ALU.subtract))
                V.then(tt(hd(dDT, 8), hd(dDT, 8), by(c_("neg_sample" if sample else "neg_prompt"), 8), ALU.add), d_diff)
                V.then(nc.vector.tensor_copy(dB, bank(4)[:, 0:256]))
                V.then(tt(hd(dXD, 8), hd(bank(5), 8), over(colG[:, 36:44], 64), ALU.mult))
                dve.wait_ge(d_exp, c + 1)
                if sample:
                    for g in range(2):
                        V.then(tt(hd(dTMP, 4), hd(dDT[:, 512 * g:512 * (g + 1)], 4), by(c_("last"), 4), ALU.mult))
                        V.then(nc.vector.reduce_sum(colK[:, 4 * g:4 * g + 4], hd(dTMP, 4), axis=AX.X))
                    V.then(nc.vector.tensor_copy(hd(colL, 8), hd(dEG, 8)[:, :, SLEN - 1:P:SLEN]))
                else:
                    V.then(nc.vector.tensor_copy(colK, hd(dDT, 8)[:, :, P - 1]))
                    V.then(nc.vector.tensor_copy(colL[:, 0:8], hd(dEG, 8)[:, :, P - 1]))
                V.then(tt(colW, colK, colG[:, 36:44], ALU.mult))
                V.then(tt(hd(dXW, 8), hd(bank(5), 8), over(colW, 64), ALU.mult))
                d4 = dDT.rearrange("p (g h t) -> p g h t", g=2, h=4)
                e4 = dEG.rearrange("p (g h t) -> p g h t", g=2, h=4)
                V.then(tt(d4, d4, hd(bank(3)[:, 0:256], 2).unsqueeze(2).to_broadcast([P, 2, 4, P]), ALU.mult))
                V.then(tt(e4, e4, XBC[:, 6:8, t0:t0 + P].unsqueeze(2).to_broadcast([P, 2, 4, P]), ALU.mult), d_ops)
                dve.wait_ge(d_y, c + 1)
                for m in range(KM):
                    V.then(stt(out=XBC[:, m, t0:t0 + P], in0=XBC[:, m, t0:t0 + P], scalar=v_("ssd_d", m),
                               in1=bank(6)[:, m * P:(m + 1) * P], op0=ALU.mult, op1=ALU.add),
                           d_ys if m == KM - 1 else None)
                if not sample:
                    dve.wait_ge(d_s, c + 1)
                    V.then(tt(hd(dH, 8), hd(dH, 8), over(colL[:, 0:8], 64), ALU.mult))
                    V.then(tt(dH, dH, bank(7), ALU.add), d_ss)
                else:
                    H0 = wait_load(dve, "ssd_state", 0).rearrange("p (b h d) -> p b h d", b=NSEQ, h=SH)
                    for b in range(NSEQ):
                        V.then(ts(dBM, dB, c_("row", b, 1), None, ALU.mult), d_bm)
                        dve.wait_ge(d_s, c + b + 1)
                        V.then(tt(H0[:, b], H0[:, b], over(hd(colL, 8)[:, :, b], 64), ALU.mult))
                        V.then(tt(H0[:, b], H0[:, b], hd(bank(7), 8), ALU.add), d_ss)
            end_phase(dve, 6)
            for m in range(KM):
                V.then(tt(XBC[:, m, :], XBC[:, m, :], Y[:, m, :], ALU.mult), d_gated)
            dve_recip(V, "ssd_ss", 0, rs_s, rt_s)
            for m in range(KM):
                V.then(stt(out=Y[:, m, :], in0=XBC[:, m, :], scalar=v_("ssd_norm", m), in1=rs_s, op0=ALU.mult, op1=ALU.mult))
            end_phase(dve, 7)
            dve_merge(V, 3)
            end_phase(dve, 8)
            lam = v_("lru_lambda", 0, 4)
            V.then(ts(lruc[:, 12:16], lam, -1.0, 0.0, ALU.mult, ALU.max))
            dve.wait_ge(l_sp, 1)
            V.then(tt(lruc[:, 12:16], lruc[:, 12:16], lruc[:, 8:12], ALU.add))
            V.then(ts(lruc[:, 0:4], lruc[:, 12:16], 8.0, None, ALU.mult))
            V.then(ts(lruc[:, 4:8], lruc[:, 12:16], -8.0, None, ALU.mult), l_col)
            dve_cb_start(V, cb_l)
            for m in range(4):
                dve_conv(V, 20 + m, cb_l, XF[:, m, :], "lru_conv", m, 4, bias=v_("lru_conv_b", m))
            lo = lru_out[:, :].rearrange("p (m b) -> p m b", b=9)
            for m in range(4):
                a, b = lt[2], lt[5]
                first = slice(NP_TOK, T, SLEN)
                dve.wait_ge(l_a, m + 1)
                V.then(tt(lt[4], a, a, ALU.mult))
                V.then(stt(out=lt[4], in0=lt[4], scalar=1.0, in1=lt[3], op0=ALU.add, op1=ALU.mult), l_m)
                V.then(tt(b, lt[1], XF[:, m, :], ALU.mult))
                dve.wait_ge(l_b, m + 1)
                V.then(tt(b, b, lt[4], ALU.mult))
                V.then(tt(lruc[:, 16:24], a[:, first], v_("lru_h0", 8 * m, 8), ALU.mult))
                V.then(tt(b[:, first], b[:, first], lruc[:, 16:24], ALU.add))
                V.then(nc.vector.memset(a[:, first], 0.0))
                V.then(nc.vector.tensor_tensor_scan(b, a, b, 0.0, ALU.mult, ALU.add))
                V.then(nc.vector.tensor_copy(lo[:, m, 0:1], b[:, NP_TOK - 1:NP_TOK]))
                V.then(nc.vector.tensor_copy(lo[:, m, 1:9], b[:, NP_TOK + SLEN - 1:T:SLEN]))
                freed(dve, "gc", m)
                V.then(tt(Y[:, m, :], Y[:, m, :], b, ALU.mult), l_done)
            end_phase(dve, 9)
            dve_merge(V, 2)
            end_phase(dve, 10)
            are, aim = v_("s5_re", 0, 16), v_("s5_im", 0, 16)
            dve.wait_ge(a_mag, 1)
            V.then(tt(s5("mag"), are, s5("dt"), ALU.mult))
            V.then(tt(s5("th"), aim, s5("dt"), ALU.mult))

            def reduce_angle(dst, shift):
                V.then(ts(s5("t1"), s5("th"), shift, None, ALU.add))
                V.then(ts(s5("t0"), s5("t1"), float(1 / (2 * np.pi)), ROUND, ALU.mult, ALU.add))
                V.then(ts(s5("t0"), s5("t0"), ROUND, None, ALU.subtract))
                V.then(stt(out=s5("t1"), in0=s5("t0"), scalar=-TWO_PI_HI, in1=s5("t1"), op0=ALU.mult, op1=ALU.add))
                V.then(stt(out=s5("t1"), in0=s5("t0"), scalar=-TWO_PI_LO, in1=s5("t1"), op0=ALU.mult, op1=ALU.add))
                V.then(ts(dst, s5("t1"), 3.141592, -3.141592, ALU.min, ALU.max))

            reduce_angle(s5("sin"), 0.0)
            reduce_angle(s5("cos"), float(np.pi / 2))
            dve.sem_inc(a_th, 1)
            dve.wait_ge(a_sin, 1)
            V.then(tt(s5("lre"), s5("mag"), s5("cos"), ALU.mult))
            V.then(tt(s5("lim"), s5("mag"), s5("sin"), ALU.mult))
            V.then(tt(s5("den"), are, are, ALU.mult))
            V.then(tt(s5("t0"), aim, aim, ALU.mult))
            V.then(tt(s5("den"), s5("den"), s5("t0"), ALU.add))
            V.then(nc.vector.reciprocal(s5("den"), s5("den")))
            V.then(ts(s5("t0"), s5("lre"), -1.0, None, ALU.add))
            V.then(tt(s5("fre"), s5("t0"), are, ALU.mult))
            V.then(tt(s5("t1"), s5("lim"), aim, ALU.mult))
            V.then(tt(s5("fre"), s5("fre"), s5("t1"), ALU.add))
            V.then(tt(s5("fre"), s5("fre"), s5("den"), ALU.mult))
            V.then(tt(s5("fim"), s5("lim"), are, ALU.mult))
            V.then(tt(s5("t1"), s5("t0"), aim, ALU.mult))
            V.then(tt(s5("fim"), s5("fim"), s5("t1"), ALU.subtract))
            V.then(tt(s5("fim"), s5("fim"), s5("den"), ALU.mult))
            V.then(nc.vector.tensor_copy(s5("pr", 0), s5("cos")))
            V.then(nc.vector.tensor_copy(s5("pi", 0), s5("sin")))
            for k in range(9):
                V.then(tt(s5("t0"), s5("pi", k), s5("pi", k), ALU.mult))
                V.then(tt(s5("pr", k + 1), s5("pr", k), s5("pr", k), ALU.mult))
                V.then(tt(s5("pr", k + 1), s5("pr", k + 1), s5("t0"), ALU.subtract))
                V.then(tt(s5("t0"), s5("pr", k), s5("pi", k), ALU.mult))
                V.then(ts(s5("pi", k + 1), s5("t0"), 2.0, None, ALU.mult))
            pw = s5p[:, :].rearrange("p (w j l) -> p w j l", w=2, l=Q5 + 1)
            V.then(nc.vector.memset(pw[:, 0, :, 0], 1.0))
            V.then(nc.vector.memset(pw[:, 1, :, 0], 0.0))
            V.then(nc.vector.tensor_copy(pw[:, 0, :, 1], s5("lre")))
            V.then(nc.vector.tensor_copy(pw[:, 1, :, 1], s5("lim")))
            for n in (1, 2, 4):
                lo, hi = slice(1, n + 1), slice(n + 1, 2 * n + 1)
                ar, ai = pw[:, 0, :, lo], pw[:, 1, :, lo]
                br, bi = over(pw[:, 0, :, n], n), over(pw[:, 1, :, n], n)
                tmp = small[:, 256:256 + 16 * n].rearrange("p (j l) -> p j l", l=n)
                V.then(tt(tmp, ai, bi, ALU.mult))
                V.then(tt(pw[:, 0, :, hi], ar, br, ALU.mult))
                V.then(tt(pw[:, 0, :, hi], pw[:, 0, :, hi], tmp, ALU.subtract))
                V.then(tt(tmp, ar, bi, ALU.mult))
                V.then(tt(pw[:, 1, :, hi], ai, br, ALU.mult))
                V.then(tt(pw[:, 1, :, hi], pw[:, 1, :, hi], tmp, ALU.add))
            for _ in range(3):
                V.then(tt(s5("mag"), s5("mag"), s5("mag"), ALU.mult))
            V.then(nc.vector.memset(sMASK, 1.0))
            V.then(nc.vector.memset(sMASK[:, 0:1], 0.0))
            V.then(nc.vector.memset(sMASK[:, NQP:NQ:2], 0.0), a_mask)
            V.then(nc.vector.memset(sDD, 0.0))
            V.then(nc.vector.tensor_copy(hd(sID4, 4), by(ident[0:32, 0:32], 4)))
            bc = wait_load(dve, "s5_bc", 0)
            br, bi, cr, ci = [bc[:, 512 * w:512 * (w + 1)].rearrange("p (j c) -> p j c", c=32) for w in range(4)]
            wb = bc[:, 2048:4096].rearrange("p (w q l c) -> p w q l c", w=2, q=4, c=32)
            t = [x[:, 0:512].rearrange("p (j c) -> p j c", c=32) for x in (sT2[0], sT2[1], sV[0], sV[1])]
            V.then(tt(t[0], br, over(s5("fre"), 32), ALU.mult))
            V.then(tt(t[1], bi, over(s5("fim"), 32), ALU.mult))
            V.then(tt(t[2], bi, over(s5("fre"), 32), ALU.mult))
            V.then(tt(t[3], br, over(s5("fim"), 32), ALU.mult))
            V.then(tt(br, t[0], t[1], ALU.subtract))
            V.then(tt(bi, t[2], t[3], ALU.add))
            so = s5_out[:, :].rearrange("p (w j b) -> p w j b", w=2, b=9)

            def lags(ap, i, n):
                return ap[:, 4 * i:4 * i + 4, :].unsqueeze(2).to_broadcast([P, 4, n, 32])

            def powers(w, i, n):
                return pw[:, w, 4 * i:4 * i + 4, 0:n].unsqueeze(3).to_broadcast([P, 4, n, 32])

            def dve_matrices(i):
                tb = sT[:, 0:1024].rearrange("p (q l c) -> p q l c", q=4, c=32)
                V.then(tt(tb, lags(bi, i, Q5), powers(1, i, Q5), ALU.mult))
                V.then(tt(wb[:, 0], lags(br, i, Q5), powers(0, i, Q5), ALU.mult))
                V.then(tt(wb[:, 0], wb[:, 0], tb, ALU.subtract))
                V.then(tt(tb, lags(br, i, Q5), powers(1, i, Q5), ALU.mult))
                V.then(tt(wb[:, 1], lags(bi, i, Q5), powers(0, i, Q5), ALU.mult))
                V.then(tt(wb[:, 1], wb[:, 1], tb, ALU.add), a_wb)
                if i >= 2:
                    dve.wait_ge(a_y, 4 * (i - 1))
                if i:
                    dve.wait_ge(a_k, i)
                for w, b in ((0, br), (1, bi)):
                    nc.vector.tensor_copy(sB4[:, w], b[:, 4 * i:4 * i + 4, :].unsqueeze(2).to_broadcast([P, 4, 4, 32]))
                tt(hd(sDIAG, 4), hd(sID4, 4), over(v_("s5_d", 4 * i, 4)[0:32], 32), ALU.mult)
                ca = sCA[i % 2]
                tc = sT[:, :].rearrange("p (q l c) -> p q l c", q=4, c=32)
                V.then(tt(tc, lags(ci, i, Q5 + 1), powers(1, i, Q5 + 1), ALU.mult))
                V.then(tt(ca[:, 0], lags(cr, i, Q5 + 1), powers(0, i, Q5 + 1), ALU.mult))
                V.then(tt(ca[:, 0], ca[:, 0], tc, ALU.subtract))
                V.then(tt(tc, lags(cr, i, Q5 + 1), powers(1, i, Q5 + 1), ALU.mult))
                V.then(tt(ca[:, 1], lags(ci, i, Q5 + 1), powers(0, i, Q5 + 1), ALU.mult))
                V.then(stt(out=ca[:, 1], in0=ca[:, 1], scalar=-1.0, in1=tc, op0=ALU.mult, op1=ALU.subtract), a_ca)

            def dve_rotation(i):
                c4, s4, t4 = hd(sCOS, 4), hd(sSIN, 4), [hd(x, 4) for x in sT2]
                V.then(nc.vector.memset(c4[:, :, 0:1], 1.0))
                V.then(nc.vector.memset(s4[:, :, 0:1], 0.0))
                for k in range(7):
                    n = 1 << k
                    pr, pi = [over(s5(x, k + 3)[:, 4 * i:4 * i + 4], n) for x in ("pr", "pi")]
                    tt(t4[0][:, :, 0:n], s4[:, :, 0:n], pi, ALU.mult)
                    tt(t4[1][:, :, 0:n], c4[:, :, 0:n], pi, ALU.mult)
                    tt(c4[:, :, n:2 * n], c4[:, :, 0:n], pr, ALU.mult)
                    V.then(tt(s4[:, :, n:2 * n], s4[:, :, 0:n], pr, ALU.mult))
                    tt(c4[:, :, n:2 * n], c4[:, :, n:2 * n], t4[0][:, :, 0:n], ALU.subtract)
                    V.then(tt(s4[:, :, n:2 * n], s4[:, :, n:2 * n], t4[1][:, :, 0:n], ALU.add))
                for x in (c4, s4):
                    nc.vector.tensor_copy(x[:, :, NQP:NQ].rearrange("p q (b m) -> p q b m", m=2),
                                          x[:, :, 0:2].unsqueeze(2).to_broadcast([P, 4, NSEQ, 2]))
                V.then(tt(hd(sR, 4), by(sMASK, 4), over(s5("mag")[:, 4 * i:4 * i + 4], NQ), ALU.mult))

            dve_matrices(0)
            dve_rotation(0)
            for i in range(4):
                dve.wait_ge(a_ve, i + 1)
                tt(sT2[0], sV[0], sCOS, ALU.mult)
                V.then(tt(sT2[1], sV[1], sSIN, ALU.mult))
                V.then(tt(sZ[0], sT2[0], sT2[1], ALU.add))
                tt(sT2[0], sV[1], sCOS, ALU.mult)
                V.then(tt(sT2[1], sV[0], sSIN, ALU.mult))
                V.then(tt(sZ[1], sT2[0], sT2[1], ALU.subtract))
                nc.vector.tensor_tensor_scan(sZ[0], sR, sZ[0], 0.0, ALU.mult, ALU.add)
                V.then(nc.vector.tensor_tensor_scan(sZ[1], sR, sZ[1], 0.0, ALU.mult, ALU.add))
                tt(sT2[0], sZ[0], sCOS, ALU.mult)
                V.then(tt(sT2[1], sZ[1], sSIN, ALU.mult))
                V.then(tt(sV[0], sT2[0], sT2[1], ALU.subtract))
                tt(sT2[0], sZ[0], sSIN, ALU.mult)
                V.then(tt(sT2[1], sZ[1], sCOS, ALU.mult))
                V.then(tt(sV[1], sT2[0], sT2[1], ALU.add), a_s)
                lr, li = [over(pw[:, w, 4 * i:4 * i + 4, Q5], 9) for w in range(2)]
                xr, xi = [hd(sV[w], 4)[:, :, NQP - 1:NQ:2] for w in range(2)]
                fr, fi = [so[:, w, 4 * i:4 * i + 4, :] for w in range(2)]
                tt(sLAST[2], xr, lr, ALU.mult)
                V.then(tt(sLAST[3], xi, li, ALU.mult))
                V.then(tt(fr, sLAST[2], sLAST[3], ALU.subtract))
                V.then(tt(fr, fr, sLAST[0], ALU.add))
                tt(sLAST[2], xr, li, ALU.mult)
                V.then(tt(sLAST[3], xi, lr, ALU.mult))
                V.then(tt(fi, sLAST[2], sLAST[3], ALU.add))
                V.then(tt(fi, fi, sLAST[1], ALU.add), a_fin)
                if i < 3:
                    dve_matrices(i + 1)
                    dve_rotation(i + 1)
            for m in range(4):
                freed(dve, "glu", m)
                V.then(tt(Y[:, m, :], U[:, m, :], st[m], ALU.mult), a_gs)
            end_phase(dve, 11)
            dve_merge(V, 0)
            end_phase(dve, 12)
            dve.wait_ge(s_xr, 16)
            for m in range(KD):
                dve_residual(V, "out", m, 16, res_tmp)
            end_phase(dve, 13)
            dve_recip(V, "ss_moe", 0, rs_e, rt_e)
            V.rs = rs_e
            dve_norm(V, X, HT, amul3[:, 1], mod3[:, 24:32, :])
            V.then(nc.vector.memset(cmpB[:, 0:NB], 0.0), m_zero)
            V.then(nc.vector.memset(ones_row[0:16], 1.0))
            dve.wait_ge(m_idz, 16)
            dve.wait_ge(m_sc, 1)
            V.then(tt(hd(rsel, 9), hd(scores, 9), by(v_("rbias", 0, NE), 9), ALU.add))

            def ranks(dst, src, n):
                s4 = src.rearrange("p (n j) -> p n j", j=4)
                si, sj = s4.unsqueeze(2).to_broadcast([P, n, 4, 4]), s4.unsqueeze(3).to_broadcast([P, n, 4, 4])
                ca = cmpA[:, 0:16 * n].rearrange("p (n j i) -> p n j i", j=4, i=4)
                cb_ = cmpB[:, 0:16 * n].rearrange("p (n j i) -> p n j i", j=4, i=4)
                V.then(tt(ca, si, sj, ALU.is_gt))
                V.then(tt(cb_, si, sj, ALU.is_equal))
                V.then(tt(cmpB[:, 0:16 * n].rearrange("p (n x) -> p n x", x=16),
                          cmpB[:, 0:16 * n].rearrange("p (n x) -> p n x", x=16), by(c_("tri"), n), ALU.mult))
                V.then(tt(cmpA[:, 0:16 * n], cmpA[:, 0:16 * n], cmpB[:, 0:16 * n], ALU.add))
                V.then(nc.vector.reduce_sum(dst.rearrange("p (n j) -> p n j", j=4), ca, axis=AX.X))

            ranks(rank, rsel, 36)
            V.then(ts(picked, rank, 1.5, None, ALU.is_lt))
            V.then(tt(rtmp, picked, rsel, ALU.mult))
            V.then(nc.vector.reduce_sum(grp[:, 0:36], hd(rtmp, 36), axis=AX.X))
            ranks(grp[:, 36:72], grp[:, 0:36], 9)
            V.then(ts(grp[:, 36:72], grp[:, 36:72], 0.5, None, ALU.is_lt))
            V.then(tt(hd(picked, 36), hd(picked, 36), over(grp[:, 36:72], 4), ALU.mult), m_mask)
            V.then(ts(first1, rank, 0.5, None, ALU.is_lt))
            V.then(tt(first1, first1, picked, ALU.mult))
            V.then(tt(weight, scores, picked, ALU.mult))
            V.then(nc.vector.reduce_sum(grp[:, 72:81], hd(weight, 9), axis=AX.X))
            V.then(nc.vector.reciprocal(grp[:, 72:81], grp[:, 72:81]))
            V.then(tt(hd(weight, 9), hd(weight, 9), over(grp[:, 72:81], NE), ALU.mult))

            def pick_both(dst, src):
                V.then(tt(rtmp, src, first1, ALU.mult))
                V.then(nc.vector.reduce_sum(dst[:, 0, :], hd(rtmp, 9), axis=AX.X))
                V.then(tt(rsel, src, picked, ALU.mult))
                V.then(tt(rsel, rsel, rtmp, ALU.subtract))
                V.then(nc.vector.reduce_sum(dst[:, 1, :], hd(rsel, 9), axis=AX.X))

            pick_both(w12, weight)
            dve.wait_ge(m_maskt, 1)
            V.then(nc.vector.tensor_copy(mask_row[0:16], psum[0:16, 2048:2048 + T]))
            V.then(nc.vector.tensor_tensor_scan(cum_row[0:16], ones_row[0:16], mask_row[0:16], 0.0, ALU.mult, ALU.add))
            V.then(ts(ecol[:, 0:1], cum_row[0:16, T - 1:T], 1.0 / BLK, (BLK - 1.0) / BLK - 0.498, ALU.mult, ALU.add))
            V.then(ts(ecol[:, 0:1], ecol[:, 0:1], ROUND, None, ALU.add))
            V.then(ts(ecol[:, 1:2], ecol[:, 0:1], ROUND, None, ALU.subtract), m_nblk)
            dve.wait_ge(m_start, 1)
            V.then(tt(ecol[:, 2:3], bank(7)[0:16, 200:201], ecol[:, 1:2], ALU.add))
            V.then(ts(ecol[:, 3:4], bank(7)[0:16, 200:201], float(BLK), -1.0, ALU.mult, ALU.add))
            V.then(ts(cum_row[0:16], cum_row[0:16], ecol[:, 3:4], None, ALU.add))
            V.then(ts(cmpB[0:16, 0:NB], c_("block")[0:16], ecol[:, 2:3], None, ALU.is_ge), m_pos)
            dve.wait_ge(m_post, 1)
            V.then(nc.vector.tensor_copy(cmpA[:, 0:144], bank(7)[:, 0:144]))
            V.then(ts(erow[:, 0, :], bank(7)[0:1, 256:256 + NB], NE - 1.0, None, ALU.min))
            pick_both(posf.rearrange("p (k c) -> p k c", k=2), cmpA[:, 0:144])
            V.then(nc.vector.tensor_copy(posi, posf), m_posi)
            ei, ej = erow[:, 0, :], erow[:, 0, :]
            big = btab[0:1].rearrange("p (j i) -> p j i", i=NB)
            V.then(tt(big, ei.unsqueeze(1).to_broadcast([1, NB, NB]), ej.unsqueeze(2).to_broadcast([1, NB, NB]), ALU.is_le))
            V.then(stt(out=big, in0=big, scalar=100.0, in1=ei.unsqueeze(1).to_broadcast([1, NB, NB]),
                       op0=ALU.mult, op1=ALU.add))
            V.then(nc.vector.tensor_reduce(erow[:, 1, :], big, AX.X, ALU.min))
            V.then(ts(erow[:, 1, :], erow[:, 1, :], NE - 1.0, None, ALU.min))
            V.then(nc.vector.memset(erow[:, 2, :], 1.0))
            V.then(tt(erow[:, 2, 1:NB], erow[:, 0, 1:NB], erow[:, 0, 0:NB - 1], ALU.not_equal))
            V.then(nc.vector.memset(erow[:, 4, :], 1.0))
            V.then(nc.vector.tensor_tensor_scan(erow[:, 3, :], erow[:, 4, :], erow[:, 2, :], 0.0, ALU.mult, ALU.add))
            V.then(ts(erow[:, 4, :], erow[:, 3, :], 0.5, -0.25, ALU.mult, ALU.add))
            V.then(ts(erow[:, 4, :], erow[:, 4, :], ROUND, None, ALU.add))
            V.then(ts(erow[:, 4, :], erow[:, 4, :], ROUND, None, ALU.subtract))
            V.then(stt(out=erow[:, 4, :], in0=erow[:, 4, :], scalar=-2.0, in1=erow[:, 3, :], op0=ALU.mult, op1=ALU.add))
            V.then(ts(erow[:, 3, :], erow[:, 4, :], float(WSET), None, ALU.mult))
            V.then(ts(erow[:, 5, :], erow[:, 3, :], -1.0, float(WSET), ALU.mult, ALU.add))
            V.then(nc.vector.tensor_copy(eint, erow[:, 0:4, :]))
            V.then(nc.vector.tensor_copy(eint_at[:, 0, :], erow[:, 5, :]), m_tab)
            dve.wait_ge(m_idt, 1)
            V.then(nc.vector.tensor_copy(idxi, bank(4)[:, 0:NB]), m_idx)
            end_phase(dve, 14)
            for j in range(NB):
                dve.wait_ge(e_sg, j + 1)
                dve.wait_ge(e_u, j + 1)
                if j:
                    dve.wait_ge(e_ht, j)
                tt(ehid, esg, bank(1), ALU.mult).then_inc(e_hid, 1)
                dve.wait_ge(e_ht, j + 1)
                nc.vector.tensor_copy(ehT, bank(4)).then_inc(e_htc, 1)
                dve.wait_ge(e_d, j + 1)
                if j >= 2:
                    dve.wait_ge(e_st[j % 2], 16 * (j // 2))
                nc.vector.tensor_copy(yb[j % 2][:, 512:1024], bank(7)).then_inc(e_yd, 1)
            end_phase(dve, 15)
            for c in range(NT):
                for k in range(2):
                    dve.wait_ge(f_y[c % 2], 32 * (c // 2 + 1))
                if c >= 2:
                    dve.wait_ge(f_t, c - 1)
                V.then(ts(ff[c % 2], yg[c % 2][0], w12[:, 0, c:c + 1], None, ALU.mult))
                V.then(stt(out=ff[c % 2], in0=yg[c % 2][1], scalar=w12[:, 1, c:c + 1], in1=ff[c % 2],
                           op0=ALU.mult, op1=ALU.add), f_f)
                dve.wait_ge(f_t, c + 1)
                p8 = psum[:, 1024 * (c % 2):1024 * (c % 2 + 1)]
                xc = X[:, :, c * P:(c + 1) * P]
                if c < NT - 1:
                    V.then(tt(hd(ftmp, 8), hd(p8, 8), over(mod3[:, 40:48, 0], P), ALU.mult))
                else:
                    V.then(tt(ftmp.rearrange("p (k b t) -> p k b t", k=8, b=8), p8.rearrange("p (k b t) -> p k b t", k=8, b=8),
                              mod3[:, 40:48, 1:9].unsqueeze(3).to_broadcast([P, 8, 8, SLEN]), ALU.mult))
                V.then(tt(xc, xc, hd(ftmp, 8), ALU.add), f_x)
            end_phase(dve, 16)
            dve_recip(V, "ss_final", 0, rs_e, rt_e)
            for k in range(KD):
                V.then(stt(out=HT[:, k, :], in0=X[:, k, :], scalar=v_("norm_final", k), in1=rs_e, op0=ALU.mult, op1=ALU.mult))
            end_phase(dve, 17)


def _outs():
    return {"yT": (P, KD, T), "hist_out": (P, 24 * 27), "s5_out": (P, 288), "lru_out": (P, 36),
            "gdn_p": (P, 512), "gdn_s": (P, 4096), "ssd_p": (P, 512), "ssd_s": (P, 4096)}


def _constants():
    c = np.zeros((P, NCST), np.float32)

    def put(name, a):
        o, w = CST[name]
        c[:, o:o + w] = a
    s, t = np.arange(P)[:, None], np.arange(P)[None, :]
    put("ident", np.eye(P))
    put("ones", 1.0)
    put("level", np.concatenate([(s >> (k + 1) == t >> (k + 1)) & ((s >> k) & 1 == 0) & ((t >> k) & 1 == 1)
                                 for k in range(7)], axis=1))
    put("neg_prompt", np.where(t >= s, 0.0, -1e30))
    put("neg_sample", np.where((t >= s) & (t // SLEN == s // SLEN), 0.0, -1e30))
    put("last", np.broadcast_to(t % SLEN == SLEN - 1, (P, P)))
    put("row", s // SLEN == np.arange(NSEQ)[None, :])
    put("eps", EPS)
    put("token", s + P * np.arange(NT)[None, :])
    put("block", np.broadcast_to(np.arange(NB), (P, NB)))
    put("before", s < np.arange(NE)[None, :])
    j, i = np.arange(16) // 4, np.arange(16) % 4
    put("tri", np.broadcast_to(i < j, (P, 16)))
    return c


def _pack(w):
    k, m = w.shape[0] // P, w.shape[1] // P
    per = 32 // k
    a = w.reshape(k, P, m, P).transpose(2, 1, 0, 3).reshape(m // per, per, P, k, P)
    return np.ascontiguousarray(a.transpose(0, 2, 1, 3, 4)).reshape(m // per, P, 4096)


def kernel(**inputs):
    import concourse.bacc as _bacc
    from concourse import mybir as _mybir
    from concourse.bass_utils import run_bass_kernel_spmd as _run

    i = {k: np.asarray(v) for k, v in inputs.items()}
    f = np.float32

    def cols(v):
        return v.reshape(-1, P).T

    def padded(a):
        out = np.zeros((P, 4096), f)
        out[:, :a.shape[1]] = a
        return out[None]

    arr = {"cst": _constants()}
    arr["xT"] = np.ascontiguousarray(np.concatenate([i["x_prompt"].reshape(NP_TOK, D), i["x_sample"].reshape(P, D)])
                                     .T.reshape(KD, P, T).transpose(1, 0, 2))
    c = np.concatenate([i["c_prompt"], i["c_sample"]])
    arr["cT"] = np.ascontiguousarray(c.T.reshape(KD, P, 9).transpose(1, 0, 2)).reshape(P, 72)
    vec = np.zeros((P, NVEC), f)

    def put(name, a):
        o, w = VEC[name]
        vec[:a.shape[0], o:o + w] = a
    for n, src in (("norm_mix", "norm_mix_w"), ("norm_moe", "norm_moe_w"), ("b_ada", "b_ada"), 
                   ("gdn_norm", "gdn_norm_w"), ("lru_conv_b", "lru_conv_b"), ("lru_b_a", "lru_b_a"),
                   ("lru_b_x", "lru_b_x"), ("lru_lambda", "lru_lambda"), ("ssd_conv_b", "ssd_conv_b"),
                   ("ssd_norm", "ssd_norm_w"), ("s5_re", "s5_a_re"), ("s5_im", "s5_a_im")):
        put(n, cols(i[src][0].reshape(-1)))
    put("norm_final", cols(i["norm_final_w"]))
    for n, src in (("gdn_conv", "gdn_conv_w"), ("lru_conv", "lru_conv_w"), ("ssd_conv", "ssd_conv_w")):
        put(n, cols(i[src][0].reshape(-1)))
    put("s5_d", i["s5_d"][0].reshape(16, 32).T)
    put("ssd_d", cols(np.repeat(i["ssd_d"][0], 64)))
    put("s5_dt", cols(np.repeat(i["s5_log_dt"][0], 64)))
    zero4 = np.zeros(4, f)
    put("alog", np.concatenate([i["gdn_a_log"][0], i["ssd_a_log"][0], zero4])[:, None])
    put("dtb", np.concatenate([i["gdn_dt_bias"][0], i["ssd_dt_bias"][0], zero4])[:, None])
    put("rbias", np.broadcast_to(i["router_bias"], (P, NE)))
    put("lru_h0", i["state_lru"][0].reshape(8, 4, P).transpose(2, 1, 0).reshape(P, 32))
    for n, src in (("s5_x0r", "state_s5_re"), ("s5_x0i", "state_s5_im")):
        put(n, i[src][0].reshape(8, 16, P).transpose(2, 1, 0).reshape(P, 128))
    arr["vec"] = vec
    h = np.concatenate([i["cache_gdn_conv"][0], i["cache_ssd_conv"][0], i["cache_lru_conv"][0]], axis=2)
    arr["hist"] = np.ascontiguousarray(h.reshape(8, 3, 24, P).transpose(3, 2, 0, 1)).reshape(P, 576)
    w = i["w_in"][0]
    o = dict(ua=0, qkv=512, zb=2048, ab=2560, bb=2564, xc=2568, gc=3080, zd=3592, xbc=4104, dt=5128, gate=5136)
    for n, width in (("ua", 512), ("qkv", 1536), ("zb", 512), ("xc", 512), ("gc", 512), ("zd", 512), ("xbc", 1024)):
        arr[n] = _pack(w[:, o[n]:o[n] + width])
    for k in range(4):
        arr["gate%d" % k] = _pack(w[:, o["gate"] + 1024 * k:o["gate"] + 1024 * (k + 1)])
        arr["br%d" % k] = _pack(i["w_branch"][0, k])
    nar = np.concatenate([w[:, o["ab"]:o["ab"] + 4], w[:, o["dt"]:o["dt"] + 8], w[:, o["bb"]:o["bb"] + 4]], axis=1)
    arr["wrows"] = np.ascontiguousarray(nar.reshape(KD, P, 16).transpose(1, 0, 2)).reshape(P, 128)
    arr["wrouter"] = np.ascontiguousarray(i["router_w"].reshape(KD, P, 16).transpose(1, 0, 2)).reshape(P, 128)
    arr["ada"] = _pack(i["w_ada"][0])
    arr["out"] = _pack(i["w_out"][0])
    g = i["s5_w_glu"][0].reshape(4, P, 4, P).transpose(1, 2, 0, 3).reshape(P, 2048)
    arr["glu"] = padded(g)
    arr["moe"] = np.concatenate([i[n][0].reshape(NE, -1, P, wd).transpose(0, 2, 1, 3).reshape(NE, P, 4096)
                                 for n, wd in (("moe_w_gate", 512), ("moe_w_up", 512), ("moe_w_down", 1024))], axis=2)
    arr["gdn_state"] = np.ascontiguousarray(i["state_gdn"][0].transpose(2, 0, 1, 3)).reshape(1, P, 4096)
    arr["ssd_state"] = np.ascontiguousarray(i["state_ssd"][0].transpose(3, 0, 1, 2)).reshape(1, P, 4096)
    lw = np.zeros((P, 2, 4, P), f)
    for j, n in enumerate(("lru_w_a", "lru_w_x")):
        for b in range(8):
            r = 64 * (b % 2)
            lw[r:r + 64, j, b // 2, r:r + 64] = i[n][0, b]
    arr["lru_w"] = padded(lw.reshape(P, 1024))
    sbc = np.zeros((P, 4, 16, 32), f)
    for j, (n, tr) in enumerate((("s5_b_re", 0), ("s5_b_im", 0), ("s5_c_re", 1), ("s5_c_im", 1))):
        for gr in range(32):
            a = i[n][0, gr]
            a = a.T if tr else a
            r = 64 * (gr % 2)
            sbc[r:r + 64, j, gr // 2, 16 * (gr % 2):16 * (gr % 2) + 16] = a
    arr["s5_bc"] = padded(sbc.reshape(P, 2048))

    nc = _bacc.Bacc("TRN2", target_bir_lowering=False, num_devices=1)
    arrays, aps = {}, {}
    for name, a in arr.items():
        a = np.ascontiguousarray(a)
        arrays["in_" + name] = a
        aps[name] = nc.dram_tensor("in_" + name, a.shape, F32, kind="ExternalInput").ap()
    for name, shape in _outs().items():
        aps[name] = nc.dram_tensor("out_" + name, shape, F32, kind="ExternalOutput").ap()
    for name, shape in (("h_rows", (T, D)), ("y_rows", (NB * BLK, D)), ("slot_token", (NB * BLK, 1))):
        aps[name] = nc.dram_tensor(name, shape, F32, kind="Internal").ap()
    build(nc, aps)
    r = _run(nc, [arrays], core_ids=[0]).results[0]
    o = {name: np.asarray(r["out_" + name]) for name in _outs()}
    y = o["yT"].transpose(1, 0, 2).reshape(D, T).T
    ho = o["hist_out"].reshape(P, 24, 9, 3).transpose(2, 3, 1, 0).reshape(9, 3, 24 * P)
    s5 = o["s5_out"].reshape(P, 2, 16, 9).transpose(1, 3, 2, 0).reshape(2, 9, 32, 64)
    lru = o["lru_out"].reshape(P, 4, 9).transpose(2, 1, 0).reshape(9, MIX)
    gp = o["gdn_p"].reshape(P, 1, GH, P).transpose(1, 2, 0, 3)
    gs = o["gdn_s"].reshape(P, NSEQ, GH, P).transpose(1, 2, 0, 3)
    sp_ = o["ssd_p"].reshape(P, 1, SH, 64).transpose(1, 2, 3, 0)
    ss = o["ssd_s"].reshape(P, NSEQ, SH, 64).transpose(1, 2, 3, 0)
    got = [y[:NP_TOK].reshape(1, NP_TOK, D), y[NP_TOK:].reshape(NSEQ, SLEN, D)]
    for a, b, gd, sd in ((0, 1, gp, sp_), (1, 9, gs, ss)):
        got += [s5[0, a:b][None], s5[1, a:b][None], gd[None], ho[a:b, :, 0:1536][None], lru[a:b][None],
                ho[a:b, :, 2560:3072][None], sd[None], ho[a:b, :, 1536:2560][None]]
    return tuple(np.ascontiguousarray(x) for x in got)
```
